# Optimizing a Trainium2 kernel written in Bass

```python
import math
import jax
import jax.numpy as jnp
from jax import lax
import numpy as np

D_MODEL = 1024
BATCH = 1
SEQ = 512
DEPTH = 1

GRID_W = 64
CTX_LEN = 256
N_BRANCH = 3
BRANCH_WIDTH = D_MODEL // 2
POOL_WINDOWS = (2, 4, 8, 16)
POOL_GROUPS = len(POOL_WINDOWS)
POOL_GROUP_DIM = BRANCH_WIDTH // POOL_GROUPS
DIFF_HEAD_DIM = 64
DIFF_HEADS = BRANCH_WIDTH // (2 * DIFF_HEAD_DIM)
DIFF_V_DIM = 2 * DIFF_HEAD_DIM
DIFF_QK_WIDTH = DIFF_HEADS * 2 * DIFF_HEAD_DIM
DIFF_V_WIDTH = DIFF_HEADS * DIFF_V_DIM
ROPE_AXIS_FREQS = DIFF_HEAD_DIM // 4
ROPE_THETA = 10000.0
Q_BLOCK = 128
RWKV_HEAD = 64
RWKV_HEADS = BRANCH_WIDTH // RWKV_HEAD
RWKV_WIDTH = RWKV_HEADS * RWKV_HEAD
DECAY_LORA = 64
AAA_LORA = 64
GATE_LORA = 128
RWKV_SPLITS = (RWKV_WIDTH, RWKV_WIDTH, RWKV_WIDTH, 2 * DECAY_LORA, 2 * AAA_LORA, GATE_LORA)
RWKV_IN = 3 * RWKV_WIDTH + 2 * DECAY_LORA + 2 * AAA_LORA + GATE_LORA
IN_SPLITS = (BRANCH_WIDTH, DIFF_QK_WIDTH, DIFF_QK_WIDTH, DIFF_V_WIDTH, RWKV_IN, N_BRANCH * D_MODEL)
IN_WIDTH = BRANCH_WIDTH + 2 * DIFF_QK_WIDTH + DIFF_V_WIDTH + RWKV_IN + N_BRANCH * D_MODEL
N_GROUPS = 4
EXPERTS_PER_GROUP = 8
N_EXPERTS = N_GROUPS * EXPERTS_PER_GROUP
TOP_K = 2
EXPERT_FF = D_MODEL // 2
MOE_BLOCK = 128
N_MOD = 6
NORM_EPS = 1e-6
GN_EPS = 64e-5


def split_cols(p, sizes):
    return jnp.split(p, [int(s) for s in np.cumsum(sizes)[:-1]], axis=-1)

def rms_norm(x, g):
    xf = x.astype(jnp.float32)
    y = xf * lax.rsqrt(jnp.mean(xf * xf, axis=-1, keepdims=True) + NORM_EPS)
    return (y * g.astype(jnp.float32)).astype(x.dtype)

def modulate(x, g, shift, scale):
    return rms_norm(x, g) * (1 + scale) + shift

def centred_window_mean(u, win):
    L = u.shape[1]
    cs = jnp.pad(jnp.cumsum(u.astype(jnp.float32), axis=1), ((0, 0), (1, 0), (0, 0)))
    t = jnp.arange(L)
    lo = jnp.clip(t - win // 2, 0, L - 1)
    hi = jnp.clip(t + win // 2 - 1, 0, L - 1)
    cnt = (hi - lo + 1).astype(jnp.float32)
    return (cs[:, hi + 1] - cs[:, lo]) / cnt[None, :, None]

def pool_mixer(u, w_pool, pool_scale):
    B, L, _ = u.shape
    ug = u.reshape(B, L, POOL_GROUPS, POOL_GROUP_DIM)
    pooled = jnp.stack([centred_window_mean(ug[:, :, i], w) for i, w in enumerate(POOL_WINDOWS)], axis=2)
    diff = pooled.astype(u.dtype) - ug
    y = jnp.einsum('blgc,gcd->blgd', diff, w_pool)
    return y.reshape(B, L, BRANCH_WIDTH) * pool_scale

def rope_rotate(u, ang):
    u1, u2 = jnp.split(u, 2, axis=-1)
    cs = jnp.cos(ang).astype(u.dtype)
    sn = jnp.sin(ang).astype(u.dtype)
    return jnp.concatenate([u1 * cs - u2 * sn, u2 * cs + u1 * sn], axis=-1)

def axial_rope(x, ang_r, ang_c):
    xr, xc = jnp.split(x, 2, axis=-1)
    ar = ang_r[None, :, None, None, :]
    ac = ang_c[None, :, None, None, :]
    return jnp.concatenate([rope_rotate(xr, ar), rope_rotate(xc, ac)], axis=-1)

def diff_qkv(pq, pk, pv, qn_g, kn_g):
    B, L, _ = pq.shape
    q = rms_norm(pq.reshape(B, L, DIFF_HEADS, 2, DIFF_HEAD_DIM), qn_g)
    k = rms_norm(pk.reshape(B, L, DIFF_HEADS, 2, DIFF_HEAD_DIM), kn_g)
    v = pv.reshape(B, L, DIFF_HEADS, DIFF_V_DIM)
    return q, k, v

def diff_attn_block(qb, keys, vals, lam):
    s = jnp.einsum('bqhmd,bkhmd->bhmqk', qb, keys).astype(jnp.float32) * (DIFF_HEAD_DIM ** -0.5)
    p = jax.nn.softmax(s, axis=-1)
    a = p[:, :, 0] - lam * p[:, :, 1]
    return jnp.einsum('bhqk,bkhv->bqhv', a.astype(vals.dtype), vals)

def diff_attn_latent(q, keys, vals, lam):
    B, L = q.shape[:2]
    nb = L // Q_BLOCK
    qb = jnp.moveaxis(q.reshape(B, nb, Q_BLOCK, DIFF_HEADS, 2, DIFF_HEAD_DIM), 1, 0)
    out = lax.map(lambda blk: diff_attn_block(blk, keys, vals, lam), qb)
    return jnp.moveaxis(out, 0, 1).reshape(B, L, DIFF_HEADS, DIFF_V_DIM)

def diff_post(o, subln_g, lam_init):
    B, L = o.shape[:2]
    return (rms_norm(o, subln_g) * (1 - lam_init)).reshape(B, L, DIFF_V_WIDTH)

def token_shift_centred(u, mu):
    prev = jnp.pad(u, ((0, 0), (1, 0), (0, 0)))[:, :-1]
    nxt = jnp.pad(u, ((0, 0), (0, 1), (0, 0)))[:, 1:]
    return u + (prev - u) * mu[0] + (nxt - u) * mu[1]

def rwkv_prepare(pr, shift_mu, w0, w2, a0, a2, g2, k_k, k_a):
    B, L, _ = pr.shape
    u = token_shift_centred(pr, shift_mu)
    r, k, v, wl, al, gl = split_cols(u, RWKV_SPLITS)
    wl = wl.reshape(B, L, 2, DECAY_LORA)
    al = al.reshape(B, L, 2, AAA_LORA)
    w_log = -jax.nn.softplus(-(w0 + jnp.einsum('bldr,drc->bldc', jnp.tanh(wl), w2))) - 0.5
    decay = jnp.exp(-jnp.exp(w_log.astype(jnp.float32)))
    a = jax.nn.sigmoid(a0 + jnp.einsum('bldr,drc->bldc', al, a2))
    g = jax.nn.sigmoid(gl) @ g2
    kk = (k * k_k).reshape(B, L, RWKV_HEADS, RWKV_HEAD).astype(jnp.float32)
    kk = kk / jnp.maximum(jnp.sqrt(jnp.sum(kk * kk, axis=-1, keepdims=True)), 1e-12)
    kk = kk.reshape(B, L, RWKV_WIDTH).astype(k.dtype)
    k_mod = k[:, :, None] * (1 + (a - 1) * k_a)
    b_vec = kk[:, :, None] * a
    return r, k_mod, v, decay, -kk, b_vec, g

def to_scan(u):
    B, L = u.shape[:2]
    u = jnp.stack([u[:, :, 0], jnp.flip(u[:, :, 1], axis=1)], axis=0)
    return jnp.moveaxis(u.reshape(2, B, L, RWKV_HEADS, RWKV_HEAD), 2, 0).astype(jnp.float32)

def wkv_step(S, inp):
    r, w, k, v, a, b = inp
    sa = jnp.einsum('dbhvk,dbhk->dbhv', S, a)
    S = S * w[..., None, :] + sa[..., None] * b[..., None, :] + v[..., None] * k[..., None, :]
    return S, jnp.einsum('dbhvk,dbhk->dbhv', S, r)

def wkv_bidir(S0, r, k_mod, v, decay, a_vec, b_vec):
    B, L, C = r.shape
    both = lambda u: jnp.broadcast_to(u[:, :, None], (B, L, 2, C))
    xs = tuple(to_scan(u) for u in (both(r), decay, k_mod, both(v), both(a_vec), b_vec))
    S, ys = lax.scan(wkv_step, S0, xs)
    y = ys[:, 0] + jnp.flip(ys[:, 1], axis=0)
    return S, jnp.moveaxis(y, 0, 1)

def rwkv_output(y, prep, r_k, gn_w, gn_b):
    r, k_mod, v, g = prep[0], prep[1], prep[2], prep[6]
    B, L, _ = r.shape
    mu = jnp.mean(y, axis=-1, keepdims=True)
    var = jnp.mean(jnp.square(y - mu), axis=-1, keepdims=True)
    yn = ((y - mu) * lax.rsqrt(var + GN_EPS)).reshape(B, L, RWKV_WIDTH) * gn_w + gn_b
    coef = jnp.sum((r[:, :, None] * k_mod * r_k.reshape(-1)).reshape(B, L, 2, RWKV_HEADS, RWKV_HEAD), axis=(2, 4))
    bonus = (coef[..., None] * v.reshape(B, L, RWKV_HEADS, RWKV_HEAD)).reshape(B, L, RWKV_WIDTH)
    return (yn.astype(r.dtype) + bonus) * g

def merge_branches(branches, gates, w_br, w_out):
    B, L, _ = gates.shape
    g = jax.nn.sigmoid(gates.reshape(B, L, N_BRANCH, D_MODEL))
    merged = g[:, :, 0] * (branches[0] @ w_br[0])
    for n in range(1, N_BRANCH):
        merged = merged + g[:, :, n] * (branches[n] @ w_br[n])
    return merged @ w_out

def expert_dispatch(h, eid, gates, w_g, w_u, w_d):
    T, D = h.shape
    A = T * TOP_K
    flat_e = eid.reshape(A)
    flat_tok = jnp.repeat(jnp.arange(T, dtype=jnp.int32), TOP_K)
    order = jnp.argsort(flat_e)
    e_sorted = flat_e[order]
    counts = jnp.bincount(flat_e, length=N_EXPERTS)
    padded = (counts + MOE_BLOCK - 1) // MOE_BLOCK * MOE_BLOCK
    start = jnp.cumsum(counts) - counts
    pend = jnp.cumsum(padded)
    pstart = pend - padded
    slot = pstart[e_sorted] + jnp.arange(A, dtype=jnp.int32) - start[e_sorted]
    P = -(-A // MOE_BLOCK) * MOE_BLOCK + N_EXPERTS * MOE_BLOCK
    n_blk = P // MOE_BLOCK
    slot_tok = jnp.full((P,), T, jnp.int32).at[slot].set(flat_tok[order])
    slot_gate = jnp.zeros((P,), h.dtype).at[slot].set(gates.reshape(A)[order])
    blk_e = jnp.minimum(jnp.searchsorted(pend, jnp.arange(n_blk, dtype=jnp.int32) * MOE_BLOCK, side='right'), N_EXPERTS - 1)
    xb = jnp.concatenate([h, jnp.zeros((1, D), h.dtype)], axis=0)[slot_tok].reshape(n_blk, MOE_BLOCK, D)

    def block_ffn(args):
        xblk, e = args
        return (jax.nn.silu(xblk @ w_g[e]) * (xblk @ w_u[e])) @ w_d[e]

    yb = lax.map(block_ffn, (xb, blk_e)).reshape(P, D)
    return jax.ops.segment_sum(yb * slot_gate[:, None], slot_tok, num_segments=T + 1)[:T]

def hier_moe(h, w_rg, w_re, w_g, w_u, w_d):
    T = h.shape[0]
    lg = (h @ w_rg).astype(jnp.float32)
    grp = jnp.argmax(lg, axis=-1)
    p_grp = jnp.take_along_axis(jax.nn.softmax(lg, axis=-1), grp[:, None], axis=-1)
    le = (h @ w_re).astype(jnp.float32).reshape(T, N_GROUPS, EXPERTS_PER_GROUP)
    le = jnp.take_along_axis(le, grp[:, None, None], axis=1)[:, 0]
    top_v, top_i = lax.top_k(le, TOP_K)
    gates = p_grp * jax.nn.softmax(top_v, axis=-1)
    eid = (grp[:, None] * EXPERTS_PER_GROUP + top_i).astype(jnp.int32)
    return expert_dispatch(h, eid, gates.astype(h.dtype), w_g, w_u, w_d)

def first_inputs(seed: int = 0) -> dict:
    key = jax.random.key(seed)
    keys = jax.random.split(key, 40)
    cnt = [0]

    def nk():
        cnt[0] += 1
        return keys[cnt[0] - 1]

    def nrm(shape, scale):
        return scale * jax.random.normal(nk(), shape, jnp.float32)

    def uni(shape, lo, hi):
        return jax.random.uniform(nk(), shape, jnp.float32, lo, hi)

    D = D_MODEL
    return {
        'x': nrm((BATCH, SEQ, D), 1.0),
        'c': nrm((BATCH, D), 1.0),
        'ctx': nrm((BATCH, CTX_LEN, D), 1.0),
        'c_ctx': nrm((D,), 1.0),
        'w_ada': nrm((DEPTH, D, N_MOD * D), 0.5 * D ** -0.5),
        'b_ada': nrm((DEPTH, N_MOD * D), 0.02),
        'norm1_g': 1.0 + nrm((DEPTH, D), 0.05),
        'norm2_g': 1.0 + nrm((DEPTH, D), 0.05),
        'w_in': nrm((DEPTH, D, IN_WIDTH), D ** -0.5),
        'pool_w': nrm((DEPTH, POOL_GROUPS, POOL_GROUP_DIM, POOL_GROUP_DIM), POOL_GROUP_DIM ** -0.5),
        'pool_scale': 1.0 + nrm((DEPTH, BRANCH_WIDTH), 0.1),
        'q_norm_g': 1.0 + nrm((DEPTH, DIFF_HEAD_DIM), 0.05),
        'k_norm_g': 1.0 + nrm((DEPTH, DIFF_HEAD_DIM), 0.05),
        'lambda_qk': nrm((DEPTH, 4, DIFF_HEAD_DIM), 0.1),
        'subln_g': 1.0 + nrm((DEPTH, DIFF_V_DIM), 0.05),
        'shift_mu': uni((DEPTH, 2, RWKV_IN), 0.0, 0.5),
        'decay_w0': uni((DEPTH, 2, RWKV_WIDTH), -4.0, 1.0),
        'decay_w2': nrm((DEPTH, 2, DECAY_LORA, RWKV_WIDTH), 0.5 * DECAY_LORA ** -0.5),
        'aaa_a0': nrm((DEPTH, 2, RWKV_WIDTH), 0.5),
        'aaa_a2': nrm((DEPTH, 2, AAA_LORA, RWKV_WIDTH), 0.5 * AAA_LORA ** -0.5),
        'gate_w2': nrm((DEPTH, GATE_LORA, RWKV_WIDTH), GATE_LORA ** -0.5),
        'k_k': 0.85 + nrm((DEPTH, RWKV_WIDTH), 0.1),
        'k_a': 1.0 + nrm((DEPTH, RWKV_WIDTH), 0.1),
        'r_k': nrm((DEPTH, RWKV_HEADS, RWKV_HEAD), 0.1),
        'gn_w': 1.0 + nrm((DEPTH, RWKV_WIDTH), 0.05),
        'gn_b': nrm((DEPTH, RWKV_WIDTH), 0.02),
        'w_br': nrm((DEPTH, N_BRANCH, BRANCH_WIDTH, D), BRANCH_WIDTH ** -0.5),
        'w_out': nrm((DEPTH, D, D), D ** -0.5),
        'w_router_group': nrm((DEPTH, D, N_GROUPS), D ** -0.5),
        'w_router_expert': nrm((DEPTH, D, N_EXPERTS), D ** -0.5),
        'w_exp_gate': nrm((DEPTH, N_EXPERTS, D, EXPERT_FF), D ** -0.5),
        'w_exp_up': nrm((DEPTH, N_EXPERTS, D, EXPERT_FF), D ** -0.5),
        'w_exp_down': nrm((DEPTH, N_EXPERTS, EXPERT_FF, D), EXPERT_FF ** -0.5),
    }

def first_block(x, c, ctx, c_ctx, w_ada, b_ada, norm1_g, norm2_g, w_in, pool_w, pool_scale, q_norm_g, k_norm_g,
              lambda_qk, subln_g, shift_mu, decay_w0, decay_w2, aaa_a0, aaa_a2, gate_w2, k_k, k_a, r_k, gn_w, gn_b,
              w_br, w_out, w_router_group, w_router_expert, w_exp_gate, w_exp_up, w_exp_down):
    B, L, D = x.shape
    C = ctx.shape[1]
    rows = L // GRID_W
    row_idx = jnp.repeat(jnp.arange(rows), GRID_W).astype(jnp.float32)
    col_idx = jnp.tile(jnp.arange(GRID_W), rows).astype(jnp.float32)
    inv_freq = ROPE_THETA ** (-jnp.arange(ROPE_AXIS_FREQS, dtype=jnp.float32) / ROPE_AXIS_FREQS)
    ang_r = row_idx[:, None] * inv_freq
    ang_c = col_idx[:, None] * inv_freq
    s_lat = jax.nn.silu(c)
    s_ctx = jax.nn.silu(c_ctx)
    S0 = jnp.zeros((2, B, RWKV_HEADS, RWKV_HEAD, RWKV_HEAD), jnp.float32)

    for l in range(DEPTH):
        last = l == DEPTH - 1
        mod = (s_lat @ w_ada[l] + b_ada[l]).reshape(B, N_MOD, 1, D)
        mod_c = (s_ctx @ w_ada[l] + b_ada[l]).reshape(N_MOD, 1, 1, D)

        p_l = modulate(x, norm1_g[l], mod[:, 0], mod[:, 1]) @ w_in[l]
        p_c = modulate(ctx, norm1_g[l], mod_c[0], mod_c[1]) @ w_in[l]
        pool_l, q_l, k_l, v_l, rw_l, gate_l = split_cols(p_l, IN_SPLITS)
        pool_c, q_c, k_c, v_c, rw_c, gate_c = split_cols(p_c, IN_SPLITS)

        lam_init = 0.8 - 0.6 * math.exp(-0.3 * l)
        lq = lambda_qk[l].astype(jnp.float32)
        lam = jnp.exp(jnp.sum(lq[0] * lq[1])) - jnp.exp(jnp.sum(lq[2] * lq[3])) + lam_init
        qh_l, kh_l, vh_l = diff_qkv(q_l, k_l, v_l, q_norm_g[l], k_norm_g[l])
        qh_l = axial_rope(qh_l, ang_r, ang_c)
        kh_l = axial_rope(kh_l, ang_r, ang_c)
        qh_c, kh_c, vh_c = diff_qkv(q_c, k_c, v_c, q_norm_g[l], k_norm_g[l])
        keys = jnp.concatenate([kh_c, kh_l], axis=1)
        vals = jnp.concatenate([vh_c, vh_l], axis=1)
        att_l = diff_post(diff_attn_latent(qh_l, keys, vals, lam), subln_g[l], lam_init)

        rw_par = (shift_mu[l], decay_w0[l], decay_w2[l], aaa_a0[l], aaa_a2[l], gate_w2[l], k_k[l], k_a[l])
        prep_c = rwkv_prepare(rw_c, *rw_par)
        S_c, y_c = wkv_bidir(S0, *prep_c[:6])
        prep_l = rwkv_prepare(rw_l, *rw_par)
        _, y_l = wkv_bidir(S_c, *prep_l[:6])
        rwo_l = rwkv_output(y_l, prep_l, r_k[l], gn_w[l], gn_b[l])

        mix_l = merge_branches((pool_mixer(pool_l, pool_w[l], pool_scale[l]), att_l, rwo_l), gate_l, w_br[l], w_out[l])
        x = x + mod[:, 2] * mix_l
        if not last:
            att_c = diff_post(diff_attn_block(qh_c, kh_c, vh_c, lam), subln_g[l], lam_init)
            rwo_c = rwkv_output(y_c, prep_c, r_k[l], gn_w[l], gn_b[l])
            mix_c = merge_branches((pool_mixer(pool_c, pool_w[l], pool_scale[l]), att_c, rwo_c), gate_c, w_br[l], w_out[l])
            ctx = ctx + mod_c[2] * mix_c

        moe_par = (w_router_group[l], w_router_expert[l], w_exp_gate[l], w_exp_up[l], w_exp_down[l])
        f_l = modulate(x, norm2_g[l], mod[:, 3], mod[:, 4]).reshape(B * L, D)
        if last:
            x = x + mod[:, 5] * hier_moe(f_l, *moe_par).reshape(B, L, D)
        else:
            f_c = modulate(ctx, norm2_g[l], mod_c[3], mod_c[4]).reshape(B * C, D)
            y = hier_moe(jnp.concatenate([f_c, f_l], axis=0), *moe_par)
            ctx = ctx + mod_c[5] * y[:B * C].reshape(B, C, D)
            x = x + mod[:, 5] * y[B * C:].reshape(B, L, D)
    return x


DEPTH_2 = 2

RMS_EPS = 1e-6
SHORT_W = 3

HY_WIDTH = 512
HY_EMB = 33
HY_FF = 64
HY_FAST = 0.3
HY_SLOW = 1.5
HY_TARGET = 1e-2
HY_SHIFT = 0.05

ML_HEADS = 4
ML_HEAD_DIM = 128
ML_WIDTH = ML_HEADS * ML_HEAD_DIM
ML_CHUNK = 64
IN0_COLS = 3 * HY_WIDTH + 4 * ML_WIDTH + 4 * ML_HEADS

MLA_HEADS = 8
MLA_NOPE = 128
MLA_ROPE = 64
MLA_V = 128
MLA_Q_RANK = 384
MLA_KV_RANK = 256
MLA_SCALE = (MLA_NOPE + MLA_ROPE) ** -0.5
ROPE_AXIS = MLA_ROPE // 2
ROPE_BASE = 10000.0

D_FF = 2816


F32 = jnp.float32

def rmsnorm(x, g):
    xf = x.astype(F32)
    y = xf * lax.rsqrt(jnp.mean(xf * xf, axis=-1, keepdims=True) + RMS_EPS)
    return (y * g.astype(F32)).astype(x.dtype)

def ada_mod(cv, w, b):
    m = jax.nn.silu(cv) @ w + b
    return jnp.split(m, N_MOD, axis=-1)

def dwconv(x, w):
    k = w.shape[0]
    return lax.conv_general_dilated(x, w[:, None, :].astype(x.dtype), (1,), [(k // 2, k // 2)],
                                    dimension_numbers=('NWC', 'WIO', 'NWC'),
                                    feature_group_count=x.shape[-1])

def hyena_filters(L, fw1, fb1, fw2, fb2, fw3, freq):
    pos = jnp.arange(L, dtype=F32)
    t = (pos / (L - 1))[:, None]
    bands = (HY_EMB - 1) // 2
    f = jnp.linspace(1e-4, bands - 1, bands, dtype=F32)
    ang = (2.0 * math.pi / L) * pos[:, None] * f[None, :]
    z = jnp.concatenate([t, jnp.cos(ang), -jnp.sin(ang)], axis=-1)
    fq = freq.astype(F32)
    h = jnp.sin(fq * (z @ fw1.astype(F32) + fb1.astype(F32)))
    h = jnp.sin(fq * (h @ fw2.astype(F32) + fb2.astype(F32)))
    h = h @ fw3.astype(F32)
    deltas = jnp.linspace(math.log(HY_TARGET) / HY_FAST, math.log(HY_TARGET) / HY_SLOW, HY_WIDTH, dtype=F32)
    decay = jnp.exp(-t * jnp.abs(jnp.tile(deltas, 2))[None, :])
    return h * (decay + HY_SHIFT)

def hyena_mix(u, conv_w, conv_b, filt, bias):
    u = dwconv(u, conv_w) + conv_b
    x0, x1, v = jnp.split(u, 3, axis=-1)
    L = u.shape[1]
    g = (v * x1).astype(F32)
    h = hyena_filters(L, *filt)
    hf, hb = h[:, :HY_WIDTH], h[:, HY_WIDTH:]
    k2 = jnp.concatenate([hf, jnp.zeros((1, HY_WIDTH), F32), hb[:0:-1]], axis=0)
    n = 2 * L
    y = jnp.fft.irfft(jnp.fft.rfft(g, n=n, axis=1) * jnp.fft.rfft(k2, axis=0)[None], n=n, axis=1)[:, :L]
    y = y + g * bias.astype(F32)
    return y.astype(u.dtype) * x0

def mlstm_chunkwise(q, k, v, ig, lf, state):
    B, H, T, d = q.shape
    nc = T // ML_CHUNK

    def chunks(a):
        return jnp.moveaxis(a.reshape((B, H, nc, ML_CHUNK) + a.shape[3:]), 2, 0)

    causal = jnp.tril(jnp.ones((ML_CHUNK, ML_CHUNK), dtype=bool))

    def step(carry, inp):
        C, nv, m = carry
        qc, kc, vc, ic, fc = inp
        b = jnp.cumsum(fc, axis=-1)
        dlog = jnp.where(causal, b[..., :, None] - b[..., None, :] + ic[..., None, :], -jnp.inf)
        inter = b + m[..., None]
        m_t = jnp.maximum(inter, jnp.max(dlog, axis=-1))
        w_in = jnp.exp(dlog - m_t[..., None])
        w_st = jnp.exp(inter - m_t)
        s = jnp.einsum('bhtd,bhsd->bhts', qc, kc) * w_in
        num = jnp.einsum('bhts,bhsd->bhtd', s, vc) + w_st[..., None] * jnp.einsum('bhve,bhte->bhtv', C, qc)
        den = jnp.sum(s, axis=-1) + w_st * jnp.einsum('bhe,bhte->bht', nv, qc)
        h = num / jnp.maximum(jnp.abs(den), jnp.exp(-m_t))[..., None]
        bl = b[..., -1]
        gs = bl[..., None] - b + ic
        m_new = jnp.maximum(bl + m, jnp.max(gs, axis=-1))
        a = jnp.exp(bl + m - m_new)
        ws = jnp.exp(gs - m_new[..., None])
        C_new = a[..., None, None] * C + jnp.einsum('bhs,bhsv,bhse->bhve', ws, vc, kc)
        n_new = a[..., None] * nv + jnp.einsum('bhs,bhse->bhe', ws, kc)
        return (C_new, n_new, m_new), h

    state, hs = lax.scan(step, state, (chunks(q), chunks(k), chunks(v), chunks(ig), chunks(lf)))
    return jnp.moveaxis(hs, 0, 2).reshape(B, H, T, d), state

def mlstm_direction(q, k, v, ig, f_pre, state, reverse):
    lf = jax.nn.log_sigmoid(f_pre)
    if reverse:
        q, k, v = jnp.flip(q, 2), jnp.flip(k, 2), jnp.flip(v, 2)
        ig, lf = jnp.flip(ig, -1), jnp.flip(lf, -1)
    h, state = mlstm_chunkwise(q, k, v, ig, lf, state)
    if reverse:
        h = jnp.flip(h, 2)
    return h, state

def mlstm_inputs(u, conv_w, gate_b):
    B, L, _ = u.shape
    off = 3 * HY_WIDTH
    qk = jax.nn.silu(dwconv(u[..., off:off + 2 * ML_WIDTH], conv_w))
    q, k = jnp.split(qk, 2, axis=-1)
    v = u[..., off + 2 * ML_WIDTH:off + 3 * ML_WIDTH]
    og = u[..., off + 3 * ML_WIDTH:off + 4 * ML_WIDTH]
    gates = u[..., off + 4 * ML_WIDTH:].astype(F32) + gate_b.astype(F32)
    gates = jnp.transpose(gates.reshape(B, L, 4, ML_HEADS), (2, 0, 3, 1))

    def heads(a):
        return jnp.transpose(a.reshape(B, L, ML_HEADS, ML_HEAD_DIM), (0, 2, 1, 3)).astype(F32)

    return heads(q) * ML_HEAD_DIM ** -0.5, heads(k), heads(v), og, gates

def mlstm_out(h, og, norm_g):
    B, H, L, d = h.shape
    t = jnp.swapaxes(h, 1, 2)
    t = t * lax.rsqrt(jnp.mean(t * t, axis=-1, keepdims=True) + RMS_EPS)
    t = t.reshape(B, L, H * d) * norm_g.astype(F32)
    return (t * jax.nn.sigmoid(og.astype(F32))).astype(og.dtype)

def mlstm_mix(u_ctx, u_lat, conv_w, gate_b, norm_g):
    qc, kc, vc, oc, gc = mlstm_inputs(u_ctx, conv_w, gate_b)
    ql, kl, vl, ol, gl = mlstm_inputs(u_lat, conv_w, gate_b)
    B = u_ctx.shape[0]
    zero = (jnp.zeros((B, ML_HEADS, ML_HEAD_DIM, ML_HEAD_DIM), F32),
            jnp.zeros((B, ML_HEADS, ML_HEAD_DIM), F32),
            jnp.zeros((B, ML_HEADS), F32))
    hc_f, st_f = mlstm_direction(qc, kc, vc, gc[0], gc[1], zero, False)
    hl_f, _ = mlstm_direction(ql, kl, vl, gl[0], gl[1], st_f, False)
    hc_b, st_b = mlstm_direction(qc, kc, vc, gc[2], gc[3], zero, True)
    hl_b, _ = mlstm_direction(ql, kl, vl, gl[2], gl[3], st_b, True)
    return mlstm_out(hc_f + hc_b, oc, norm_g), mlstm_out(hl_f + hl_b, ol, norm_g)

def hyena_mlstm_mixer(h_ctx, h_lat, w_in, hy_conv_w, hy_conv_b, hy_filter, hy_bias,
                      ml_conv_w, ml_gate_b, ml_norm_g, w_out):
    u_ctx = h_ctx @ w_in
    u_lat = h_lat @ w_in
    hy_c = hyena_mix(u_ctx[..., :3 * HY_WIDTH], hy_conv_w, hy_conv_b, hy_filter, hy_bias)
    hy_l = hyena_mix(u_lat[..., :3 * HY_WIDTH], hy_conv_w, hy_conv_b, hy_filter, hy_bias)
    ml_c, ml_l = mlstm_mix(u_ctx, u_lat, ml_conv_w, ml_gate_b, ml_norm_g)
    y_ctx = jnp.concatenate([hy_c, ml_c], axis=-1) @ w_out
    y_lat = jnp.concatenate([hy_l, ml_l], axis=-1) @ w_out
    return y_ctx, y_lat

def rope_tables(T):
    n_rows = T // GRID_W
    row = jnp.repeat(jnp.arange(n_rows, dtype=F32), GRID_W)
    col = jnp.tile(jnp.arange(GRID_W, dtype=F32), n_rows)
    inv = ROPE_BASE ** (-jnp.arange(0, ROPE_AXIS, 2, dtype=F32) / ROPE_AXIS)
    ang = jnp.stack([row[:, None] * inv, col[:, None] * inv], axis=1)
    return jnp.cos(ang), jnp.sin(ang)

def apply_rope2d(x, cos, sin):
    xa = x.reshape(x.shape[:-1] + (2, ROPE_AXIS))
    x1, x2 = jnp.split(xa, 2, axis=-1)
    c = cos[None, :, None].astype(x.dtype)
    s = sin[None, :, None].astype(x.dtype)
    return jnp.concatenate([x1 * c - x2 * s, x2 * c + x1 * s], axis=-1).reshape(x.shape)

def mla_down(h, w_down):
    return jnp.split(h @ w_down, [MLA_Q_RANK, MLA_Q_RANK + MLA_KV_RANK], axis=-1)

def mla_q(q_a, q_norm, w_uq, rope):
    B, L, _ = q_a.shape
    q = (rmsnorm(q_a, q_norm) @ w_uq).reshape(B, L, MLA_HEADS, MLA_NOPE + MLA_ROPE)
    if rope is None:
        return q
    q_n, q_r = jnp.split(q, [MLA_NOPE], axis=-1)
    return jnp.concatenate([q_n, apply_rope2d(q_r, *rope)], axis=-1)

def mla_kv(kv_a, k_r, kv_norm, w_ukv, rope):
    B, L, _ = kv_a.shape
    kv = (rmsnorm(kv_a, kv_norm) @ w_ukv).reshape(B, L, MLA_HEADS, MLA_NOPE + MLA_V)
    k_n, v = jnp.split(kv, [MLA_NOPE], axis=-1)
    k_r = k_r[:, :, None, :]
    if rope is not None:
        k_r = apply_rope2d(k_r, *rope)
    k = jnp.concatenate([k_n, jnp.broadcast_to(k_r, (B, L, MLA_HEADS, MLA_ROPE))], axis=-1)
    return k, v

def attend(q, k, v):
    s = jnp.einsum('bqhd,bkhd->bhqk', q, k).astype(F32) * MLA_SCALE
    p = jax.nn.softmax(s, axis=-1).astype(v.dtype)
    return jnp.einsum('bhqk,bkhd->bqhd', p, v)

def mla_mixer(h_ctx, h_lat, ctx_queries, w_down, q_norm, kv_norm, w_uq, w_ukv, w_o):
    B, S, _ = h_lat.shape
    rope = rope_tables(S)
    qa_c, kva_c, kr_c = mla_down(h_ctx, w_down)
    qa_l, kva_l, kr_l = mla_down(h_lat, w_down)
    k_c, v_c = mla_kv(kva_c, kr_c, kv_norm, w_ukv, None)
    k_l, v_l = mla_kv(kva_l, kr_l, kv_norm, w_ukv, rope)
    q_l = mla_q(qa_l, q_norm, w_uq, rope)
    k_all = jnp.concatenate([k_c, k_l], axis=1)
    v_all = jnp.concatenate([v_c, v_l], axis=1)
    nb = S // Q_BLOCK
    qb = jnp.moveaxis(q_l.reshape(B, nb, Q_BLOCK, MLA_HEADS, MLA_NOPE + MLA_ROPE), 1, 0)
    o_l = lax.map(lambda blk: attend(blk, k_all, v_all), qb)
    y_lat = jnp.moveaxis(o_l, 0, 1).reshape(B, S, MLA_HEADS * MLA_V) @ w_o
    y_ctx = None
    if ctx_queries:
        q_c = mla_q(qa_c, q_norm, w_uq, None)
        y_ctx = attend(q_c, k_c, v_c).reshape(B, h_ctx.shape[1], MLA_HEADS * MLA_V) @ w_o
    return y_ctx, y_lat

def conv_ffn(h, w_up, conv_w, conv_b, w_down):
    g, u = jnp.split(h @ w_up, 2, axis=-1)
    g = dwconv(g, conv_w) + conv_b
    return (jax.nn.silu(g) * u) @ w_down

def second_inputs(seed: int = 0) -> dict:
    key = jax.random.key(seed)
    keys = iter(jax.random.split(key, 64))

    def nrm(shape, scale):
        return jax.random.normal(next(keys), shape, F32) * scale

    def gain(n):
        return 1.0 + nrm((n,), 0.02)

    def ffn():
        return (nrm((D_MODEL, 2 * D_FF), D_MODEL ** -0.5), nrm((SHORT_W, D_FF), SHORT_W ** -0.5),
                nrm((D_FF,), 0.02), nrm((D_FF, D_MODEL), D_FF ** -0.5))

    x = nrm((BATCH, SEQ, D_MODEL), 1.0)
    c = nrm((BATCH, D_MODEL), 1.0)
    ctx = nrm((BATCH, CTX_LEN, D_MODEL), 1.0)
    c_ctx = nrm((D_MODEL,), 1.0)
    forget_b = jnp.linspace(3.0, 6.0, ML_HEADS, dtype=F32)
    ml_gate_b = jnp.concatenate([nrm((ML_HEADS,), 0.1), forget_b + nrm((ML_HEADS,), 0.01),
                                 nrm((ML_HEADS,), 0.1), forget_b + nrm((ML_HEADS,), 0.01)])
    f0 = ffn()
    f1 = ffn()
    mix_w = HY_WIDTH + ML_WIDTH
    return {
        'x': x, 'c': c, 'ctx': ctx, 'c_ctx': c_ctx,
        'ada_w_0': nrm((D_MODEL, N_MOD * D_MODEL), 0.5 * D_MODEL ** -0.5),
        'ada_b_0': nrm((N_MOD * D_MODEL,), 0.02),
        'norm_mix_0': gain(D_MODEL), 'norm_ffn_0': gain(D_MODEL),
        'w_in_0': nrm((D_MODEL, IN0_COLS), D_MODEL ** -0.5),
        'hy_conv_w': nrm((SHORT_W, 3 * HY_WIDTH), SHORT_W ** -0.5),
        'hy_conv_b': nrm((3 * HY_WIDTH,), 0.02),
        'hy_fw1': nrm((HY_EMB, HY_FF), HY_EMB ** -0.5),
        'hy_fb1': nrm((HY_FF,), 0.02),
        'hy_fw2': nrm((HY_FF, HY_FF), HY_FF ** -0.5),
        'hy_fb2': nrm((HY_FF,), 0.02),
        'hy_fw3': nrm((HY_FF, 2 * HY_WIDTH), 0.05 * HY_FF ** -0.5),
        'hy_freq': gain(HY_FF),
        'hy_bias': nrm((HY_WIDTH,), 0.1),
        'ml_conv_w': nrm((SHORT_W, 2 * ML_WIDTH), SHORT_W ** -0.5),
        'ml_gate_b': ml_gate_b,
        'ml_norm_g': gain(ML_WIDTH),
        'w_out_0': nrm((mix_w, D_MODEL), mix_w ** -0.5),
        'ffn_up_0': f0[0], 'ffn_conv_w_0': f0[1], 'ffn_conv_b_0': f0[2], 'ffn_down_0': f0[3],
        'ada_w_1': nrm((D_MODEL, N_MOD * D_MODEL), 0.5 * D_MODEL ** -0.5),
        'ada_b_1': nrm((N_MOD * D_MODEL,), 0.02),
        'norm_mix_1': gain(D_MODEL), 'norm_ffn_1': gain(D_MODEL),
        'mla_w_down': nrm((D_MODEL, MLA_Q_RANK + MLA_KV_RANK + MLA_ROPE), D_MODEL ** -0.5),
        'mla_q_norm': gain(MLA_Q_RANK), 'mla_kv_norm': gain(MLA_KV_RANK),
        'mla_w_uq': nrm((MLA_Q_RANK, MLA_HEADS * (MLA_NOPE + MLA_ROPE)), MLA_Q_RANK ** -0.5),
        'mla_w_ukv': nrm((MLA_KV_RANK, MLA_HEADS * (MLA_NOPE + MLA_V)), MLA_KV_RANK ** -0.5),
        'mla_w_o': nrm((MLA_HEADS * MLA_V, D_MODEL), (MLA_HEADS * MLA_V) ** -0.5),
        'ffn_up_1': f1[0], 'ffn_conv_w_1': f1[1], 'ffn_conv_b_1': f1[2], 'ffn_down_1': f1[3],
        'final_norm': gain(D_MODEL),
    }

def second_block(x, c, ctx, c_ctx, ada_w_0, ada_b_0, norm_mix_0, norm_ffn_0, w_in_0, hy_conv_w, hy_conv_b,
              hy_fw1, hy_fb1, hy_fw2, hy_fb2, hy_fw3, hy_freq, hy_bias, ml_conv_w, ml_gate_b, ml_norm_g,
              w_out_0, ffn_up_0, ffn_conv_w_0, ffn_conv_b_0, ffn_down_0, ada_w_1, ada_b_1, norm_mix_1,
              norm_ffn_1, mla_w_down, mla_q_norm, mla_kv_norm, mla_w_uq, mla_w_ukv, mla_w_o, ffn_up_1,
              ffn_conv_w_1, ffn_conv_b_1, ffn_down_1, final_norm):
    ada_w = (ada_w_0, ada_w_1)
    ada_b = (ada_b_0, ada_b_1)
    norm_mix = (norm_mix_0, norm_mix_1)
    norm_ffn = (norm_ffn_0, norm_ffn_1)
    ffn_p = ((ffn_up_0, ffn_conv_w_0, ffn_conv_b_0, ffn_down_0),
             (ffn_up_1, ffn_conv_w_1, ffn_conv_b_1, ffn_down_1))
    hy_filter = (hy_fw1, hy_fb1, hy_fw2, hy_fb2, hy_fw3, hy_freq)
    x_lat, x_ctx = x, ctx
    for layer in range(DEPTH_2):
        last = layer == DEPTH_2 - 1
        sh1, sc1, g1, sh2, sc2, g2 = ada_mod(c[:, None, :], ada_w[layer], ada_b[layer])
        csh1, csc1, cg1, csh2, csc2, cg2 = ada_mod(c_ctx, ada_w[layer], ada_b[layer])
        h_lat = rmsnorm(x_lat, norm_mix[layer]) * (1 + sc1) + sh1
        h_ctx = rmsnorm(x_ctx, norm_mix[layer]) * (1 + csc1) + csh1
        if layer % 2 == 0:
            y_ctx, y_lat = hyena_mlstm_mixer(h_ctx, h_lat, w_in_0, hy_conv_w, hy_conv_b, hy_filter, hy_bias,
                                             ml_conv_w, ml_gate_b, ml_norm_g, w_out_0)
        else:
            y_ctx, y_lat = mla_mixer(h_ctx, h_lat, not last, mla_w_down, mla_q_norm, mla_kv_norm,
                                     mla_w_uq, mla_w_ukv, mla_w_o)
        x_lat = x_lat + g1 * y_lat
        x_lat = x_lat + g2 * conv_ffn(rmsnorm(x_lat, norm_ffn[layer]) * (1 + sc2) + sh2, *ffn_p[layer])
        if not last:
            x_ctx = x_ctx + cg1 * y_ctx
            x_ctx = x_ctx + cg2 * conv_ffn(rmsnorm(x_ctx, norm_ffn[layer]) * (1 + csc2) + csh2, *ffn_p[layer])
    return rmsnorm(x_lat, final_norm)


def setup_inputs(seed=0):
    out = dict(first_inputs(seed))
    for name, value in second_inputs(seed + 1).items():
        if name != "x":
            out[name + "_2"] = value
    return out


def reference(
    x, c, ctx, c_ctx, w_ada, b_ada, norm1_g, norm2_g, w_in, pool_w, pool_scale, q_norm_g,
    k_norm_g, lambda_qk, subln_g, shift_mu, decay_w0, decay_w2, aaa_a0, aaa_a2, gate_w2, k_k,
    k_a, r_k, gn_w, gn_b, w_br, w_out, w_router_group, w_router_expert, w_exp_gate, w_exp_up,
    w_exp_down, c_2, ctx_2, c_ctx_2, ada_w_0_2, ada_b_0_2, norm_mix_0_2, norm_ffn_0_2, w_in_0_2,
    hy_conv_w_2, hy_conv_b_2, hy_fw1_2, hy_fb1_2, hy_fw2_2, hy_fb2_2, hy_fw3_2, hy_freq_2,
    hy_bias_2, ml_conv_w_2, ml_gate_b_2, ml_norm_g_2, w_out_0_2, ffn_up_0_2, ffn_conv_w_0_2,
    ffn_conv_b_0_2, ffn_down_0_2, ada_w_1_2, ada_b_1_2, norm_mix_1_2, norm_ffn_1_2,
    mla_w_down_2, mla_q_norm_2, mla_kv_norm_2, mla_w_uq_2, mla_w_ukv_2, mla_w_o_2, ffn_up_1_2,
    ffn_conv_w_1_2, ffn_conv_b_1_2, ffn_down_1_2, final_norm_2,
):
    x = first_block(
        x, c, ctx, c_ctx, w_ada, b_ada, norm1_g, norm2_g, w_in, pool_w, pool_scale, q_norm_g,
        k_norm_g, lambda_qk, subln_g, shift_mu, decay_w0, decay_w2, aaa_a0, aaa_a2, gate_w2,
        k_k, k_a, r_k, gn_w, gn_b, w_br, w_out, w_router_group, w_router_expert, w_exp_gate,
        w_exp_up, w_exp_down,
    )
    return second_block(
        x, c_2, ctx_2, c_ctx_2, ada_w_0_2, ada_b_0_2, norm_mix_0_2, norm_ffn_0_2, w_in_0_2,
        hy_conv_w_2, hy_conv_b_2, hy_fw1_2, hy_fb1_2, hy_fw2_2, hy_fb2_2, hy_fw3_2, hy_freq_2,
        hy_bias_2, ml_conv_w_2, ml_gate_b_2, ml_norm_g_2, w_out_0_2, ffn_up_0_2, ffn_conv_w_0_2,
        ffn_conv_b_0_2, ffn_down_0_2, ada_w_1_2, ada_b_1_2, norm_mix_1_2, norm_ffn_1_2,
        mla_w_down_2, mla_q_norm_2, mla_kv_norm_2, mla_w_uq_2, mla_w_ukv_2, mla_w_o_2,
        ffn_up_1_2, ffn_conv_w_1_2, ffn_conv_b_1_2, ffn_down_1_2, final_norm_2,
    )


_drawn_inputs = setup_inputs


def setup_inputs(seed=0):
    import zlib

    import numpy as np

    out = dict(_drawn_inputs(seed))
    spreads = {}
    factors = {'norm1_g': 3.363,
     'pool_scale': 2.903,
     'q_norm_g': 8.0,
     'k_norm_g': 8.0,
     'lambda_qk': 8.0,
     'subln_g': 5.804,
     'decay_w2': 5.369,
     'aaa_a2': 3.552,
     'k_k': 3.682,
     'k_a': 2.785,
     'gn_w': 8.0,
     'gn_b': 29.579,
     'ctx_2': 2.973,
     'ada_b_0_2': 2.799,
     'norm_mix_0_2': 8.0,
     'norm_ffn_0_2': 31.531,
     'hy_conv_b_2': 8.0,
     'hy_fb1_2': 8.0,
     'hy_fb2_2': 8.0,
     'hy_freq_2': 8.0,
     'ml_norm_g_2': 64.0,
     'ffn_conv_b_0_2': 47.89,
     'ada_b_1_2': 3.174,
     'norm_mix_1_2': 37.092,
     'norm_ffn_1_2': 47.493,
     'mla_q_norm_2': 48.463,
     'mla_kv_norm_2': 57.984,
     'ffn_conv_b_1_2': 64.0,
     'final_norm_2': 8.656,
     'norm2_g': 3.602,
     'ml_conv_w_2': 8.0,
     'ml_gate_b_2': 3.18}
    for name, (base, spread) in spreads.items():
        noise = np.random.default_rng([zlib.crc32(name.encode()), seed]).standard_normal(out[name].shape)
        drawn = base * np.exp(spread * noise) if base else spread * noise
        out[name] = jnp.asarray(drawn.astype(out[name].dtype))
    for name, factor in factors.items():
        out[name] = (out[name] * factor).astype(out[name].dtype)
    return out
```

```python
from contextlib import ExitStack, contextmanager

import numpy as np
import concourse.bass as bass
from concourse import mybir

ALU = mybir.AluOpType
ACT = mybir.ActivationFunctionType
F32 = mybir.dt.float32
AX = mybir.AxisListType.X

P = 128
D = 1024
KD = D // P
CTX = 256
LAT = 512
TOK = CTX + LAT
NT = TOK // P
NTC = CTX // P
NTL = LAT // P
PAD = TOK + 3
SEGS = ((0, 1, CTX), (CTX, CTX + 2, LAT))
BRW = 512
KB = BRW // P
HEADS = 4
HD = 64
RH = 8
CH = 64
N_EXP = 32
N_GRP = 4
EFF = 512
DFF = 2816
KF = DFF // P
EPS = 1e-6
GN_EPS = 64e-5
LAM_INIT = 0.2
BIG = 1e30


class Memory:
    pass


@contextmanager
def stage(nc, **names):
    sems = []
    handles = []
    for key, n in names.items():
        made = [nc.alloc_semaphore(f"{key}_{nc.next_id()}") for _ in range(n)]
        handles += made
        sems.append(made[0] if n == 1 else made)
    with nc.Block() as block:
        yield block, *sems
    nc.clear_and_free_semaphores(handles)
    nc.all_engine_barrier()


class Chain:

    def __init__(self, eng, sem):
        self.eng, self.sem, self.n = eng, sem, 0

    def __call__(self, ins):
        self.n += 1
        ins.then_inc(self.sem, 1)
        self.eng.wait_ge(self.sem, self.n)


def buffers(nc, ctx, **shapes):
    return [ctx.enter_context(nc.sbuf_tensor(f"{name}_{nc.next_id()}", [P, *shape], F32)) for name, shape in shapes.items()]


def bc(ap, n):
    return ap.to_broadcast([ap.shape[0], ap.shape[1], n])



WSLOTS = 3
BANKS = 4


def products(nc, m, jobs, xT, evac, evac_on, bank0=0, kt=KD, wslots=WSLOTS, beside=None, width=512):
    with ExitStack() as ctx:
        slots = [ctx.enter_context(nc.sbuf_tensor(f"w_{nc.next_id()}", [P, kt, width], F32)) for _ in range(wslots)]
        with stage(nc, w_landed=wslots, made=1, read=1, chain=1, aux=1) as (block, w_landed_sem, made_sem, read_sem, chain_sem, aux_sem):
            m.aux_sem = aux_sem
            landed = w_landed_sem if wslots > 1 else [w_landed_sem]

            @block.sync
            def _(sp):
                ended = 0
                for j, (w, n, results) in enumerate(jobs):
                    if j >= wslots:
                        ended += len(jobs[j - wslots][2])
                        sp.wait_ge(made_sem, ended)
                    at = 0
                    for part in (w if isinstance(w, tuple) else (w,)):
                        pn = part.shape[1]
                        sp.dma_start(slots[j % wslots][:, :, at:at + pn], part.rearrange("(k p) n -> p k n", p=P)
                                     ).then_inc(landed[j % wslots], 16)
                        at += pn

            @block.tensor
            def _(pe):
                r = 0
                for j, (w, n, results) in enumerate(jobs):
                    parts = len(w) if isinstance(w, tuple) else 1
                    pe.wait_ge(landed[j % wslots], 16 * parts * (j // wslots + 1))
                    for kind, *at in results:
                        if r >= BANKS:
                            pe.wait_ge(read_sem, r - BANKS + 1)
                        bank = bank0 + r % BANKS
                        for k in range(kt):
                            wk = slots[j % wslots][:, k, :]
                            if kind == "T":
                                c, cw, t0, tn = at
                                out = m.ps[0:cw, bank, 0:tn]
                                lhsT, rhs = wk[:, c:c + cw], xT(k, t0, tn, j)
                            else:
                                t, tw = at
                                out = m.ps[:, bank, 0:tw]
                                lhsT, rhs = xT(k, t * P, P, j), wk[:, 0:tw]
                            mm = nc.tensor.matmul(out, lhsT, rhs, start=(k == 0), stop=(k == kt - 1))
                        mm.then_inc(made_sem, 1)
                        r += 1

            def reader(eng):
                chain = Chain(eng, chain_sem)
                r = 0
                for j, (w, n, results) in enumerate(jobs):
                    for kind, *at in results:
                        eng.wait_ge(made_sem, r + 1)
                        out = m.ps[0:at[1], bank0 + r % BANKS, 0:at[3]] if kind == "T" else m.ps[:, bank0 + r % BANKS, 0:at[1]]
                        evac(out, j, at, chain).then_inc(read_sem, 1)
                        r += 1

            if evac_on == "scalar":
                @block.scalar
                def _(act):
                    reader(act)
            else:
                @block.vector
                def _(dve):
                    reader(dve)

                if beside is not None:
                    @block.scalar
                    def _(act):
                        beside(act, read_sem, aux_sem)


def transposes(nc, m, moves):
    with stage(nc, turned=1, read=1) as (block, turned_sem, read_sem):
        @block.tensor
        def _(pe):
            for i, (blocks, dst, mul, add) in enumerate(moves):
                if i >= 4:
                    pe.wait_ge(read_sem, i - 3)
                for n, b in enumerate(blocks):
                    mm = nc.tensor.transpose(m.ps[:, i % 4, n * P:(n + 1) * P], b, m.ident)
                mm.then_inc(turned_sem, 1)

        @block.vector
        def _(dve):
            for i, (blocks, dst, mul, add) in enumerate(moves):
                dve.wait_ge(turned_sem, i + 1)
                src = m.ps[:, i % 4, 0:len(blocks) * P].rearrange("p (n t) -> p n t", t=P)
                if mul is None:
                    nc.vector.tensor_copy(dst, src).then_inc(read_sem, 1)
                elif add is None:
                    nc.vector.tensor_scalar(dst, src, mul, None, ALU.mult).then_inc(read_sem, 1)
                else:
                    nc.vector.tensor_scalar(dst, src, mul, add, ALU.mult, ALU.add).then_inc(read_sem, 1)


def modulation(nc, m, w_ada, conds, bias, gates, gate_bias_row, mod, gate_rows):
    n_gates = gates
    with ExitStack() as ctx:
        b = Memory()
        b.cond, b.wide, b.bias_row = buffers(nc, ctx, cond=[KD, 2], wide=[KD, 2, P], bias_row=[2, D])
        with stage(nc, in_=1, chain=1, act=1) as (block, in_sem, chain_sem, act_sem):
            @block.sync
            def _(sp):
                for g, chunk in enumerate((2, 5)):
                    sp.dma_start(b.bias_row[:, g, :], gate_bias_row[:, chunk * D:(chunk + 1) * D].to_broadcast([P, D])
                                 ).then_inc(in_sem, 16)
                sp.wait_ge(in_sem, 32)

            @block.scalar
            def _(act):
                for j in range(2):
                    nc.scalar.activation(b.cond[:, :, j], conds[j], ACT.Silu).then_inc(act_sem, 1)

            @block.vector
            def _(dve):
                dve.wait_ge(act_sem, 2)
                for j in range(2):
                    nc.vector.tensor_copy(b.wide[:, :, j, :], bc(b.cond[:, :, j:j + 1], P)).then_inc(chain_sem, 1)
        jobs = []
        for c in range(0, 6 * D, 512):
            res = [("T", x, P, 0, 2) for x in range(0, 512, P)]
            if c // D in (2, 5):
                res = [("N", j, 512) for j in range(n_gates)]
            jobs.append((w_ada[:, c:c + 512], 512, res))

        def operand(k, t0, tn, j):
            return b.cond[:, k, :] if tn == 2 else b.wide[:, k, t0 // P, :]

        def evac(out, j, at, chain):
            c = 512 * j
            if len(at) == 4:
                tile = c // P + at[0] // P
                return nc.vector.tensor_scalar(mod[:, tile, :], out, bias[:, tile:tile + 1], None, ALU.add)
            g = 0 if c // D == 2 else 1
            lo = c % D
            return nc.vector.tensor_tensor(gate_rows[:, g, at[0], lo:lo + 512], out, b.bias_row[:, g, lo:lo + 512], ALU.add)

        products(nc, m, jobs, operand, lambda out, j, at, chain: evac(out, j, at, chain), "vector")


def normed(nc, m, tiles, hT, affine):
    kinds = sorted(affine)
    n = len(tiles)
    with ExitStack() as ctx:
        b = Memory()
        b.xn, b.sq, b.ss, b.root, b.rstd, b.gain = buffers(nc, ctx, xn=[2, D], sq=[D], ss=[n], root=[n], rstd=[n], gain=[len(kinds), KD])
        with stage(nc, summed=1, rooted=1, scaled=1, turned=1, read=1, chain=1) as (
                block, summed_sem, rooted_sem, scaled_sem, turned_sem, read_sem, chain_sem):
            @block.scalar
            def _(act):
                act.wait_ge(summed_sem, 1)
                nc.scalar.activation(b.root[:, :], b.ss[:, :], ACT.Sqrt).then_inc(rooted_sem, 1)

            @block.vector
            def _(dve):
                chain = Chain(dve, chain_sem)
                for i, k in enumerate(kinds):
                    g, scale, shift = affine[k]
                    chain(nc.vector.scalar_tensor_tensor(b.gain[:, i, :], scale, 1.0, g, ALU.add, ALU.mult))
                for i, (x, t0, k) in enumerate(tiles):
                    chain(nc.vector.tensor_tensor_reduce(b.sq[:, :], x, x, 1.0, 0.0, ALU.mult, ALU.add, b.ss[:, i:i + 1]))
                nc.vector.tensor_scalar(b.ss[:, :], b.ss[:, :], 1.0 / D, EPS, ALU.mult, ALU.add).then_inc(summed_sem, 1)
                dve.wait_ge(rooted_sem, 1)
                chain(nc.vector.reciprocal(b.rstd[:, :], b.root[:, :]))

                def scale_rows(i):
                    if i >= 2:
                        dve.wait_ge(turned_sem, 2 * (i - 1))
                    nc.vector.tensor_scalar(b.xn[:, i % 2, :], tiles[i][0], b.rstd[:, i:i + 1], None, ALU.mult).then_inc(scaled_sem, 1)

                scale_rows(0)
                for i, (x, t0, k) in enumerate(tiles):
                    if i + 1 < n:
                        scale_rows(i + 1)
                    shift = affine[k][2]
                    for h in range(2):
                        dve.wait_ge(turned_sem, 2 * i + h + 1)
                        for j in range(4):
                            f = 4 * h + j
                            last = nc.vector.tensor_scalar(
                                hT[:, f, t0:t0 + P], m.ps[:, (2 * i + h) % 4, j * P:(j + 1) * P],
                                b.gain[:, kinds.index(k), f:f + 1], shift[:, f:f + 1], ALU.mult, ALU.add)
                        last.then_inc(read_sem, 1)

            @block.tensor
            def _(pe):
                for i in range(n):
                    pe.wait_ge(scaled_sem, i + 1)
                    for h in range(2):
                        q = 2 * i + h
                        if q >= 4:
                            pe.wait_ge(read_sem, q - 3)
                        for j in range(4):
                            f = 4 * h + j
                            mm = nc.tensor.transpose(m.ps[:, q % 4, j * P:(j + 1) * P], b.xn[:, i % 2, f * P:(f + 1) * P], m.ident)
                        mm.then_inc(turned_sem, 1)


def head_norms(nc, m, xs, width, eps, out_scale=None):
    total = sum(x.shape[1] for x, g in xs)
    biggest = max(x.shape[1] for x, g in xs)
    with ExitStack() as ctx:
        b = Memory()
        b.sq, b.ss, b.root, b.rstd = buffers(nc, ctx, sq=[biggest, width], ss=[total], root=[total], rstd=[total, 1])
        with stage(nc, summed=1, rooted=1, chain=1) as (block, summed_sem, rooted_sem, chain_sem):
            @block.scalar
            def _(act):
                act.wait_ge(summed_sem, 1)
                nc.scalar.activation(b.root[:, :], b.ss[:, :], ACT.Sqrt).then_inc(rooted_sem, 1)

            @block.vector
            def _(dve):
                chain = Chain(dve, chain_sem)
                o = 0
                for x, g in xs:
                    a = x.shape[1]
                    chain(nc.vector.tensor_tensor(b.sq[:, 0:a, :], x, x, ALU.mult))
                    chain(nc.vector.tensor_reduce(b.ss[:, o:o + a], b.sq[:, 0:a, :], AX, ALU.add))
                    o += a
                nc.vector.tensor_scalar(b.ss[:, :], b.ss[:, :], 1.0 / width, eps, ALU.mult, ALU.add).then_inc(summed_sem, 1)
                dve.wait_ge(rooted_sem, 1)
                chain(nc.vector.reciprocal(b.rstd[:, :, 0], b.root[:, :]))
                o = 0
                for x, g in xs:
                    a = x.shape[1]
                    chain(nc.vector.tensor_tensor(x, x, bc(b.rstd[:, o:o + a, :], width), ALU.mult))
                    if g is not None:
                        chain(nc.vector.tensor_tensor(x, x, g.unsqueeze(1).to_broadcast([P, a, width]), ALU.mult))
                    o += a


def rope(nc, m, tiles):
    with ExitStack() as ctx:
        b = Memory()
        (b.swapped,) = buffers(nc, ctx, swapped=[2, 8, HD])
        with stage(nc, chain=1) as (block, chain_sem):
            @block.vector
            def _(dve):
                chain = Chain(dve, chain_sem)
                for i, (x, heads, t) in enumerate(tiles):
                    xv = x.rearrange("p n (a h e) -> p n a h e", a=2, h=2)
                    sw = b.swapped[:, i % 2, 0:heads, :].rearrange("p n (a h e) -> p n a h e", a=2, h=2)
                    sn = m.rope_sin[:, t, :].rearrange("p (a h e) -> p a h e", a=2, h=2)
                    for h in range(2):
                        nc_sin = sn[:, :, h, :].unsqueeze(1).to_broadcast([P, heads, 2, 16])
                        chain(nc.vector.tensor_tensor(sw[:, :, :, h, :], xv[:, :, :, 1 - h, :], nc_sin, ALU.mult))
                    cs = m.rope_cos[:, t, :].unsqueeze(1).to_broadcast([P, heads, HD])
                    chain(nc.vector.tensor_tensor(x, x, cs, ALU.mult))
                    chain(nc.vector.tensor_tensor(x, x, b.swapped[:, i % 2, 0:heads, :], ALU.add))


def attention(nc, m, items, maps, scale, other_weight):
    n = len(items)
    with ExitStack() as ctx:
        b = Memory()
        b.e, b.a, b.aT, b.mx, b.nb, b.sums, b.rec = buffers(
            nc, ctx, e=[2, maps, TOK], a=[2, TOK], aT=[TOK], mx=[maps], nb=[2, maps], sums=[2, maps], rec=[maps])
        with stage(nc, scored=1, biased=1, exped=1, mixed=1, turned=1, copied=1, valued=1, stored=1, chain=1) as (
                block, scored_sem, biased_sem, exped_sem, mixed_sem, turned_sem, copied_sem, valued_sem, stored_sem, chain_sem):
            @block.tensor
            def _(pe):
                def scores(i):
                    if i >= 1:
                        pe.wait_ge(exped_sem, maps * i)
                    for q in range(maps):
                        parts = items[i][0][q]
                        for j, (lhsT, rhs) in enumerate(parts):
                            for c, w in ((0, 512), (512, 256)):
                                mm = nc.tensor.matmul(m.ps[:, 2 * q + c // 512, 0:w], lhsT, rhs[:, c:c + w],
                                                      start=(j == 0), stop=(j == len(parts) - 1))
                    mm.then_inc(scored_sem, 1)

                scores(0)
                for i in range(n):
                    if i + 1 < n:
                        scores(i + 1)
                    pe.wait_ge(mixed_sem, i + 1)
                    if i >= 1:
                        pe.wait_ge(copied_sem, i)
                    for k in range(NT):
                        mm = nc.tensor.transpose(m.ps[:, 4 + k // 4, (k % 4) * P:(k % 4 + 1) * P], b.a[:, i % 2, k * P:(k + 1) * P], m.ident)
                    mm.then_inc(turned_sem, 1)
                    pe.wait_ge(copied_sem, i + 1)
                    if i >= 1:
                        pe.wait_ge(stored_sem, i)
                    for k in range(NT):
                        mm = nc.tensor.matmul(m.ps[:, 6, 0:P], b.aT[:, k * P:(k + 1) * P], items[i][1](k),
                                              start=(k == 0), stop=(k == NT - 1))
                    mm.then_inc(valued_sem, 1)

            @block.scalar
            def _(act):
                for i in range(n):
                    act.wait_ge(biased_sem, i + 1)
                    for q in range(maps):
                        nc.scalar.activation(b.e[:, i % 2, q, :], m.ps[:, 2 * q:2 * q + 2, :].rearrange("p a b -> p (a b)")[:, 0:TOK],
                                             ACT.Exp, bias=b.nb[:, i % 2, q:q + 1], scale=scale,
                                             accum_out=b.sums[:, i % 2, q:q + 1]).then_inc(exped_sem, 1)
                    act.wait_ge(turned_sem, i + 1)
                    if i >= 1:
                        act.wait_ge(valued_sem, i)
                    nc.scalar.copy(b.aT[:, :], m.ps[:, 4:6, :].rearrange("p a b -> p (a b)")[:, 0:TOK]).then_inc(copied_sem, 1)

            @block.vector
            def _(dve):
                chain = Chain(dve, chain_sem)

                def maxima(i):
                    dve.wait_ge(scored_sem, i + 1)
                    for q in range(maps):
                        last = nc.vector.tensor_reduce(b.mx[:, q:q + 1], m.ps[:, 2 * q:2 * q + 2, :].rearrange("p a b -> p (a b)")[:, 0:TOK], AX, ALU.max)
                        chain(last)
                    if i >= 2:
                        dve.wait_ge(exped_sem, maps * (i - 1))
                    nc.vector.tensor_scalar(b.nb[:, i % 2, :], b.mx[:, :], -scale, None, ALU.mult).then_inc(biased_sem, 1)

                maxima(0)
                for i in range(n):
                    dve.wait_ge(exped_sem, maps * (i + 1))
                    chain(nc.vector.reciprocal(b.rec[:, :], b.sums[:, i % 2, :]))
                    if i >= 2:
                        dve.wait_ge(turned_sem, i - 1)
                    if maps == 1:
                        nc.vector.tensor_scalar(b.a[:, i % 2, :], b.e[:, i % 2, 0, :], b.rec[:, 0:1], None, ALU.mult).then_inc(mixed_sem, 1)
                    else:
                        chain(nc.vector.tensor_tensor(b.rec[:, 1:2], b.rec[:, 1:2], other_weight, ALU.mult))
                        chain(nc.vector.tensor_scalar(b.a[:, i % 2, :], b.e[:, i % 2, 0, :], b.rec[:, 0:1], None, ALU.mult))
                        nc.vector.scalar_tensor_tensor(b.a[:, i % 2, :], b.e[:, i % 2, 1, :], b.rec[:, 1:2], b.a[:, i % 2, :],
                                                       ALU.mult, ALU.add).then_inc(mixed_sem, 1)
                    if i + 1 < n:
                        maxima(i + 1)
                    dve.wait_ge(valued_sem, i + 1)
                    nc.vector.tensor_copy(items[i][2], m.ps[:, 6, 0:P]).then_inc(stored_sem, 1)


def cols(m, name):
    a, n = m.where[name]
    return m.cols[:, a:a + n]


def load(nc, pairs):
    with stage(nc, landed=1) as (block, landed_sem):
        @block.sync
        def _(sp):
            for dst, src in pairs:
                sp.dma_start(dst[:], src).then_inc(landed_sem, 16)
            sp.wait_ge(landed_sem, 16 * len(pairs))


def load_constants(nc, m, a):
    m.loads = [(m.ident, a["ident"]), (m.cols, a["cols"]), (m.rope_cos, a["rope_cos"]), (m.rope_sin, a["rope_sin"]),
               (m.qk_gain, a["rows"][:, 0:2 * HD].to_broadcast([P, 2 * HD])),
               (m.lam_rows, a["rows"][:, 2 * HD:6 * HD].to_broadcast([P, 4 * HD])),
               (m.masks, a["masks"]), (m.restart, a["restart"]), (m.headsum, a["headsum"]), (m.headspread, a["headspread"]),
               (m.head_mask, a["head_mask"])]
    with stage(nc, landed=1, lam=1, chain=1) as (block, landed_sem, lam_sem, chain_sem):
        @block.sync
        def _(sp):
            for dst, src in m.loads:
                sp.dma_start(dst[:], src).then_inc(landed_sem, 16)
            sp.wait_ge(landed_sem, 16 * len(m.loads))

        @block.vector
        def _(dve):
            chain = Chain(dve, chain_sem)
            dve.wait_ge(landed_sem, 16 * len(m.loads))
            pairs = m.lam_rows[:, :].rearrange("p (a b c) -> p a b c", a=2, b=2)
            chain(nc.vector.tensor_tensor(m.lam_prod[:, :, :], pairs[:, :, 0, :], pairs[:, :, 1, :], ALU.mult))
            nc.vector.tensor_reduce(m.lam_sum[:, :], m.lam_prod[:, :, :], AX, ALU.add).then_inc(lam_sem, 1)
            dve.wait_ge(lam_sem, 2)
            chain(nc.vector.tensor_tensor(m.neg_lam[:, :], m.lam_exp[:, 1:2], m.lam_exp[:, 0:1], ALU.subtract))
            chain(nc.vector.tensor_scalar(m.neg_lam[:, :], m.neg_lam[:, :], -LAM_INIT, None, ALU.add))
            chain(nc.vector.tensor_scalar(m.subln[:, :], cols(m, "subln_g"), 1.0 - LAM_INIT, None, ALU.mult))

        @block.scalar
        def _(act):
            act.wait_ge(lam_sem, 1)
            nc.scalar.activation(m.lam_exp[:, :], m.lam_sum[:, :], ACT.Exp).then_inc(lam_sem, 1)


def block_one(nc, m, a):
    with ExitStack() as outer:
        m.hT, m.mod, m.gate_rows = buffers(nc, outer, hT=[KD, TOK], mod=[48, 2], gate_rows=[2, 1, D])
        branches = outer.enter_context(ExitStack())
        (m.br_rw,) = buffers(nc, branches, br_rw=[KB, LAT])
        with ExitStack() as c1:
            m.lam_rows, m.lam_prod, m.lam_sum, m.lam_exp = buffers(nc, c1, lam_rows=[4 * HD], lam_prod=[2, HD], lam_sum=[2], lam_exp=[2])
            load_constants(nc, m, a)
        modulation(nc, m, a["w_ada"], (cols(m, "c"), cols(m, "c_ctx")), cols(m, "b_ada"), 1, a["b_ada_row"], m.mod, m.gate_rows)

        def mods(chunk, j):
            return m.mod[:, 8 * chunk:8 * chunk + 8, j]

        g1 = cols(m, "norm1_g")
        with ExitStack() as rows:
            m.x, m.xc = buffers(nc, rows, x=[NTL, D], xc=[NTC, D])
            load(nc, [(m.x, a["x"].rearrange("(t p) d -> p t d", p=P)), (m.xc, a["ctx"].rearrange("(t p) d -> p t d", p=P))])
            normed(nc, m, [(m.xc[:, t, :], t * P, "ctx") for t in range(NTC)] + [(m.x[:, t, :], CTX + t * P, "lat") for t in range(NTL)],
                   m.hT, {"ctx": (g1, mods(1, 1), mods(0, 1)), "lat": (g1, mods(1, 0), mods(0, 0))})
        rwkv_branch(nc, m, a)
        m.x = m.keep.enter_context(nc.sbuf_tensor("x_rows", [P, NTL, D], F32, side="right"))
        (m.brT,) = buffers(nc, branches, brT=[2, KB, LAT])
        attention_branch(nc, m, a)
        pool_branch(nc, m, a)
        load(nc, [(m.x, a["x"].rearrange("(t p) d -> p t d", p=P))])
        with ExitStack() as mix:
            (m.merged,) = buffers(nc, mix, merged=[KD, LAT])
            merge(nc, m, a)
            project_add(nc, m, a["w_out"], lambda k, t0, tn, j: m.merged[:, k, t0:t0 + tn], KD,
                        [(t, m.x[:, t, :], m.gate_rows[:, 0, 0, :]) for t in range(NTL)])
        branches.close()
        normed(nc, m, [(m.x[:, t, :], CTX + t * P, "lat") for t in range(NTL)], m.hT, {"lat": (cols(m, "norm2_g"), mods(4, 0), mods(3, 0))})
        expert_layer(nc, m, a)


def hT_of(m):
    return lambda k, t0, tn, j: m.hT[:, k, t0:t0 + tn]


def attention_branch(nc, m, a):
    with ExitStack() as ctx:
        m.v, m.qT, m.kT = buffers(nc, ctx, v=[NT, 512], qT=[HEADS, LAT], kT=[HEADS, TOK])
        with ExitStack() as rows:
            m.q, m.k = buffers(nc, rows, q=[NTL, 512], k=[NT, 512])
            jobs = [(a["w_in"][:, 512:1024], 512, [("N", NTC + t, 512) for t in range(NTL)]),
                    (a["w_in"][:, 1024:1536], 512, [("N", t, 512) for t in range(NT)]),
                    (a["w_in"][:, 1536:2048], 512, [("N", t, 512) for t in range(NT)])]

            def evac(out, j, at, chain):
                dst = (m.q, m.k, m.v)[j][:, at[0] - (NTC if j == 0 else 0), :]
                return nc.vector.tensor_copy(dst, out)

            products(nc, m, jobs, hT_of(m), evac, "vector")
            head_norms(nc, m, [(m.q[:].rearrange("p t (n e) -> p (t n) e", e=HD), m.qk_gain[:, 0:HD]),
                               (m.k[:].rearrange("p t (n e) -> p (t n) e", e=HD), m.qk_gain[:, HD:2 * HD])], HD, EPS)
            heads = lambda x, t: x[:, t, :].rearrange("p (n e) -> p n e", e=HD)
            rope(nc, m, [(heads(m.q, t), 8, t) for t in range(NTL)] + [(heads(m.k, NTC + t), 8, t) for t in range(NTL)])
            transposes(nc, m, [([m.q[:, t, h * P:(h + 1) * P] for h in range(4)], m.qT[:, :, t * P:(t + 1) * P], None, None) for t in range(NTL)]
                       + [([m.k[:, t, h * P:(h + 1) * P] for h in range(4)], m.kT[:, :, t * P:(t + 1) * P], None, None) for t in range(NT)])
        (m.att,) = buffers(nc, ctx, att=[NTL, 512])
        items = []
        for t in range(NTL):
            for h in range(HEADS):
                scores = [[(m.qT[q * HD:(q + 1) * HD, h, t * P:(t + 1) * P], m.kT[q * HD:(q + 1) * HD, h, :])] for q in range(2)]
                items.append((scores, lambda k, h=h: m.v[:, k, h * P:(h + 1) * P], m.att[:, t, h * P:(h + 1) * P]))
        attention(nc, m, items, 2, HD ** -0.5, m.neg_lam[:, :])
        head_norms(nc, m, [(m.att[:].rearrange("p t (h e) -> p (t h) e", e=P), None)], P, EPS)
        transposes(nc, m, [([m.att[:, t, h * P:(h + 1) * P] for h in range(4)], m.brT[:, 1, :, t * P:(t + 1) * P], m.subln[:, :], None) for t in range(NTL)])


def pool_branch(nc, m, a):
    with ExitStack() as ctx:
        m.u, m.bands, m.pw, m.diffT = buffers(nc, ctx, u=[NTL, 512], bands=[2, NTL, LAT], pw=[4, P], diffT=[2, LAT])

        def evac(out, j, at, chain):
            return nc.scalar.copy(m.u[:, at[0] - NTC, :], out)

        products(nc, m, [(a["w_in"][:, 0:512], 512, [("N", NTC + t, 512) for t in range(NTL)])], hT_of(m), evac, "scalar", wslots=1)
        with stage(nc, weights=1, banded=2, diffed=1, copied=1, mapped=1, read=1) as (
                block, weights_sem, banded_sem, diffed_sem, copied_sem, mapped_sem, read_sem):
            @block.sync
            def _(sp):
                sp.dma_start(m.pw[:], a["pool_w"].rearrange("g c d -> c g d")).then_inc(weights_sem, 16)
                for g in range(4):
                    if g >= 2:
                        sp.wait_ge(diffed_sem, g - 1)
                    sp.dma_start(m.bands[:, g % 2], a["bands"][g].rearrange("(k p) t -> p k t", p=P)).then_inc(banded_sem[g % 2], 16)

            @block.tensor
            def _(pe):
                for g in range(4):
                    pe.wait_ge(banded_sem[g % 2], 16 * (g // 2 + 1))
                    if g >= 2:
                        pe.wait_ge(copied_sem, g - 1)
                    for k in range(NTL):
                        mm = nc.tensor.matmul(m.ps[:, g % 2, :], m.u[:, k, g * P:(g + 1) * P], m.bands[:, g % 2, k, :],
                                              start=(k == 0), stop=(k == NTL - 1))
                    mm.then_inc(diffed_sem, 1)
                    pe.wait_ge(copied_sem, g + 1)
                    if g == 0:
                        pe.wait_ge(weights_sem, 16)
                    if g >= 2:
                        pe.wait_ge(read_sem, g - 1)
                    nc.tensor.matmul(m.ps[:, 2 + g % 2, :], m.pw[:, g, :], m.diffT[:, g % 2, :], start=True, stop=True).then_inc(mapped_sem, 1)

            @block.vector
            def _(dve):
                for g in range(4):
                    dve.wait_ge(diffed_sem, g + 1)
                    if g >= 2:
                        dve.wait_ge(mapped_sem, g - 1)
                    nc.vector.tensor_copy(m.diffT[:, g % 2, :], m.ps[:, g % 2, :]).then_inc(copied_sem, 1)
                    dve.wait_ge(mapped_sem, g + 1)
                    nc.vector.tensor_scalar(m.brT[:, 0, g, :], m.ps[:, 2 + g % 2, :], cols(m, "pool_scale")[:, g:g + 1], None,
                                            ALU.mult).then_inc(read_sem, 1)



DECAY_C = float(np.exp(-0.5))
MASKS = ("below16", "rest_below", "above16", "rest_above", "above_eq", "below_eq", "above", "below")


def mask(m, name, n):
    return m.masks[:, MASKS.index(name), :].unsqueeze(1).to_broadcast([P, n, P])


def pad_zeros(nc, m, bufs):
    with stage(nc, done=1) as (block, done_sem):
        @block.vector
        def _(dve):
            for b in bufs:
                for at in (0, CTX + 1, PAD - 1):
                    nc.vector.memset(b[:, at:at + 1], 0.0).then_inc(done_sem, 1)


def taps(dve, chain, pad, seg, w, bias, dst):
    t0, p0, n = SEGS[seg]
    if bias is None:
        chain(dve.tensor_scalar(dst, pad[:, p0 - 1:p0 - 1 + n], w[0], None, ALU.mult))
    else:
        chain(dve.tensor_scalar(dst, pad[:, p0 - 1:p0 - 1 + n], w[0], bias, ALU.mult, ALU.add))
    chain(dve.scalar_tensor_tensor(dst, pad[:, p0:p0 + n], w[1], dst, ALU.mult, ALU.add))
    return dve.scalar_tensor_tensor(dst, pad[:, p0 + 1:p0 + 1 + n], w[2], dst, ALU.mult, ALU.add)


def rwkv_branch(nc, m, a):
    with ExitStack() as ctx:
        m.rw, m.v_rows, m.y, m.coef, m.knorm = buffers(nc, ctx, rw=[15, TOK], v_rows=[NT, 512], y=[NTL, 512], coef=[LAT], knorm=[TOK])
        rwkv_inputs(nc, m, a)
        with ExitStack() as run:
            m.w2, m.a2, m.at, m.bt, m.kt, m.rt, m.wc, m.zeros, m.bt_rows, m.kt_rows, m.z, m.u, m.S, m.wmask = buffers(
                nc, run, w2=[512], a2=[512], at=[4, P], bt=[4, P], kt=[4, P], rt=[4, P], wc=[4, 2], zeros=[512], bt_rows=[512], kt_rows=[512], z=[512], u=[512], S=[4, P], wmask=[4, P])
            pairs = [2, 4, P]
            m.D, m.DT, m.N, m.NT, m.AKT, m.RBT, m.RKT = buffers(
                nc, run, D=pairs, DT=pairs, N=pairs, NT=pairs, AKT=pairs, RBT=pairs, RKT=pairs)
            m.D2, m.D2T, m.D4, m.D4T, m.D8, m.ET = buffers(nc, run, D2=pairs, D2T=pairs, D4=pairs, D4T=pairs, D8=pairs, ET=pairs)
            m.filled = nc.alloc_semaphore("rows_filled")
            m.y_dram = nc.dram_tensor("expert_rows", [TAB * SLOTS, D], F32).ap()
            rwkv_start(nc, m, a)
            for d in range(2):
                order = range(NT) if d == 0 else [1, 0, 5, 4, 3, 2]
                for n, t in enumerate(order):
                    rwkv_rows(nc, m, d, t)
                    rwkv_products(nc, m, d, t)
                    rwkv_inverse(nc, m)
                    rwkv_chunks(nc, m, d, t, first=(n == 0), last=(n == NT - 1))
            with nc.Block() as block:
                @block.sync
                def _(sp):
                    sp.wait_ge(m.filled, 16 * FILLS)
        rwkv_result(nc, m, a)


def rwkv_inputs(nc, m, a):
    with ExitStack() as ctx:
        m.pad, m.mid = buffers(nc, ctx, pad=[2, PAD], mid=[15])
        pad_zeros(nc, m, [m.pad[:, 0, :], m.pad[:, 1, :]])
        mu0, mu1 = cols(m, "mu0"), cols(m, "mu1")
        with stage(nc, chain=1) as (block, chain_sem):
            @block.vector
            def _(dve):
                chain = Chain(dve, chain_sem)
                chain(nc.vector.tensor_tensor(m.mid[:, :], mu0, mu1, ALU.add))
                chain(nc.vector.tensor_scalar(m.mid[:, :], m.mid[:, :], -1.0, 1.0, ALU.mult, ALU.add))
        jobs, where = [], []
        for c in range(0, 1920, 512):
            n = min(512, 1920 - c)
            results = []
            for x in range(0, n, P):
                tile = (c + x) // P
                for seg in ((1,) if tile < 4 or tile == 14 else (0, 1)):
                    t0, p0, tn = SEGS[seg]
                    results.append(("T", x, P, t0, tn))
            jobs.append((a["w_in"][:, 2048 + c:2048 + c + n], n, results))

        def evac(out, j, at, chain):
            tile = 4 * j + at[0] // P
            seg = 0 if at[2] == 0 else 1
            t0, p0, tn = SEGS[seg]
            pad = m.pad[:, tile % 2, :]
            chain(nc.vector.tensor_copy(pad[:, p0:p0 + tn], out))
            return taps(nc.vector, chain, pad, seg, (mu0[:, tile:tile + 1], m.mid[:, tile:tile + 1], mu1[:, tile:tile + 1]),
                        None, m.rw[:, tile, t0:t0 + tn])

        products(nc, m, jobs, hT_of(m), evac, "vector", wslots=2)
    transposes(nc, m, [([m.rw[:, 8 + p, t * P:(t + 1) * P] for p in range(4)], m.v_rows[:, t, :].rearrange("p (n e) -> p n e", e=P), None, None)
                       for t in range(NT)])
    with ExitStack() as ctx:
        (m.sq,) = buffers(nc, ctx, sq=[4, TOK])
        with stage(nc, squared=1, summed=1, rooted=1, chain=1) as (block, squared_sem, summed_sem, rooted_sem, chain_sem):
            @block.scalar
            def _(act):
                nc.scalar.activation(m.rw[:, 12, :], m.rw[:, 12, :], ACT.Tanh)
                nc.scalar.activation(m.rw[:, 14, CTX:TOK], m.rw[:, 14, CTX:TOK], ACT.Sigmoid)
                act.wait_ge(summed_sem, 1)
                nc.scalar.activation(m.knorm[0:RH, :], m.ps[0:RH, 0:2, :].rearrange("p a b -> p (a b)")[:, 0:TOK], ACT.Sqrt).then_inc(rooted_sem, 1)

            @block.vector
            def _(dve):
                chain = Chain(dve, chain_sem)
                chain(nc.vector.tensor_tensor(m.sq[:, :, :], m.rw[:, 4:8, :], bc(cols(m, "k_k").unsqueeze(2), TOK), ALU.mult))
                nc.vector.tensor_tensor(m.sq[:, :, :], m.sq[:, :, :], m.sq[:, :, :], ALU.mult).then_inc(squared_sem, 1)
                dve.wait_ge(rooted_sem, 1)
                chain(nc.vector.tensor_scalar(m.knorm[0:RH, :], m.knorm[0:RH, :], 1e-12, None, ALU.max))
                chain(nc.vector.reciprocal(m.knorm[0:RH, :], m.knorm[0:RH, :]))

            @block.tensor
            def _(pe):
                pe.wait_ge(squared_sem, 1)
                for c, w in ((0, 512), (512, 256)):
                    for p in range(4):
                        mm = nc.tensor.matmul(m.ps[0:RH, c // 512, 0:w], m.headsum[:, p, :], m.sq[:, p, c:c + w], start=(p == 0), stop=(p == 3))
                mm.then_inc(summed_sem, 1)


def rwkv_start(nc, m, a):
    with stage(nc, landed=1, done=1) as (block, landed_sem, done_sem):
        @block.sync
        def _(sp):
            sp.dma_start(m.w2[:, :], a["decay_w2"].rearrange("d r c -> (d r) c")).then_inc(landed_sem, 16)
            sp.dma_start(m.a2[:, :], a["aaa_a2"].rearrange("d r c -> (d r) c")).then_inc(landed_sem, 16)
            sp.wait_ge(landed_sem, 32)
            sp.wait_ge(done_sem, 1)
            fill_rows(nc, m, m.zeros[:, :])

        @block.vector
        def _(dve):
            nc.vector.memset(m.zeros[:, :], 0.0).then_inc(done_sem, 1)
            nc.vector.memset(m.z[:, :], 0.0).then_inc(done_sem, 1)
            nc.vector.memset(m.u[:, :], 0.0).then_inc(done_sem, 1)


def rwkv_rows(nc, m, d, t):
    t0 = t * P
    lat = t >= NTC
    r, k = m.rw[:, 0:4, t0:t0 + P], m.rw[:, 4:8, t0:t0 + P]
    rows = slice(HD * d, HD * (d + 1))
    with ExitStack() as ctx:
        b = Memory()
        b.sg, b.aa, b.cs, b.kk, b.km, b.e_up, b.e_dn, b.e_pr, b.cf = [
            x[:, i] for x in (m.D2, m.D2T, m.D4, m.D4T, m.D8) for i in range(2)][0:9]
        col = lambda name, o=0: bc(cols(m, name)[:, o:o + 4].unsqueeze(2), P)
        with stage(nc, made=1, gated=1, run=1, exps=1, coefs=1, summed=1, chain=1) as (
                block, made_sem, gated_sem, run_sem, exps_sem, coefs_sem, summed_sem, chain_sem):
            @block.tensor
            def _(pe):
                for w, x, bank in ((m.w2, 12, 0), (m.a2, 13, 1)):
                    for p in range(4):
                        nc.tensor.matmul(m.ps[:, bank, p * P:(p + 1) * P], w[rows, p * P:(p + 1) * P], m.rw[rows, x, t0:t0 + P], start=True, stop=True)
                for p in range(4):
                    mm = nc.tensor.matmul(m.ps[:, 2, p * P:(p + 1) * P], m.headspread[0:RH, p, :], m.knorm[0:RH, t0:t0 + P], start=True, stop=True)
                mm.then_inc(made_sem, 1)
                if lat:
                    pe.wait_ge(coefs_sem, 1)
                    for p in range(4):
                        mm = nc.tensor.matmul(m.ps[0:RH, 3, 0:P], m.headsum[:, p, :], b.cf[:, p, :], start=(p == 0), stop=(p == 3))
                    mm.then_inc(summed_sem, 1)

            @block.scalar
            def _(act):
                act.wait_ge(made_sem, 1)
                for name, dst, bank in (("w0", b.sg, 0), ("a0", b.aa, 1)):
                    for p in range(4):
                        nc.scalar.activation(dst[:, p, :], m.ps[:, bank, p * P:(p + 1) * P], ACT.Sigmoid,
                                             bias=cols(m, name)[:, 4 * d + p:4 * d + p + 1]).then_inc(gated_sem, 1)
                act.wait_ge(run_sem, 2)
                nc.scalar.activation(b.e_up[:, :, :], b.cs[:, :, :], ACT.Exp, scale=DECAY_C).then_inc(exps_sem, 1)
                nc.scalar.activation(b.e_dn[:, :, :], b.cs[:, :, :], ACT.Exp, scale=-DECAY_C).then_inc(exps_sem, 1)
                nc.scalar.activation(b.e_pr[:, :, :], b.sg[:, :, :], ACT.Exp, scale=-DECAY_C).then_inc(exps_sem, 1)

            @block.vector
            def _(dve):
                chain = Chain(dve, chain_sem)
                chain(nc.vector.tensor_tensor(b.kk[:, :, :], k, col("k_k"), ALU.mult))
                dve.wait_ge(made_sem, 1)
                chain(nc.vector.tensor_tensor(b.kk[:, :, :], b.kk[:, :, :], m.ps[:, 2, :].rearrange("p (n e) -> p n e", e=P), ALU.mult))
                dve.wait_ge(gated_sem, 8)
                flat = lambda x: x[:, :, :].rearrange("p n e -> p (n e)")
                sg, cs = flat(b.sg), flat(b.cs)
                restart = m.restart[:, d, :]
                if d:
                    sg, cs, restart = sg[:, ::-1], cs[:, ::-1], restart[:, ::-1]
                nc.vector.tensor_tensor_scan(cs, restart, sg, 0.0, ALU.mult, ALU.add).then_inc(run_sem, 1)
                dve.wait_ge(run_sem, 1)
                nc.vector.tensor_tensor(b.sg[:, :, :], b.cs[:, :, :], b.sg[:, :, :], ALU.subtract).then_inc(run_sem, 1)
                chain(nc.vector.scalar_tensor_tensor(b.km[:, :, :], b.aa[:, :, :], 1.0, col("k_a"), ALU.subtract, ALU.mult))
                chain(nc.vector.scalar_tensor_tensor(b.km[:, :, :], b.km[:, :, :], 1.0, k, ALU.add, ALU.mult))
                chain(nc.vector.tensor_tensor(b.aa[:, :, :], b.aa[:, :, :], b.kk[:, :, :], ALU.mult))
                if lat:
                    chain(nc.vector.tensor_tensor(b.cf[:, :, :], b.km[:, :, :], r, ALU.mult))
                    nc.vector.tensor_tensor(b.cf[:, :, :], b.cf[:, :, :], col("r_k"), ALU.mult).then_inc(coefs_sem, 1)
                dve.wait_ge(exps_sem, 3)
                chain(nc.vector.tensor_tensor(m.bt[:, :, :], b.aa[:, :, :], b.e_up[:, :, :], ALU.mult))
                chain(nc.vector.tensor_tensor(m.kt[:, :, :], b.km[:, :, :], b.e_up[:, :, :], ALU.mult))
                chain(nc.vector.scalar_tensor_tensor(m.at[:, :, :], b.kk[:, :, :], -1.0, b.e_pr[:, :, :], ALU.mult, ALU.mult))
                end = 0 if d else CH - 1
                chain(nc.vector.tensor_copy(m.wc[:, :, :], b.e_dn[:, :, :].rearrange("p n (c e) -> p n c e", e=CH)[:, :, :, end]))
                if lat:
                    chain(nc.vector.tensor_tensor(m.rt[:, :, :], r, b.e_dn[:, :, :], ALU.mult))
                    dve.wait_ge(summed_sem, 1)
                    c = m.coef[0:RH, t0 - CTX:t0 - CTX + P]
                    if d == 0:
                        chain(nc.vector.tensor_copy(c, m.ps[0:RH, 3, 0:P]))
                    else:
                        chain(nc.vector.tensor_tensor(c, c, m.ps[0:RH, 3, 0:P], ALU.add))


def rwkv_products(nc, m, d, t):
    lat = t >= NTC
    lo, up = ("below", "above") if d == 0 else ("above", "below")
    kinds = [(m.at, m.bt, [(m.D, lo + "16"), (m.N, "rest_" + lo)]), (m.bt, m.at, [(m.DT, up + "16"), (m.NT, "rest_" + up)]),
             (m.kt, m.at, [(m.AKT, up)])]
    if lat:
        kinds += [(m.bt, m.rt, [(m.RBT, up + "_eq")]), (m.kt, m.rt, [(m.RKT, up + "_eq")])]
    with stage(nc, turned=1, made=1, read=1, chain=1) as (block, turned_sem, made_sem, read_sem, chain_sem):
        @block.tensor
        def _(pe):
            for i, (lhs, rhs, outs) in enumerate(kinds):
                for hh in range(2):
                    q = 2 * i + hh
                    if q >= 6:
                        pe.wait_ge(read_sem, q - 5)
                    h = slice(HD * hh, HD * (hh + 1))
                    for p in range(4):
                        mm = nc.tensor.matmul(m.ps[:, 2 + q % 6, p * P:(p + 1) * P], lhs[h, p, :], rhs[h, p, :], start=True, stop=True)
                    mm.then_inc(made_sem, 1)
                if i == 1:
                    for bank, x in ((0, m.bt), (1, m.kt)):
                        for p in range(4):
                            mm = nc.tensor.transpose(m.ps[:, bank, p * P:(p + 1) * P], x[:, p, :], m.ident)
                        mm.then_inc(turned_sem, 1)

        @block.scalar
        def _(act):
            for i, dst in enumerate((m.bt_rows, m.kt_rows)):
                act.wait_ge(turned_sem, i + 1)
                nc.scalar.copy(dst[:, :], m.ps[:, i, :])

        @block.vector
        def _(dve):
            for i, (lhs, rhs, outs) in enumerate(kinds):
                for hh in range(2):
                    q = 2 * i + hh
                    dve.wait_ge(made_sem, q + 1)
                    src = m.ps[:, 2 + q % 6, :].rearrange("p (n e) -> p n e", e=P)
                    for dst, name in outs:
                        last = nc.vector.tensor_tensor(dst[:, hh, :, :], src, mask(m, name, 4), ALU.mult)
                    last.then_inc(read_sem, 1)


def rwkv_inverse(nc, m):
    copies = (2, 2, 1, 0, 1, 2, 1, 0, 0)
    adds = (0, 1, 1, 1, 0, 0, 0, 1, 1)
    with stage(nc, ready=1, made=2, copied=2, added=2) as (block, ready_sem, made_sem, copied_sem, added_sem):
        def rounds(hh):
            x = lambda b: b[:, hh]
            D, DT, N, NT, D2, D2T, D4, D4T, D8, ET = (x(b) for b in (m.D, m.DT, m.N, m.NT, m.D2, m.D2T, m.D4, m.D4T, m.D8, m.ET))
            E, M, MT, M2, Y = D8, D2, D2T, D4, D4T
            return [([(DT, D, D2), (D, DT, D2T)], []),
                    ([(D2T, D2, D4), (D2, D2T, D4T)], [(D2, ET, ET, ET)]),
                    ([(D4T, D4, D8)], [(D4, ET, ET, ET)]),
                    ([], [(D8, ET, ET, ET)]),
                    ([(ET, None, E)], []),
                    ([(NT, E, M), (E, NT, MT)], []),
                    ([(MT, M, M2)], []),
                    ([], [(M2, ET, ET, Y)]),
                    ([], [(M, Y, Y, D)])]

        @block.tensor
        def _(pe):
            for r in range(9):
                for hh in range(2):
                    copy, add = rounds(hh)[r]
                    if r == 1:
                        pe.wait_ge(ready_sem, hh + 1)
                    if sum(copies[:r]):
                        pe.wait_ge(copied_sem[hh], sum(copies[:r]))
                    if sum(adds[:r]):
                        pe.wait_ge(added_sem[hh], sum(adds[:r]))
                    for q, (lhsT, rhs, *_) in enumerate(copy + add):
                        for p in range(4):
                            mm = nc.tensor.matmul(m.ps[:, 4 * hh + q, p * P:(p + 1) * P], lhsT[:, p, :],
                                                  m.ident if rhs is None else rhs[:, p, :], start=True, stop=True)
                    mm.then_inc(made_sem[hh], 1)

        @block.scalar
        def _(act):
            for r in range(9):
                for hh in range(2):
                    copy, add = rounds(hh)[r]
                    if copy:
                        act.wait_ge(made_sem[hh], r + 1)
                    for q, (lhsT, rhs, dst) in enumerate(copy):
                        nc.scalar.copy(dst, m.ps[:, 4 * hh + q, :].rearrange("p (n e) -> p n e", e=P)).then_inc(copied_sem[hh], 1)

        @block.vector
        def _(dve):
            for hh in range(2):
                nc.vector.tensor_tensor(m.ET[:, hh], m.DT[:, hh], m.ident.unsqueeze(1).to_broadcast([P, 4, P]), ALU.add).then_inc(ready_sem, 1)
            for r in range(9):
                for hh in range(2):
                    copy, add = rounds(hh)[r]
                    if add:
                        dve.wait_ge(made_sem[hh], r + 1)
                        if sum(adds[:r]):
                            dve.wait_ge(added_sem[hh], sum(adds[:r]))
                        else:
                            dve.wait_ge(ready_sem, hh + 1)
                    for q, (lhsT, rhs, addend, dst) in enumerate(add):
                        nc.vector.tensor_tensor(dst, m.ps[:, 4 * hh + len(copy) + q, :].rearrange("p (n e) -> p n e", e=P), addend,
                                                ALU.add).then_inc(added_sem[hh], 1)


def rwkv_chunks(nc, m, d, t, first, last):
    lat = t >= NTC
    chunks = (0, 1) if d == 0 else (1, 0)
    with stage(nc, cleared=1, z_made=1, z_read=1, u_made=1, u_read=1, y_made=1, y_read=1, s_made=1, s_new=1, chain=1) as (
            block, cleared_sem, z_made_sem, z_read_sem, u_made_sem, u_read_sem, y_made_sem, y_read_sem, s_made_sem, s_new_sem, chain_sem):
        @block.tensor
        def _(pe):
            if first:
                pe.wait_ge(cleared_sem, 1)
            for i, c in enumerate(chunks):
                R = slice(CH * c, CH * (c + 1))
                if i:
                    pe.wait_ge(s_new_sem, i)
                    pe.wait_ge(z_read_sem, i)
                for p in range(4):
                    nc.tensor.matmul(m.ps[R, 0, p * P:(p + 1) * P], m.at[:, p, R], m.S[:, p, :], start=True, stop=False)
                    for hh in range(2):
                        h = slice(p * P + hh * HD, p * P + (hh + 1) * HD)
                        mm = nc.tensor.matmul(m.ps[R, 0, h], m.AKT[:, hh, p, R], m.v_rows[:, t, h], start=False, stop=(hh == 1))
                mm.then_inc(z_made_sem, 1)
                pe.wait_ge(z_read_sem, i + 1)
                for p in range(4):
                    for hh in range(2):
                        h = slice(p * P + hh * HD, p * P + (hh + 1) * HD)
                        mm = nc.tensor.matmul(m.ps[R, 1, h], m.D[:, hh, p, R], m.z[:, h], start=True, stop=True)
                mm.then_inc(u_made_sem, 1)
                pe.wait_ge(u_read_sem, i + 1)
                if lat:
                    if i:
                        pe.wait_ge(y_read_sem, i)
                    for p in range(4):
                        nc.tensor.matmul(m.ps[R, 2, p * P:(p + 1) * P], m.rt[:, p, R], m.S[:, p, :], start=True, stop=False)
                        for hh in range(2):
                            h = slice(p * P + hh * HD, p * P + (hh + 1) * HD)
                            nc.tensor.matmul(m.ps[R, 2, h], m.RBT[:, hh, p, R], m.u[:, h], start=False, stop=False)
                            mm = nc.tensor.matmul(m.ps[R, 2, h], m.RKT[:, hh, p, R], m.v_rows[:, t, h], start=False, stop=(hh == 1))
                    mm.then_inc(y_made_sem, 1)
                for p in range(4):
                    w = slice(p * P, (p + 1) * P)
                    nc.tensor.matmul(m.ps[:, 3, w], m.bt_rows[R, w], m.u[R, w], start=True, stop=False)
                    mm = nc.tensor.matmul(m.ps[:, 3, w], m.kt_rows[R, w], m.v_rows[R, t, w], start=False, stop=True)
                mm.then_inc(s_made_sem, 1)

        @block.scalar
        def _(act):
            for i, c in enumerate(chunks):
                R = slice(CH * c, CH * (c + 1))
                act.wait_ge(z_made_sem, i + 1)
                nc.scalar.copy(m.z[R, :], m.ps[R, 0, :]).then_inc(z_read_sem, 1)
                act.wait_ge(u_made_sem, i + 1)
                nc.scalar.copy(m.u[R, :], m.ps[R, 1, :]).then_inc(u_read_sem, 1)

        @block.vector
        def _(dve):
            chain = Chain(dve, chain_sem)
            if first:
                nc.vector.memset(m.S[:, :, :], 0.0).then_inc(cleared_sem, 1)
                dve.wait_ge(cleared_sem, 1)
            for i, c in enumerate(chunks):
                R = slice(CH * c, CH * (c + 1))
                chain(nc.vector.tensor_tensor(m.wmask[:, :, :], m.head_mask.unsqueeze(1).to_broadcast([P, 4, P]), bc(m.wc[:, :, c:c + 1], P), ALU.mult))
                if lat:
                    dve.wait_ge(y_made_sem, i + 1)
                    y = m.y[R, t - NTC, :]
                    if d == 0:
                        nc.vector.tensor_copy(y, m.ps[R, 2, :]).then_inc(y_read_sem, 1)
                    else:
                        nc.vector.tensor_tensor(y, y, m.ps[R, 2, :], ALU.add).then_inc(y_read_sem, 1)
                dve.wait_ge(s_made_sem, i + 1)
                chain(nc.vector.tensor_tensor(m.S[:, :, :], m.S[:, :, :], m.ps[:, 3, :].rearrange("p (n e) -> p n e", e=P), ALU.add))
                nc.vector.tensor_tensor(m.S[:, :, :], m.S[:, :, :], m.wmask[:, :, :], ALU.mult).then_inc(s_new_sem, 1)
                dve.wait_ge(s_new_sem, i + 1)


def rwkv_result(nc, m, a):
    with ExitStack() as ctx:
        b = Memory()
        b.mean, b.ss, b.root, b.rstd, b.sq, b.g2, b.t = buffers(
            nc, ctx, mean=[NTL * RH, 1], ss=[NTL * RH], root=[NTL * RH], rstd=[NTL * RH, 1], sq=[NTL * RH, HD], g2=[512], t=[KB, LAT])
        y = m.y[:].rearrange("p t (h e) -> p (t h) e", e=HD)
        n = NTL * RH
        with stage(nc, landed=1, summed=1, rooted=1, chain=1) as (block, landed_sem, summed_sem, rooted_sem, chain_sem):
            @block.sync
            def _(sp):
                sp.dma_start(b.g2[:, :], a["gate_w2"]).then_inc(landed_sem, 16)
                sp.wait_ge(landed_sem, 16)

            @block.scalar
            def _(act):
                act.wait_ge(summed_sem, 1)
                nc.scalar.activation(b.root[:, :], b.ss[:, :], ACT.Sqrt).then_inc(rooted_sem, 1)

            @block.vector
            def _(dve):
                chain = Chain(dve, chain_sem)
                chain(nc.vector.tensor_reduce(b.mean[:, :, 0], y, AX, ALU.add))
                chain(nc.vector.tensor_scalar(b.mean[:, :, 0], b.mean[:, :, 0], 1.0 / HD, None, ALU.mult))
                chain(nc.vector.tensor_tensor(y, y, bc(b.mean[:, :, :], HD), ALU.subtract))
                chain(nc.vector.tensor_tensor(b.sq[:, :, :], y, y, ALU.mult))
                chain(nc.vector.tensor_reduce(b.ss[:, :], b.sq[:, :, :], AX, ALU.add))
                nc.vector.tensor_scalar(b.ss[:, :], b.ss[:, :], 1.0 / HD, GN_EPS, ALU.mult, ALU.add).then_inc(summed_sem, 1)
                dve.wait_ge(rooted_sem, 1)
                chain(nc.vector.reciprocal(b.rstd[:, :, 0], b.root[:, :]))
                chain(nc.vector.tensor_tensor(y, y, bc(b.rstd[:, :, :], HD), ALU.mult))
        gw, gb = cols(m, "gn_w"), cols(m, "gn_b")
        transposes(nc, m, [([m.y[:, t, h * P:(h + 1) * P]], m.br_rw[:, h:h + 1, t * P:(t + 1) * P], gw[:, h:h + 1], gb[:, h:h + 1])
                           for t in range(NTL) for h in range(KB)])
        with stage(nc, made=1, chain=1) as (block, made_sem, chain_sem):
            @block.tensor
            def _(pe):
                for p in range(KB):
                    nc.tensor.matmul(m.ps[:, p, :], b.g2[:, p * P:(p + 1) * P], m.rw[:, 14, CTX:TOK], start=True, stop=True)
                    nc.tensor.matmul(m.ps[:, 4 + p, :], m.headspread[0:RH, p, :], m.coef[0:RH, :], start=True, stop=True).then_inc(made_sem, 1)

            @block.vector
            def _(dve):
                chain = Chain(dve, chain_sem)
                for p in range(KB):
                    dve.wait_ge(made_sem, p + 1)
                    chain(nc.vector.tensor_tensor(b.t[:, p, :], m.ps[:, 4 + p, :], m.rw[:, 8 + p, CTX:TOK], ALU.mult))
                    chain(nc.vector.tensor_tensor(b.t[:, p, :], b.t[:, p, :], m.br_rw[:, p, :], ALU.add))
                    chain(nc.vector.tensor_tensor(m.br_rw[:, p, :], b.t[:, p, :], m.ps[:, p, :], ALU.mult))



I32 = mybir.dt.int32
U32 = mybir.dt.uint32
SLOTS = 128
TAB = 2 * LAT // SLOTS + N_EXP
FILLS = TAB


def merge(nc, m, a):
    with ExitStack() as ctx:
        (m.gates,) = buffers(nc, ctx, gates=[3, KD, LAT])
        jobs = [(a["w_in"][:, 3968 + c:3968 + c + 512], 512, [("T", x, P, CTX, LAT) for x in range(0, 512, P)]) for c in range(0, 3 * D, 512)]
        products(nc, m, jobs, hT_of(m), lambda out, j, at, chain: nc.scalar.activation(
            m.gates[:, j // 2, 4 * (j % 2) + at[0] // P, :], out, ACT.Sigmoid), "scalar")
        branch = (m.brT[:, 0], m.brT[:, 1], m.br_rw)
        jobs = [(a["w_br"][j // 2][:, (j % 2) * 512:(j % 2 + 1) * 512], 512, [("T", x, P, 0, LAT) for x in range(0, 512, P)]) for j in range(6)]

        def evac(out, j, at, chain):
            tile = 4 * (j % 2) + at[0] // P
            gate, sum_ = m.gates[:, j // 2, tile, :], m.merged[:, tile, :]
            if j < 2:
                return nc.vector.tensor_tensor(sum_, out, gate, ALU.mult)
            chain(nc.vector.tensor_tensor(gate, out, gate, ALU.mult))
            return nc.vector.tensor_tensor(sum_, sum_, gate, ALU.add)

        products(nc, m, jobs, lambda k, t0, tn, j: branch[j // 2][:, k, t0:t0 + tn], evac, "vector", kt=KB)


def project_add(nc, m, w, xT, kt, tiles, wslots=3, width=512):
    jobs = [(w[:, c:c + width], width, [("N", t, width) for t, _, _ in tiles]) for c in range(0, D, width)]
    by_tile = {t: (x, g) for t, x, g in tiles}
    with ExitStack() as ctx:
        b = Memory()
        (b.t,) = buffers(nc, ctx, t=[2, 512])
        turn = [0]

        def evac(out, j, at, chain):
            x, g = by_tile[at[0]]
            c = slice(width * j, width * (j + 1))
            turn[0] ^= 1
            chain(nc.vector.tensor_tensor(b.t[:, turn[0], 0:width], out, g[:, c], ALU.mult))
            return nc.vector.tensor_tensor(x[:, c], x[:, c], b.t[:, turn[0], 0:width], ALU.add)

        products(nc, m, jobs, xT, evac, "vector", kt=kt, wslots=wslots, width=width)


def first_highest(nc, chain, values, top, found, iota, work, hot):
    tiles, n = values.shape[1], values.shape[2]
    chain(nc.vector.tensor_reduce(top, values, AX, ALU.max))
    chain(nc.vector.tensor_tensor(hot, values, bc(top.unsqueeze(2), n), ALU.is_equal))
    chain(nc.vector.scalar_tensor_tensor(work, hot, -float(n), iota, ALU.mult, ALU.add))
    chain(nc.vector.tensor_reduce(found, work, AX, ALU.min))
    chain(nc.vector.tensor_tensor(hot, work, bc(found.unsqueeze(2), n), ALU.is_equal))


def route(nc, m, a):
    T = NTL
    with ExitStack() as ctx:
        b = Memory()
        (b.w, b.iota, b.tri, b.ones, b.tok_id, b.lg, b.le, b.top, b.found, b.work4, b.group, b.e4, b.p,
         b.work, b.hot1, b.hot2, b.m1, b.m2, b.e2, b.den, b.mask, b.where, b.count, b.blocks, b.more, b.end,
         b.one, b.bid, b.cmp, b.exp, b.slot, b.nb) = buffers(
            nc, ctx, w=[KD, N_GRP + N_EXP], iota=[1, N_EXP], tri=[P], ones=[P], tok_id=[T], lg=[T, N_GRP], le=[T, N_EXP], top=[T], found=[T], work4=[T, N_GRP], group=[T, N_GRP], e4=[T, N_GRP], p=[T], work=[T, N_EXP], hot1=[T, N_EXP], hot2=[T, N_EXP], m1=[T], m2=[T], e2=[T], den=[T], mask=[T, N_EXP], where=[T, N_EXP], count=[N_EXP], blocks=[N_EXP], more=[N_EXP], end=[N_EXP], one=[N_EXP], bid=[TAB], cmp=[TAB, N_EXP], exp=[TAB], slot=[2, T], nb=[1])
        tok_i = ctx.enter_context(nc.sbuf_tensor(f"tok_i_{nc.next_id()}", [P, T], U32))
        zero_i = ctx.enter_context(nc.sbuf_tensor(f"zero_i_{nc.next_id()}", [P, TAB + 1], U32))
        with stage(nc, landed=1, logits=1, expd=1, masked=1, ranked=1, table=1, cleared=1, scattered=1, chain=1, zeroed=1) as (
                block, landed_sem, logits_sem, expd_sem, masked_sem, ranked_sem, table_sem, cleared_sem, scattered_sem, chain_sem, zeroed_sem):
            @block.sync
            def _(sp):
                for dst, src in ((b.w[:, :, :], a["w_router"].rearrange("(k p) n -> p k n", p=P)), (b.iota[:, :, :], a["iota32"]),
                                 (b.tri[:, :], a["tri"]), (b.tok_id[:, :], a["tok_id"]), (b.bid[:, :], a["block_id"])):
                    sp.dma_start(dst, src).then_inc(landed_sem, 16)
                sp.wait_ge(zeroed_sem, 1)
                sp.dma_start(m.table_dram.rearrange("(p b) o -> p (b o)", p=P), zero_i[:, :]).then_inc(cleared_sem, 16)
                sp.wait_ge(scattered_sem, 16 * 2 * T)
                with nc.allow_non_contiguous_dma(reason="a small table turned over"):
                    sp.dma_start(m.token_of[:, :], m.table_dram.rearrange("(b p) o -> p (b o)", p=P)).then_inc(cleared_sem, 16)
                sp.wait_ge(cleared_sem, 32)

            @block.tensor
            def _(pe):
                pe.wait_ge(landed_sem, 80)
                for t in range(T):
                    for k in range(KD):
                        mm = nc.tensor.matmul(m.ps[:, 0, t * 64:t * 64 + N_GRP + N_EXP], m.hT[:, k, CTX + t * P:CTX + (t + 1) * P],
                                              b.w[:, k, :], start=(k == 0), stop=(k == KD - 1))
                mm.then_inc(logits_sem, 1)
                pe.wait_ge(masked_sem, 1)
                for t in range(T):
                    out = m.ps[:, 1, t * N_EXP:(t + 1) * N_EXP]
                    for q in range(t):
                        nc.tensor.matmul(out, b.ones[:, :], b.mask[:, q, :], start=(q == 0), stop=False)
                    nc.tensor.matmul(out, b.tri[:, :], b.mask[:, t, :], start=(t == 0), stop=True)
                for q in range(T):
                    mm = nc.tensor.matmul(m.ps[:, 2, 0:N_EXP], b.ones[:, :], b.mask[:, q, :], start=(q == 0), stop=(q == T - 1))
                mm.then_inc(ranked_sem, 1)

            @block.scalar
            def _(act):
                act.wait_ge(table_sem, 1)
                nc.scalar.activation(b.e4[:, :, :], b.e4[:, :, :], ACT.Exp).then_inc(expd_sem, 1)
                act.wait_ge(table_sem, 2)
                nc.scalar.activation(b.e2[:, :], b.e2[:, :], ACT.Exp).then_inc(expd_sem, 1)

            @block.vector
            def _(dve):
                chain = Chain(dve, chain_sem)
                v = nc.vector
                v.memset(zero_i[:, :], 0).then_inc(zeroed_sem, 1)
                chain(v.memset(b.ones[:, :], 1.0))
                chain(v.memset(b.one[:, :], 1.0))
                dve.wait_ge(landed_sem, 80)
                dve.wait_ge(logits_sem, 1)
                L = m.ps[:, 0, 0:T * 64].rearrange("p (t e) -> p t e", e=64)
                chain(v.tensor_copy(b.lg[:, :, :], L[:, :, 0:N_GRP]))
                chain(v.tensor_copy(b.le[:, :, :], L[:, :, N_GRP:N_GRP + N_EXP]))
                first_highest(nc, chain, b.lg[:, :, :], b.top[:, :], b.found[:, :], b.iota[:, :, 0:N_GRP].to_broadcast([P, T, N_GRP]), b.work4[:, :, :], b.group[:, :, :])
                v.tensor_tensor(b.e4[:, :, :], b.lg[:, :, :], bc(b.top[:, :].unsqueeze(2), N_GRP), ALU.subtract).then_inc(table_sem, 1)
                chain(v.tensor_scalar(b.work4[:, :, :], b.group[:, :, :], 1.0, BIG, ALU.subtract, ALU.mult))
                le = b.le[:, :, :].rearrange("p t (g e) -> p t g e", g=N_GRP)
                chain(v.tensor_tensor(le, le, b.work4[:, :, :].unsqueeze(3).to_broadcast([P, T, N_GRP, N_EXP // N_GRP]), ALU.add))
                iota = b.iota[:, :, :].to_broadcast([P, T, N_EXP])
                first_highest(nc, chain, b.le[:, :, :], b.m1[:, :], b.found[:, :], iota, b.work[:, :, :], b.hot1[:, :, :])
                chain(v.scalar_tensor_tensor(b.le[:, :, :], b.hot1[:, :, :], -BIG, b.le[:, :, :], ALU.mult, ALU.add))
                first_highest(nc, chain, b.le[:, :, :], b.m2[:, :], b.found[:, :], iota, b.work[:, :, :], b.hot2[:, :, :])
                chain(v.tensor_tensor(b.mask[:, :, :], b.hot1[:, :, :], b.hot2[:, :, :], ALU.add))
                v.sem_inc(masked_sem, 1)
                v.tensor_tensor(b.e2[:, :], b.m2[:, :], b.m1[:, :], ALU.subtract).then_inc(table_sem, 1)
                dve.wait_ge(expd_sem, 2)
                chain(v.tensor_reduce(b.p[:, :], b.e4[:, :, :], AX, ALU.add))
                chain(v.tensor_scalar(b.den[:, :], b.e2[:, :], 1.0, None, ALU.add))
                chain(v.tensor_tensor(b.den[:, :], b.den[:, :], b.p[:, :], ALU.mult))
                chain(v.reciprocal(m.gate_of[:, 0, :], b.den[:, :]))
                chain(v.tensor_tensor(m.gate_of[:, 1, :], m.gate_of[:, 0, :], b.e2[:, :], ALU.mult))
                dve.wait_ge(ranked_sem, 1)
                chain(v.tensor_copy(b.count[:, :], m.ps[:, 2, 0:N_EXP]))
                chain(v.tensor_scalar(b.blocks[:, :], b.count[:, :], 0.5, None, ALU.is_gt))
                for n in range(SLOTS, LAT, SLOTS):
                    chain(v.tensor_scalar(b.more[:, :], b.count[:, :], n + 0.5, None, ALU.is_gt))
                    chain(v.tensor_tensor(b.blocks[:, :], b.blocks[:, :], b.more[:, :], ALU.add))
                chain(v.tensor_tensor_scan(b.end[:, :], b.one[:, :], b.blocks[:, :], 0.0, ALU.mult, ALU.add))
                chain(v.tensor_scalar(b.nb[:, :], b.end[:, N_EXP - 1:N_EXP], 0.5, 0.25, ALU.mult, ALU.add))
                chain(v.tensor_copy(m.n_pairs[:, :], b.nb[:, :]))
                chain(v.tensor_tensor(b.cmp[:, :, :], b.end[:, :].unsqueeze(1).to_broadcast([P, TAB, N_EXP]), bc(b.bid[:, :].unsqueeze(2), N_EXP), ALU.is_le))
                chain(v.tensor_reduce(b.exp[:, :], b.cmp[:, :, :], AX, ALU.add))
                chain(v.tensor_scalar(b.exp[:, :], b.exp[:, :], float(N_EXP - 1), None, ALU.min))
                chain(v.tensor_copy(m.expert_of[:, :], b.exp[:, :]))
                chain(v.tensor_tensor(b.end[:, :], b.end[:, :], b.blocks[:, :], ALU.subtract))
                chain(v.scalar_tensor_tensor(b.where[:, :, :], b.end[:, :].unsqueeze(1).to_broadcast([P, T, N_EXP]), float(SLOTS),
                                             m.ps[:, 1, 0:T * N_EXP].rearrange("p (t e) -> p t e", e=N_EXP), ALU.mult, ALU.add))
                for j, hot in enumerate((b.hot1, b.hot2)):
                    chain(v.tensor_tensor(b.work[:, :, :], hot[:, :, :], b.where[:, :, :], ALU.mult))
                    chain(v.tensor_reduce(b.slot[:, j, :], b.work[:, :, :], AX, ALU.add))
                    chain(v.tensor_copy(m.place_of[:, j, :], b.slot[:, j, :]))
                v.tensor_copy(tok_i[:, :], b.tok_id[:, :]).then_inc(table_sem, 1)

            @block.gpsimd
            def _(pool):
                pool.wait_ge(table_sem, 3)
                pool.wait_ge(cleared_sem, 16)
                for j in range(2):
                    for t in range(T):
                        nc.gpsimd.indirect_dma_start(m.table_dram, bass.IndirectOffsetOnAxis(ap=m.place_of[:, j, t:t + 1], axis=0),
                                                     tok_i[:, t:t + 1], None).then_inc(scattered_sem, 16)
                pool.wait_ge(scattered_sem, 16 * 2 * T)


def experts(nc, m, a):
    with ExitStack() as ctx:
        b = Memory()
        b.xg0, b.xg1, b.xT, b.wg0, b.wg1, b.wu0, b.wu1, b.wd0, b.wd1, b.sg, b.h, b.hT, b.y0, b.y1 = buffers(
            nc, ctx, xg0=[D], xg1=[D], xT=[KD, P], wg0=[KD, EFF], wg1=[KD, EFF], wu0=[KD, EFF], wu1=[KD, EFF], wd0=[4, D], wd1=[4, D], sg=[EFF], h=[EFF], hT=[4, P], y0=[D], y1=[D])
        xg, wg, wu, wd, y = (b.xg0, b.xg1), (b.wg0, b.wg1), (b.wu0, b.wu1), (b.wd0, b.wd1), (b.y0, b.y1)
        idx = [ctx.enter_context(nc.sbuf_tensor(f"idx{u}_{nc.next_id()}", [P, 1], U32)) for u in range(2)]
        n_pairs_max = TAB // 2
        with stage(nc, x_in=2, g_in=2, u_in=2, d_in=2, idx_new=1, turned=1, x_copied=1, g_made=1, u_made=1, silu=1, h_new=1, h_turned=1,
                   h_copied=1, y_made=1, y_read=1, stored=2, chain=1, credit=1) as (
                block, x_in_sem, g_in_sem, u_in_sem, d_in_sem, idx_new_sem, turned_sem, x_copied_sem, g_made_sem, u_made_sem, silu_sem, h_new_sem, h_turned_sem, h_copied_sem, y_made_sem, y_read_sem, stored_sem, chain_sem, credit_sem):
            def pairs(eng):
                return eng.value_load(m.n_pairs[0:1, 0:1], min_val=1, max_val=n_pairs_max)

            @block.sync
            def _(sp):
                with sp.Fori(0, pairs(sp)) as it:
                    for u in range(2):
                        e = sp.value_load(m.expert_of[0:1, bass.ds(2 * it + u, 1)], min_val=0, max_val=N_EXP - 1)
                        sp.wait_ge(g_made_sem, 2 * it + u + 1)
                        sp.dma_start(wg[u][:, :, :], a["w_exp_gate"][bass.ds(e, 1)].rearrange("o (k p) n -> p (o k) n", p=P)).then_inc(g_in_sem[u], 16)
                        sp.wait_ge(u_made_sem, 2 * it + u + 1)
                        sp.dma_start(wu[u][:, :, :], a["w_exp_up"][bass.ds(e, 1)].rearrange("o (k p) n -> p (o k) n", p=P)).then_inc(u_in_sem[u], 16)
                        sp.wait_ge(y_made_sem, 2 * it + u + 1)
                        sp.dma_start(wd[u][:, :, :], a["w_exp_down"][bass.ds(e, 1)].rearrange("o (k p) n -> p (o k) n", p=P)).then_inc(d_in_sem[u], 16)

            @block.gpsimd
            def _(pool):
                def gather(i, u, count):
                    nc.gpsimd.tensor_copy(idx[u][:, :], m.token_of[:, i]).then_inc(idx_new_sem, 1)
                    pool.wait_ge(idx_new_sem, count)
                    pool.sem_inc(credit_sem, 1)
                    nc.gpsimd.indirect_dma_start(xg[u][:, :], None, m.f_dram, bass.IndirectOffsetOnAxis(ap=idx[u][:, :], axis=0)).then_inc(x_in_sem[u], 16)

                gather(slice(0, 1), 0, 1)
                with pool.Fori(0, pairs(pool)) as it:
                    for u in range(2):
                        i = 2 * it + u
                        pool.wait_ge(turned_sem, i + 1)
                        gather(bass.ds(i + 1, 1), 1 - u, i + 2)

            @block.tensor
            def _(pe):
                pe.sem_inc(g_made_sem, 2)
                pe.sem_inc(u_made_sem, 2)
                pe.sem_inc(y_made_sem, 2)

                def turn(u, landed):
                    pe.wait_ge(x_in_sem[u], landed)
                    for k in range(KD):
                        mm = nc.tensor.transpose(m.ps[:, k // 4, (k % 4) * P:(k % 4 + 1) * P], xg[u][:, k * P:(k + 1) * P], m.ident)
                    mm.then_inc(turned_sem, 1)

                turn(0, 16)
                with pe.Fori(0, pairs(pe)) as it:
                    for u in range(2):
                        i = 2 * it + u
                        pe.wait_ge(x_copied_sem, i + 1)
                        for w, bank, landed, made in ((wg, 2, g_in_sem, g_made_sem), (wu, 3, u_in_sem, u_made_sem)):
                            pe.wait_ge(landed[u], 16 * it + 16)
                            for k in range(KD):
                                mm = nc.tensor.matmul(m.ps[:, bank, :], b.xT[:, k, :], w[u][:, k, :], start=(k == 0), stop=(k == KD - 1))
                            mm.then_inc(made, 1)
                        turn(1 - u, 16 * it + 16 + (16 if u else 0))
                        pe.wait_ge(h_new_sem, i + 1)
                        for k in range(4):
                            mm = nc.tensor.transpose(m.ps[:, 4, k * P:(k + 1) * P], b.h[:, k * P:(k + 1) * P], m.ident)
                        mm.then_inc(h_turned_sem, 1)
                        pe.wait_ge(h_copied_sem, i + 1)
                        pe.wait_ge(d_in_sem[u], 16 * it + 16)
                        pe.wait_ge(y_read_sem, i + 1)
                        for c in range(2):
                            for k in range(4):
                                mm = nc.tensor.matmul(m.ps[:, 5 + c, :], b.hT[:, k, :], wd[u][:, k, c * 512:(c + 1) * 512], start=(k == 0), stop=(k == 3))
                        mm.then_inc(y_made_sem, 1)

            @block.scalar
            def _(act):
                act.sem_inc(stored_sem[0], 16)
                act.sem_inc(stored_sem[1], 16)

                def copy_x(i):
                    act.wait_ge(turned_sem, i + 1)
                    nc.scalar.copy(b.xT[:, :, :].rearrange("p k e -> p (k e)"), m.ps[:, 0:2, :].rearrange("p a b -> p (a b)")).then_inc(x_copied_sem, 1)

                copy_x(0)
                n = pairs(act)
                with act.Fori(0, n) as it:
                    for u in range(2):
                        i = 2 * it + u
                        act.wait_ge(g_made_sem, i + 3)
                        nc.scalar.activation(b.sg[:, :], m.ps[:, 2, :], ACT.Silu).then_inc(silu_sem, 1)
                        copy_x(i + 1)
                        act.wait_ge(h_turned_sem, i + 1)
                        nc.scalar.copy(b.hT[:, :, :].rearrange("p k e -> p (k e)"), m.ps[:, 4, :]).then_inc(h_copied_sem, 1)
                        act.wait_ge(y_read_sem, i + 2)
                        act.dma_start(m.y_dram[bass.ds(i * SLOTS, SLOTS), :], y[u][:, :]).then_inc(stored_sem[u], 16)
                for u in range(2):
                    act.wait_ge(stored_sem[u], 16 * n + 16)
                    act.sem_inc(credit_sem, 1)

            @block.vector
            def _(dve):
                dve.sem_inc(y_read_sem, 1)
                with dve.Fori(0, pairs(dve)) as it:
                    for u in range(2):
                        i = 2 * it + u
                        dve.wait_ge(silu_sem, i + 1)
                        dve.wait_ge(u_made_sem, i + 3)
                        nc.vector.tensor_tensor(b.h[:, :], b.sg[:, :], m.ps[:, 3, :], ALU.mult).then_inc(h_new_sem, 1)
                        dve.wait_ge(y_made_sem, i + 3)
                        dve.wait_ge(stored_sem[u], 16 * it + 16)
                        nc.vector.tensor_copy(y[u][:, :], m.ps[:, 5:7, :].rearrange("p a b -> p (a b)")).then_inc(y_read_sem, 1)


def combine(nc, m):
    with ExitStack() as ctx:
        b = Memory()
        b.r0, b.r1 = buffers(nc, ctx, r0=[NTL, D], r1=[NTL, D])
        rows = (b.r0, b.r1)
        with stage(nc, landed=8, chain=1) as (block, landed_sem, chain_sem):
            @block.gpsimd
            def _(pool):
                for t in range(NTL):
                    for j in range(2):
                        nc.gpsimd.indirect_dma_start(rows[j][:, t, :], None, m.y_dram, bass.IndirectOffsetOnAxis(ap=m.place_of[:, j, t:t + 1], axis=0)
                                                     ).then_inc(landed_sem[2 * t + j], 16)

            @block.vector
            def _(dve):
                chain = Chain(dve, chain_sem)
                for t in range(NTL):
                    dve.wait_ge(landed_sem[2 * t], 16)
                    chain(nc.vector.tensor_scalar(rows[0][:, t, :], rows[0][:, t, :], m.gate_of[:, 0, t:t + 1], None, ALU.mult))
                    dve.wait_ge(landed_sem[2 * t + 1], 16)
                    chain(nc.vector.scalar_tensor_tensor(rows[0][:, t, :], rows[1][:, t, :], m.gate_of[:, 1, t:t + 1], rows[0][:, t, :], ALU.mult, ALU.add))
                    chain(nc.vector.tensor_tensor(rows[0][:, t, :], rows[0][:, t, :], m.gate_rows[:, 1, 0, :], ALU.mult))
                    chain(nc.vector.tensor_tensor(m.x[:, t, :], m.x[:, t, :], rows[0][:, t, :], ALU.add))


def fill_rows(nc, m, zeros):
    view = m.y_dram.rearrange("(f p) (h n) -> f p h n", p=P, h=2)
    for f in range(FILLS):
        nc.sync.dma_start(view[f], zeros.unsqueeze(1).to_broadcast([P, 2, 512])).then_inc(m.filled, 16)


def expert_layer(nc, m, a):
    with ExitStack() as ctx:
        def ints(name, shape, dt):
            return ctx.enter_context(nc.sbuf_tensor(f"{name}_{nc.next_id()}", [P, *shape], dt))
        m.place_of = ints("place_of", [2, NTL], U32)
        m.token_of = ints("token_of", [TAB + 1], U32)
        m.expert_of = ints("expert_of", [TAB], I32)
        m.n_pairs = ints("n_pairs", [1], I32)
        (m.gate_of,) = buffers(nc, ctx, gate_of=[2, NTL])
        m.f_dram = nc.dram_tensor("expert_inputs", [LAT, D], F32).ap()
        m.table_dram = nc.dram_tensor("token_table", [(TAB + 1) * SLOTS, 1], U32).ap()
        rows_back(nc, m)
        route(nc, m, a)
        experts(nc, m, a)
        combine(nc, m)


def rows_back(nc, m):
    with ExitStack() as ctx:
        b = Memory()
        (b.f,) = buffers(nc, ctx, f=[2, D])
        with stage(nc, turned=1, read=1, stored=2) as (block, turned_sem, read_sem, stored_sem):
            @block.tensor
            def _(pe):
                for t in range(NTL):
                    if t >= 2:
                        pe.wait_ge(read_sem, t - 1)
                    for k in range(KD):
                        mm = nc.tensor.transpose(m.ps[:, 2 * (t % 2) + k // 4, (k % 4) * P:(k % 4 + 1) * P], m.hT[:, k, CTX + t * P:CTX + (t + 1) * P], m.ident)
                    mm.then_inc(turned_sem, 1)

            @block.vector
            def _(dve):
                for t in range(NTL):
                    dve.wait_ge(turned_sem, t + 1)
                    if t >= 2:
                        dve.wait_ge(stored_sem[t % 2], 16 * (t // 2))
                    nc.vector.tensor_copy(b.f[:, t % 2, :], m.ps[:, 2 * (t % 2):2 * (t % 2) + 2, :].rearrange("p a b -> p (a b)")).then_inc(read_sem, 1)

            @block.sync
            def _(sp):
                for t in range(NTL):
                    sp.wait_ge(read_sem, t + 1)
                    sp.dma_start(m.f_dram[t * P:(t + 1) * P, :], b.f[:, t % 2, :]).then_inc(stored_sem[t % 2], 16)
                for u in range(2):
                    sp.wait_ge(stored_sem[u], 16 * NTL // 2)



TWO_PI_HI = 6.28125
TWO_PI_LO = float(2 * np.pi - TWO_PI_HI)
ROUND = 1.5 * 2.0 ** 23
QSCALE = float(P) ** -0.5


def key_runs(d, t):
    if d == 0:
        return [(0, t + 1)]
    if t < NTC:
        return [(t, NTC)]
    return [(0, NT)] if t == NTC else [(0, NTC), (t, NT)]


def second_block(nc, m, a):
    m.xc = m.keep.enter_context(nc.sbuf_tensor("ctx_rows", [P, NTC, D], F32, side="right"))
    load(nc, [(m.xc, a["ctx_2"].rearrange("(t p) d -> p t d", p=P))])
    lat = [(t, m.x[:, t, :]) for t in range(NTL)]
    for layer in range(2):
        with ExitStack() as ctx:
            n = 2 - layer
            m.mod, m.gate_rows = buffers(nc, ctx, mod=[48, 2], gate_rows=[2, n, D])
            modulation(nc, m, a[f"ada_w_{layer}"], (cols(m, "c_2"), cols(m, "c_ctx_2")), cols(m, f"ada_b_{layer}"), n, a[f"ada_b_{layer}_row"],
                       m.mod, m.gate_rows)
            mods = lambda chunk, j: m.mod[:, 8 * chunk:8 * chunk + 8, j]
            both = [(m.xc[:, t, :], t * P, "ctx") for t in range(NTC)] + [(x, CTX + t * P, "lat") for t, x in lat]

            def adds(g, with_ctx):
                c = [(t, m.xc[:, t, :], m.gate_rows[:, g, 1, :]) for t in range(NTC)] if with_ctx else []
                return c + [(NTC + t, x, m.gate_rows[:, g, 0, :]) for t, x in lat]

            with ExitStack() as c1:
                (m.hT,) = buffers(nc, c1, hT=[KD, TOK])
                g = cols(m, f"norm_mix_{layer}")
                normed(nc, m, both, m.hT, {"ctx": (g, mods(1, 1), mods(0, 1)), "lat": (g, mods(1, 0), mods(0, 0))})
                if layer == 0:
                    (m.mixT,) = buffers(nc, c1, mixT=[KD, TOK])
                    hyena(nc, m, a)
                    mlstm(nc, m, a)
                    project_add(nc, m, a["w_out_0"], lambda k, t0, tn, j: m.mixT[:, k, t0:t0 + tn], KD, adds(0, True))
                else:
                    (m.oT,) = buffers(nc, c1, oT=[KD, LAT])
                    latent_attention(nc, m, a)
                    project_add(nc, m, a["mla_w_o"], lambda k, t0, tn, j: m.oT[:, k, t0 - CTX:t0 - CTX + tn], KD, adds(0, False))
            with ExitStack() as c1:
                (m.fT,) = buffers(nc, c1, fT=[KF, TOK])
                g = cols(m, f"norm_ffn_{layer}")
                kinds = {"ctx": (g, mods(4, 1), mods(3, 1)), "lat": (g, mods(4, 0), mods(3, 0))}
                if layer:
                    both, kinds = both[NTC:], {"lat": kinds["lat"]}
                with ExitStack() as c2:
                    (m.hT,) = buffers(nc, c2, hT=[KD, TOK])
                    normed(nc, m, both, m.hT, kinds)
                    ffn_up(nc, m, a, layer, (1,) if layer else (0, 1))
                project_add(nc, m, a[f"ffn_down_{layer}"], lambda k, t0, tn, j: m.fT[:, k, t0:t0 + tn], KF, adds(1, layer == 0), width=256)
    with ExitStack() as ctx:
        (m.final_gain,) = buffers(nc, ctx, final_gain=[D])
        load(nc, [(m.final_gain, a["rows"][:, 6 * HD:6 * HD + D].to_broadcast([P, D]))])
        head_norms(nc, m, [(m.x[:, :, :], m.final_gain[:, :])], D, EPS)
    with stage(nc, stored=1) as (block, stored_sem):
        @block.sync
        def _(sp):
            sp.dma_start(a["out"][0].rearrange("(t p) d -> p t d", p=P), m.x[:]).then_inc(stored_sem, 16)
            sp.wait_ge(stored_sem, 16)


def tapped(nc, m, w, c0, tiles, cw, cb, ncw, dst):
    with ExitStack() as ctx:
        (m.pad,) = buffers(nc, ctx, pad=[2, PAD])
        pad_zeros(nc, m, [m.pad[:, 0, :], m.pad[:, 1, :]])
        jobs = [(w[:, c0 + c:c0 + c + 512], 512, [("T", x, P, SEGS[s][0], SEGS[s][2]) for x in range(0, 512, P) for s in range(2)])
                for c in range(0, tiles * P, 512)]

        def evac(out, j, at, chain):
            tile, seg = 4 * j + at[0] // P, int(at[2] > 0)
            t0, p0, tn = SEGS[seg]
            pad = m.pad[:, tile % 2, :]
            chain(nc.vector.tensor_copy(pad[:, p0:p0 + tn], out))
            return taps(nc.vector, chain, pad, seg, [cw[:, q * ncw + tile:q * ncw + tile + 1] for q in range(3)],
                        None if cb is None else cb[:, tile:tile + 1], dst[:, tile, t0:t0 + tn])

        products(nc, m, jobs, hT_of(m), evac, "vector", wslots=2)


def sines(nc, chain, reduced_sem, x, k):
    v = nc.vector
    chain(v.tensor_scalar(k, x, float(1 / (2 * np.pi)), ROUND, ALU.mult, ALU.add))
    chain(v.tensor_scalar(k, k, ROUND, None, ALU.subtract))
    chain(v.scalar_tensor_tensor(x, k, -TWO_PI_HI, x, ALU.mult, ALU.add))
    chain(v.scalar_tensor_tensor(x, k, -TWO_PI_LO, x, ALU.mult, ALU.add))
    v.tensor_scalar(x, x, float(np.float32(3.1415925)), -float(np.float32(3.1415925)), ALU.min, ALU.max).then_inc(reduced_sem, 1)


def hyena(nc, m, a):
    with ExitStack() as ctx:
        (m.hy,) = buffers(nc, ctx, hy=[12, TOK])
        tapped(nc, m, a["w_in_0"], 0, 12, cols(m, "hy_conv_w"), cols(m, "hy_conv_b"), 12, m.hy)
        with stage(nc, chain=1) as (block, chain_sem):
            @block.vector
            def _(dve):
                Chain(dve, chain_sem)(nc.vector.tensor_tensor(m.hy[:, 4:8, :], m.hy[:, 4:8, :], m.hy[:, 8:12, :], ALU.mult))
        for seg in range(2):
            t0, _, L = SEGS[seg]
            n = L // P
            with ExitStack() as c1:
                b = Memory()
                b.Kc, b.Ks, b.Kr, b.Ki = buffers(nc, c1, Kc=[n, 512], Ks=[n, 512], Kr=[n, 512], Ki=[n, 512])
                b.g = m.hy[:, 8:12, :].rearrange("p a b -> p (a b)")[:, 0:n * 512].rearrange("p (n e) -> p n e", e=512)
                with ExitStack() as c2:
                    b.z, b.w1, b.w2, b.w3, b.h1, b.h2, b.turns, b.decay = buffers(
                        nc, c2, z=[L], w1=[HD], w2=[HD], w3=[2 * 512], h1=[L], h2=[L], turns=[L], decay=[2, 1024])
                    fb1, fb2, fq = cols(m, "hy_fb1"), cols(m, "hy_fb2"), cols(m, "hy_freq")
                    R = slice(0, HD)
                    with stage(nc, landed=1, decays=2, made=1, reduced=1, sined=1, read=1, chain=1) as (
                            block, landed_sem, decays_sem, made_sem, reduced_sem, sined_sem, read_sem, chain_sem):
                        @block.sync
                        def _(sp):
                            for dst, src in ((b.z[0:33, :], a[f"hy_z_{L}"]), (b.w1[0:33, :], a["hy_fw1"]), (b.w2[R, :], a["hy_fw2"]), (b.w3[R, :], a["hy_fw3"])):
                                sp.dma_start(dst, src).then_inc(landed_sem, 16)
                            for t in range(n):
                                if t >= 2:
                                    sp.wait_ge(read_sem, 2 * (t - 1))
                                sp.dma_start(b.decay[:, t % 2, :], a[f"hy_decay_{L}"][t * P:(t + 1) * P, :]).then_inc(decays_sem[t % 2], 16)

                        @block.tensor
                        def _(pe):
                            pe.wait_ge(landed_sem, 64)
                            nc.tensor.matmul(m.ps[R, 0, 0:L], b.w1[0:33, :], b.z[0:33, :], start=True, stop=True).then_inc(made_sem, 1)
                            pe.wait_ge(sined_sem, 1)
                            nc.tensor.matmul(m.ps[R, 1, 0:L], b.w2[R, :], b.h1[R, :], start=True, stop=True).then_inc(made_sem, 1)
                            pe.wait_ge(sined_sem, 2)
                            for t in range(n):
                                if t >= 2:
                                    pe.wait_ge(read_sem, 2 * (t - 1))
                                for c in range(2):
                                    mm = nc.tensor.matmul(m.ps[:, 2 + 2 * (t % 2) + c, :], b.h2[R, t * P:(t + 1) * P], b.w3[R, c * 512:(c + 1) * 512], start=True, stop=True)
                                mm.then_inc(made_sem, 1)

                        @block.scalar
                        def _(act):
                            for i, h in enumerate((b.h1, b.h2)):
                                act.wait_ge(reduced_sem, i + 1)
                                nc.scalar.activation(h[R, :], h[R, :], ACT.Sin).then_inc(sined_sem, 1)

                        @block.vector
                        def _(dve):
                            chain = Chain(dve, chain_sem)
                            for i, (h, fb) in enumerate(((b.h1, fb1), (b.h2, fb2))):
                                dve.wait_ge(made_sem, i + 1)
                                chain(nc.vector.tensor_scalar(h[R, :], m.ps[R, i, 0:L], fb[R, :], fq[R, :], ALU.add, ALU.mult))
                                if i:
                                    dve.wait_ge(sined_sem, 1)
                                sines(nc, chain, reduced_sem, h[R, :], b.turns[R, :])
                            for t in range(n):
                                dve.wait_ge(made_sem, 3 + t)
                                dve.wait_ge(decays_sem[t % 2], 16 * (t // 2 + 1))
                                dec = b.decay[:, t % 2, :]
                                chain(nc.vector.tensor_tensor(b.Kr[:, t, :], m.ps[:, 2 + 2 * (t % 2), :], dec[:, 0:512], ALU.mult))
                                chain(nc.vector.tensor_tensor(b.Ki[:, t, :], m.ps[:, 3 + 2 * (t % 2), :], dec[:, 512:1024], ALU.mult))
                                nc.vector.tensor_tensor(b.Kc[:, t, :], b.Kr[:, t, :], b.Ki[:, t, :], ALU.add).then_inc(read_sem, 1)
                                nc.vector.tensor_tensor(b.Ks[:, t, :], b.Ki[:, t, :], b.Kr[:, t, :], ALU.subtract).then_inc(read_sem, 1)
                transposes(nc, m, [([m.hy[:, 4 + p, t0 + t * P:t0 + (t + 1) * P] for p in range(4)], b.g[:, t, :].rearrange("p (n e) -> p n e", e=P), None, None)
                                   for t in range(n)])
                b.C, b.S, b.Gr, b.Gs = buffers(nc, c1, C=[n, L], S=[n, L], Gr=[n, 512], Gs=[n, 512])
                specs = [(b.C, b.Kc, b.Kr), (b.S, b.Ks, b.Ki), (b.C, b.g, b.Gr), (b.S, b.g, b.Gs)]
                with stage(nc, landed=4, made=1, read=1, mixed=1, out=1, chain=1) as (
                        block, landed_sem, made_sem, read_sem, mixed_sem, out_sem, chain_sem):
                    @block.sync
                    def _(sp):
                        for i, (dst, name) in enumerate(((b.C, "dft_c"), (b.S, "dft_s"), (b.C, "idft_c"), (b.S, "idft_s"))):
                            if i >= 2:
                                sp.wait_ge(made_sem, (i + 1) * n)
                            sp.dma_start(dst[:], a[f"{name}_{L}"].rearrange("(k p) f -> p k f", p=P)).then_inc(landed_sem[i], 16)
                        for i in range(4):
                            sp.wait_ge(landed_sem[i], 16)

                    @block.tensor
                    def _(pe):
                        r = 0
                        for i, (table, x, dst) in enumerate(specs):
                            pe.wait_ge(landed_sem[i % 2], 16)
                            for f in range(n):
                                if r >= 4:
                                    pe.wait_ge(read_sem, r - 3)
                                for k in range(n):
                                    mm = nc.tensor.matmul(m.ps[:, r % 4, :], table[:, k, f * P:(f + 1) * P], x[:, k, :], start=(k == 0), stop=(k == n - 1))
                                mm.then_inc(made_sem, 1)
                                r += 1
                        pe.wait_ge(landed_sem[2], 16)
                        pe.wait_ge(landed_sem[3], 16)
                        pe.wait_ge(mixed_sem, 1)
                        for p in range(4):
                            for j, (spec, table) in enumerate(((b.Kc, b.C), (b.Ks, b.S))):
                                for f in range(n):
                                    mm = nc.tensor.matmul(m.ps[:, 4 + p, 0:L], spec[:, f, p * P:(p + 1) * P], table[:, f, :], start=(j == 0 and f == 0), stop=(j == 1 and f == n - 1))
                            mm.then_inc(out_sem, 1)

                    @block.scalar
                    def _(act):
                        r = 0
                        for i, (table, x, dst) in enumerate(specs):
                            for f in range(n):
                                act.wait_ge(made_sem, r + 1)
                                nc.scalar.copy(dst[:, f, :], m.ps[:, r % 4, :]).then_inc(read_sem, 1)
                                r += 1

                    @block.vector
                    def _(dve):
                        chain = Chain(dve, chain_sem)
                        v = nc.vector
                        dve.wait_ge(read_sem, 4 * n)
                        x = lambda t: t[:, :, :]
                        chain(v.tensor_tensor(x(b.Kc), x(b.Gr), x(b.Kr), ALU.mult))
                        chain(v.tensor_tensor(x(b.Ks), x(b.Gr), x(b.Ki), ALU.mult))
                        chain(v.tensor_tensor(x(b.Ki), x(b.Gs), x(b.Ki), ALU.mult))
                        chain(v.tensor_tensor(x(b.Kr), x(b.Gs), x(b.Kr), ALU.mult))
                        chain(v.tensor_tensor(x(b.Kc), x(b.Kc), x(b.Ki), ALU.add))
                        v.tensor_tensor(x(b.Ks), x(b.Ks), x(b.Kr), ALU.subtract).then_inc(mixed_sem, 1)
                        for p in range(4):
                            dve.wait_ge(out_sem, p + 1)
                            T = slice(t0, t0 + L)
                            chain(v.scalar_tensor_tensor(m.mixT[:, p, T], m.hy[:, 4 + p, T], cols(m, "hy_bias")[:, p:p + 1], m.ps[:, 4 + p, 0:L], ALU.mult, ALU.add))
                            chain(v.tensor_tensor(m.mixT[:, p, T], m.mixT[:, p, T], m.hy[:, p, T], ALU.mult))


def mlstm(nc, m, a):
    with ExitStack() as ctx:
        m.qkT, m.v, m.og, m.gi, m.gf = buffers(nc, ctx, qkT=[8, TOK], v=[NT, 512], og=[4, TOK], gi=[TOK], gf=[TOK])
        tapped(nc, m, a["w_in_0"], 1536, 8, cols(m, "ml_conv_w"), None, 8, m.qkT)
        w = a["w_in_0"]
        jobs = [(w[:, 2560:3072], 512, [("N", t, 512) for t in range(NT)]),
                (w[:, 3072:3584], 512, [("T", x, P, SEGS[s][0], SEGS[s][2]) for x in range(0, 512, P) for s in range(2)]),
                (w[:, 3584:3600], 16, [("T", x, 8, SEGS[s][0], SEGS[s][2]) for x in (0, 8) for s in range(2)])]

        def evac(out, j, at, chain):
            if j == 0:
                return nc.scalar.copy(m.v[:, at[0], :], out)
            T = slice(at[2], at[2] + at[3])
            if j == 1:
                return nc.scalar.activation(m.og[:, at[0] // P, T], out, ACT.Sigmoid)
            dst, bias = (m.gf, "gate_f") if at[0] else (m.gi, "gate_i")
            return nc.scalar.activation(dst[0:8, T], out, ACT.Identity, bias=cols(m, bias)[0:8, :])

        products(nc, m, jobs, hT_of(m), evac, "scalar", wslots=2)
        m.h, m.F, m.r, m.Fcol = buffers(nc, ctx, h=[NT, 512], F=[2, TOK], r=[2, TOK], Fcol=[NT, 2, 8])
        with ExitStack() as c1:
            b = Memory()
            b.e, b.one = buffers(nc, c1, e=[TOK], one=[TOK])
            R = slice(0, 8)
            with stage(nc, expd=1, bent=1, rows=1, turned=1, chain=1) as (block, expd_sem, bent_sem, rows_sem, turned_sem, chain_sem):
                @block.scalar
                def _(act):
                    act.wait_ge(bent_sem, 1)
                    nc.scalar.activation(b.e[R, :], b.e[R, :], ACT.Exp).then_inc(expd_sem, 1)
                    act.wait_ge(bent_sem, 2)
                    nc.scalar.activation(b.e[R, :], b.e[R, :], ACT.Ln).then_inc(expd_sem, 1)
                    for n in (0, 1):
                        nc.scalar.activation(m.qkT[:, 4 * n:4 * n + 4, :], m.qkT[:, 4 * n:4 * n + 4, :], ACT.Silu)

                @block.vector
                def _(dve):
                    chain = Chain(dve, chain_sem)
                    v = nc.vector
                    chain(v.memset(b.one[R, :], 1.0))
                    chain(v.tensor_scalar(b.e[R, :], m.gf[R, :], -1.0, None, ALU.mult))
                    v.tensor_tensor(b.e[R, :], b.e[R, :], m.gf[R, :], ALU.min).then_inc(bent_sem, 1)
                    dve.wait_ge(expd_sem, 1)
                    v.tensor_scalar(b.e[R, :], b.e[R, :], 1.0, None, ALU.add).then_inc(bent_sem, 1)
                    dve.wait_ge(expd_sem, 2)
                    chain(v.tensor_scalar(m.gf[R, :], m.gf[R, :], 0.0, None, ALU.min))
                    chain(v.tensor_tensor(m.gf[R, :], m.gf[R, :], b.e[R, :], ALU.subtract))
                    chain(v.tensor_tensor_scan(m.F[R, 0, :], b.one[R, :], m.gf[R, :], 0.0, ALU.mult, ALU.add))
                    back = lambda x, lo, hi: x[R, hi - 1:(lo - 1 if lo else None):-1]
                    chain(v.tensor_tensor_scan(back(m.F[:, 1, :], 0, CTX), back(b.one, 0, CTX), back(m.gf, 0, CTX), 0.0, ALU.mult, ALU.add))
                    chain(v.tensor_tensor_scan(back(m.F[:, 1, :], CTX, TOK), back(b.one, CTX, TOK), back(m.gf, CTX, TOK), m.F[R, 1, 0:1], ALU.mult, ALU.add))
                    for d in range(2):
                        v.tensor_tensor(m.r[R, d, :], m.gi[R, :], m.F[R, d, :], ALU.subtract).then_inc(rows_sem, 1)
                    dve.wait_ge(turned_sem, 1)
                    chain(v.tensor_copy(m.Fcol[:, :, :, :].rearrange("p t d h -> p (t d h)"), m.ps[:, 0, 0:NT * 16]))

                @block.tensor
                def _(pe):
                    pe.wait_ge(rows_sem, 2)
                    for t in range(NT):
                        for d in range(2):
                            o = (t * 2 + d) * 8
                            mm = nc.tensor.transpose(m.ps[:, 0, o:o + 8], m.F[R, d, t * P:(t + 1) * P], m.ident[R, R])
                    mm.then_inc(turned_sem, 1)
        mlstm_heads(nc, m, a)
        head_norms(nc, m, [(m.h[:].rearrange("p t (h e) -> p (t h) e", e=P), None)], P, EPS)
        g = cols(m, "ml_norm_g")
        transposes(nc, m, [([m.h[:, t, h * P:(h + 1) * P]], m.mixT[:, 4 + h:5 + h, t * P:(t + 1) * P], g[:, h:h + 1], None) for t in range(NT) for h in range(4)])
        with stage(nc, chain=1) as (block, chain_sem):
            @block.vector
            def _(dve):
                Chain(dve, chain_sem)(nc.vector.tensor_tensor(m.mixT[:, 4:8, :], m.mixT[:, 4:8, :], m.og[:, :, :], ALU.mult))


def mlstm_heads(nc, m, a):
    with ExitStack() as ctx:
        b = Memory()
        b.pick, b.causal, b.seen, b.dm, b.tm, b.seen_max, b.mu, b.neg_mu, b.em, b.den, b.dn, b.rec, b.wT = buffers(
            nc, ctx, pick=[8, P], causal=[2, P], seen=[2, NT, NT], dm=[2, NT], tm=[2, NT], seen_max=[2, NT, NT], mu=[2, NT], neg_mu=[2, NT], em=[2, NT], den=[2, 2], dn=[2], rec=[2], wT=[2, NT, P])
        b.rb, b.dg, b.e, b.w = [m.hT[:, 2 * i:2 * i + 2, :].rearrange("p d (t e) -> p d t e", e=P) for i in range(4)]
        with stage(nc, landed=1, spread=1, copied=1, mu=1, bounded=1, scored=1, expd=1, weighed=1, turned=1, wt=1, valued=1, stored=1, chain=1) as (
                block, landed_sem, spread_sem, copied_sem, mu_sem, bounded_sem, scored_sem, expd_sem, weighed_sem, turned_sem, wt_sem, valued_sem, stored_sem, chain_sem):
            units = [(h, t) for h in range(HEADS) for t in range(NT)]

            def flat(bank):
                return m.ps[:, bank:bank + 2, :].rearrange("p a b -> p (a b)")[:, 0:TOK]

            @block.sync
            def _(sp):
                sp.dma_start(b.pick[0:8, :, :], a["pick"]).then_inc(landed_sem, 16)
                sp.dma_start(b.causal[:, :, :], a["causal"]).then_inc(landed_sem, 16)
                sp.dma_start(b.seen[:, :, :, :], a["seen"]).then_inc(landed_sem, 16)
                sp.wait_ge(landed_sem, 48)

            @block.tensor
            def _(pe):
                def rows(h):
                    for d in range(2):
                        for c, w in ((0, 512), (512, 256)):
                            mm = nc.tensor.matmul(m.ps[:, 4 + 2 * d + c // 512, 0:w], b.pick[0:8, 4 * d + h, :], m.r[0:8, d, c:c + w], start=True, stop=True)
                    mm.then_inc(spread_sem, 1)

                pe.wait_ge(landed_sem, 48)
                for i, (h, t) in enumerate(units):
                    if t == 0:
                        if i:
                            pe.wait_ge(stored_sem, 2 * i)
                        rows(h)
                    if i:
                        pe.wait_ge(weighed_sem, 2 * i)
                    n = NTC if t < NTC else NT
                    for c, w in ((0, min(n, 4)), (4, n - 4)):
                        if w > 0:
                            mm = nc.tensor.matmul(m.ps[:, c // 4, 0:w * P], m.qkT[:, h, t * P:(t + 1) * P], m.qkT[:, 4 + h, c * P:(c + w) * P], start=True, stop=True)
                    mm.then_inc(scored_sem, 1)
                    if t == 0:
                        pe.wait_ge(copied_sem, 2 * (h + 1))
                    for d in range(2):
                        pe.wait_ge(weighed_sem, 2 * i + d + 1)
                        if i or d:
                            pe.wait_ge(wt_sem, 2 * i + d)
                        for lo, hi in key_runs(d, t):
                            for k in range(lo, hi):
                                mm = nc.tensor.transpose(m.ps[:, 2 + k // 4, (k % 4) * P:(k % 4 + 1) * P], b.w[:, d, k, :], m.ident)
                        mm.then_inc(turned_sem, 1)
                        pe.wait_ge(wt_sem, 2 * i + d + 1)
                        if i:
                            pe.wait_ge(stored_sem, 2 * i - 1 + d)
                        keys = [k for lo, hi in key_runs(d, t) for k in range(lo, hi)]
                        for k in keys:
                            mm = nc.tensor.matmul(m.ps[:, 4 + d, 0:P], b.wT[:, d, k, :], m.v[:, k, h * P:(h + 1) * P], start=(k == keys[0]), stop=(k == keys[-1]))
                        mm.then_inc(valued_sem, 1)

            @block.scalar
            def _(act):
                for i, (h, t) in enumerate(units):
                    if t == 0:
                        act.wait_ge(spread_sem, h + 1)
                        if i:
                            act.wait_ge(weighed_sem, 2 * i)
                        for d in range(2):
                            nc.scalar.copy(b.rb[:, d, :, :].rearrange("p t e -> p (t e)"), flat(4 + 2 * d)).then_inc(copied_sem, 1)
                        act.wait_ge(mu_sem, h + 1)
                        nc.scalar.activation(b.em[:, :, :], b.em[:, :, :], ACT.Exp, scale=-1.0).then_inc(bounded_sem, 1)
                    for d in range(2):
                        if i:
                            act.wait_ge(weighed_sem, 2 * i - 1 + d)
                        nm = b.neg_mu[:, d, t:t + 1]
                        for lo, hi in key_runs(d, t):
                            for x0, x1 in ((lo, min(hi, t)), (max(lo, t + 1), hi)):
                                if x1 > x0:
                                    nc.scalar.activation(b.e[:, d, x0:x1, :], b.rb[:, d, x0:x1, :], ACT.Exp, bias=nm)
                        nc.scalar.activation(b.e[:, d, t, :], b.dg[:, d, t, :], ACT.Exp, bias=nm).then_inc(expd_sem, 1)
                    for d in range(2):
                        act.wait_ge(turned_sem, 2 * i + d + 1)
                        if i:
                            act.wait_ge(valued_sem, 2 * i - 1 + d)
                        runs = key_runs(d, t)
                        for j, (lo, hi) in enumerate(runs):
                            src = m.ps[:, 2:4, :].rearrange("p a (b e) -> p (a b) e", e=P)[:, lo:hi, :]
                            last = nc.scalar.copy(b.wT[:, d, lo:hi, :], src)
                        last.then_inc(wt_sem, 1)

            @block.vector
            def _(dve):
                chain = Chain(dve, chain_sem)
                v = nc.vector
                dve.wait_ge(landed_sem, 48)
                for i, (h, t) in enumerate(units):
                    if t == 0:
                        dve.wait_ge(copied_sem, 2 * (h + 1))
                        for d in range(2):
                            chain(v.tensor_tensor(b.dg[:, d, :, :], b.rb[:, d, :, :], b.causal[:, d, :].unsqueeze(1).to_broadcast([P, NT, P]), ALU.add))
                        chain(v.tensor_reduce(b.dm[:, :, :], b.dg[:, :, :, :], AX, ALU.max))
                        chain(v.tensor_reduce(b.tm[:, :, :], b.rb[:, :, :, :], AX, ALU.max))
                        for d in range(2):
                            chain(v.tensor_tensor(b.seen_max[:, d, :, :], b.seen[:, d, :, :], b.tm[:, d, :].unsqueeze(1).to_broadcast([P, NT, NT]), ALU.add))
                        chain(v.tensor_reduce(b.mu[:, :, :], b.seen_max[:, :, :, :], AX, ALU.max))
                        chain(v.scalar_tensor_tensor(b.mu[:, :, :], b.mu[:, :, :], 0.0, b.dm[:, :, :], ALU.max, ALU.max))
                        chain(v.tensor_scalar(b.neg_mu[:, :, :], b.mu[:, :, :], -1.0, None, ALU.mult))
                        for d in range(2):
                            last = v.tensor_tensor(b.em[:, d, :], b.mu[:, d, :], m.Fcol[:, :, d, 4 * d + h], ALU.add)
                            if d == 0:
                                chain(last)
                        last.then_inc(mu_sem, 1)
                        dve.wait_ge(bounded_sem, h + 1)
                    dve.wait_ge(scored_sem, i + 1)
                    for d in range(2):
                        dve.wait_ge(expd_sem, 2 * i + d + 1)
                        if i:
                            dve.wait_ge(turned_sem, 2 * i - 1 + d)
                        runs = key_runs(d, t)
                        if len(runs) == 1:
                            chain(v.memset(b.den[:, d, 1:2], 0.0))
                        for j, (lo, hi) in enumerate(runs):
                            last = v.scalar_tensor_tensor(b.w[:, d, lo:hi, :].rearrange("p t e -> p (t e)"), flat(0)[:, lo * P:hi * P], QSCALE,
                                                          b.e[:, d, lo:hi, :].rearrange("p t e -> p (t e)"), ALU.mult, ALU.mult, accum_out=b.den[:, d, j:j + 1])
                            if j < len(runs) - 1:
                                chain(last)
                        last.then_inc(weighed_sem, 1)
                    dve.wait_ge(weighed_sem, 2 * i + 2)
                    chain(v.tensor_tensor(b.dn[:, :], b.den[:, :, 0], b.den[:, :, 1], ALU.add))
                    chain(v.scalar_tensor_tensor(b.dn[:, :], b.dn[:, :], -1.0, b.dn[:, :], ALU.mult, ALU.max))
                    chain(v.tensor_tensor(b.dn[:, :], b.dn[:, :], b.em[:, :, t], ALU.max))
                    chain(v.reciprocal(b.rec[:, :], b.dn[:, :]))
                    out = m.h[:, t, h * P:(h + 1) * P]
                    dve.wait_ge(valued_sem, 2 * i + 1)
                    v.tensor_scalar(out, m.ps[:, 4, 0:P], b.rec[:, 0:1], None, ALU.mult).then_inc(stored_sem, 1)
                    dve.wait_ge(valued_sem, 2 * i + 2)
                    dve.wait_ge(stored_sem, 2 * i + 1)
                    v.scalar_tensor_tensor(out, m.ps[:, 5, 0:P], b.rec[:, 1:2], out, ALU.mult, ALU.add).then_inc(stored_sem, 1)
                    dve.wait_ge(stored_sem, 2 * i + 2)


def latent_attention(nc, m, a):
    with ExitStack() as ctx:
        m.v, m.knT, m.krT, m.qnT, m.qrT = buffers(nc, ctx, v=[NT, D], knT=[8, TOK], krT=[1, TOK], qnT=[8, LAT], qrT=[4, LAT])
        with ExitStack() as c1:
            flat = m.oT[:, :, :].rearrange("p a b -> p (a b)")
            m.qa = flat[:, 0:NTL * 384].rearrange("p (t n) -> p t n", n=384)
            m.kva = flat[:, NTL * 384:NTL * 384 + NT * 320].rearrange("p (t n) -> p t n", n=320)
            m.kr2, m.qaT, m.kvaT, m.qr = buffers(nc, c1, kr2=[NT, P], qaT=[3, LAT], kvaT=[2, TOK], qr=[NTL, 512])
            jobs = [(a["mla_w_down"][:, 0:384], 384, [("N", NTC + t, 384) for t in range(NTL)]),
                    (a["mla_w_down"][:, 384:704], 320, [("N", t, 320) for t in range(NT)])]
            products(nc, m, jobs, hT_of(m), lambda out, j, at, chain: nc.vector.tensor_copy(
                m.kva[:, at[0], :] if j else m.qa[:, at[0] - NTC, :], out), "vector", wslots=1)
            head_norms(nc, m, [(m.qa[:, :, :], None)], 384, EPS)
            head_norms(nc, m, [(m.kva[:, :, 0:256], None)], 256, EPS)
            rope(nc, m, [(m.kva[:, NTC + t, 256:320].unsqueeze(1), 1, t) for t in range(NTL)])
            with stage(nc, done=1) as (block, done_sem):
                @block.vector
                def _(dve):
                    for c in range(2):
                        nc.vector.tensor_copy(m.kr2[:, :, c * HD:(c + 1) * HD], m.kva[:, :, 256:320]).then_inc(done_sem, 1)
            gq, gkv = cols(m, "mla_q_norm"), cols(m, "mla_kv_norm")
            transposes(nc, m, [([m.qa[:, t, k * P:(k + 1) * P]], m.qaT[:, k:k + 1, t * P:(t + 1) * P], gq[:, k:k + 1], None) for t in range(NTL) for k in range(3)]
                       + [([m.kva[:, t, k * P:(k + 1) * P]], m.kvaT[:, k:k + 1, t * P:(t + 1) * P], gkv[:, k:k + 1], None) for t in range(NT) for k in range(2)]
                       + [([m.kr2[:, t, :]], m.krT[:, 0:1, t * P:(t + 1) * P], None, None) for t in range(NT)])
            w = a["mla_w_uq"]
            jobs = [(w[:, 0:512], 512, [("T", x, P, 0, LAT) for x in range(0, 512, P)]), (w[:, 512:1024], 512, [("T", x, P, 0, LAT) for x in range(0, 512, P)]),
                    (w[:, 1024:1536], 512, [("N", t, 512) for t in range(NTL)])]
            products(nc, m, jobs, lambda k, t0, tn, j: m.qaT[:, k, t0:t0 + tn], lambda out, j, at, chain: nc.vector.tensor_copy(
                m.qr[:, at[0], :] if j == 2 else m.qnT[:, 4 * j + at[0] // P, :], out), "vector", kt=3)
            rope(nc, m, [(m.qr[:, t, :].rearrange("p (n e) -> p n e", e=HD), 8, t) for t in range(NTL)])
            transposes(nc, m, [([m.qr[:, t, p * P:(p + 1) * P] for p in range(4)], m.qrT[:, :, t * P:(t + 1) * P], None, None) for t in range(NTL)])
            w = a["mla_w_ukv"]
            jobs = [(w[:, c:c + 512], 512, [("T", x, P, SEGS[s][0], SEGS[s][2]) for x in range(0, 512, P) for s in range(2)]) for c in (0, 512)]
            jobs += [(w[:, c:c + 512], 512, [("N", t, 512) for t in range(NT)]) for c in (1024, 1536)]
            products(nc, m, jobs, lambda k, t0, tn, j: m.kvaT[:, k, t0:t0 + tn], lambda out, j, at, chain: nc.vector.tensor_copy(
                m.v[:, at[0], (j - 2) * 512:(j - 1) * 512] if j >= 2 else m.knT[:, 4 * j + at[0] // P, at[2]:at[2] + at[3]], out), "vector", kt=2)
        (m.att,) = buffers(nc, ctx, att=[NTL, D])
        items = []
        for t in range(NTL):
            T = slice(t * P, (t + 1) * P)
            for h in range(8):
                R = slice(HD * (h % 2), HD * (h % 2 + 1))
                items.append(([[(m.qnT[:, h, T], m.knT[:, h, :]), (m.qrT[R, h // 2, T], m.krT[R, 0, :])]],
                              lambda k, h=h: m.v[:, k, h * P:(h + 1) * P], m.att[:, t, h * P:(h + 1) * P]))
        attention(nc, m, items, 1, float(192) ** -0.5, None)
        transposes(nc, m, [([m.att[:, t, (4 * g + q) * P:(4 * g + q + 1) * P] for q in range(4)], m.oT[:, 4 * g:4 * g + 4, t * P:(t + 1) * P], None, None)
                           for t in range(NTL) for g in range(2)])


def ffn_up(nc, m, a, layer, segs):
    w, cw, cb = a[f"ffn_up_{layer}"], cols(m, f"ffn_conv_w_{layer}"), cols(m, f"ffn_conv_b_{layer}")
    with ExitStack() as ctx:
        (m.pad,) = buffers(nc, ctx, pad=[2, PAD])
        pad_zeros(nc, m, [m.pad[:, 0, :], m.pad[:, 1, :]])
        jobs = []
        for c in range(0, DFF, 256):
            results = [("T", x + o, P, SEGS[s][0], SEGS[s][2]) for x in (0, P) for o in (0, 256) for s in segs]
            jobs.append(((w[:, c:c + 256], w[:, DFF + c:DFF + c + 256]), 512, results))

        def evac(out, j, at, chain):
            up = at[0] >= 256
            tile, seg = 2 * j + (at[0] % 256) // P, int(at[2] > 0)
            t0, p0, tn = SEGS[seg]
            dst = m.fT[:, tile, t0:t0 + tn]
            if up:
                nc.vector.wait_ge(m.aux_sem, len(segs) * tile + segs.index(seg) + 1)
                return nc.vector.tensor_tensor(dst, out, dst, ALU.mult)
            pad = m.pad[:, tile % 2, :]
            chain(nc.vector.tensor_copy(pad[:, p0:p0 + tn], out))
            return taps(nc.vector, chain, pad, seg, [cw[:, q * KF + tile:q * KF + tile + 1] for q in range(3)], cb[:, tile:tile + 1], dst)

        def silus(act, read_sem, aux_sem):
            for tile in range(KF):
                for i, seg in enumerate(segs):
                    t0, p0, tn = SEGS[seg]
                    act.wait_ge(read_sem, 2 * len(segs) * tile + i + 1)
                    nc.scalar.activation(m.fT[:, tile, t0:t0 + tn], m.fT[:, tile, t0:t0 + tn], ACT.Silu).then_inc(aux_sem, 1)

        products(nc, m, jobs, hT_of(m), evac, "vector", wslots=2, beside=silus)


def build(nc, a, where):
    m = Memory()
    m.where = where
    n_cols = a["cols"].shape[1]
    with ExitStack() as ctx:
        m.ps = ctx.enter_context(nc.psum_tensor("banks", [P, 8, 512], F32))
        m.ident, m.cols, m.rope_cos, m.rope_sin, m.qk_gain, m.neg_lam, m.subln, m.masks, m.restart, m.headsum, m.headspread, m.head_mask = buffers(
            nc, ctx, ident=[P], cols=[n_cols], rope_cos=[NTL, HD], rope_sin=[NTL, HD], qk_gain=[2 * HD], neg_lam=[1], subln=[1], masks=[len(MASKS), P], restart=[2, 512], headsum=[4, RH], headspread=[4, P], head_mask=[P])
        m.ident, m.cols, m.head_mask = m.ident[:, :], m.cols[:, :], m.head_mask[:, :]
        m.keep = ctx.enter_context(ExitStack())
        block_one(nc, m, a)
        second_block(nc, m, a)



def tables():
    c = {}
    f = np.float32
    c["ident"] = np.eye(P, dtype=f)
    pos = np.arange(LAT)
    inv = f(10000.0) ** (-np.arange(16, dtype=f) / f(16))
    ang = np.stack([(pos // 64).astype(f)[:, None] * inv, (pos % 64).astype(f)[:, None] * inv], 1)
    cs, sn = np.cos(ang.astype(np.float64)), np.sin(ang.astype(np.float64))
    fold = lambda x: x.reshape(NTL, P, HD).transpose(1, 0, 2).astype(f)
    c["rope_cos"] = fold(np.stack([cs, cs], 2).reshape(LAT, HD))
    c["rope_sin"] = fold(np.stack([-sn, sn], 2).reshape(LAT, HD))
    bands = np.zeros((4, LAT, LAT))
    for g, w in enumerate((2, 4, 8, 16)):
        lo, hi = np.clip(pos - w // 2, 0, LAT - 1), np.clip(pos + w // 2 - 1, 0, LAT - 1)
        s = np.arange(LAT)[:, None]
        bands[g] = ((s >= lo) & (s <= hi)) / (hi - lo + 1) - (s == pos)
    c["bands"] = bands.astype(f)
    r, q = np.arange(P)[:, None], np.arange(P)[None]
    chunk, block = r // CH == q // CH, r // 16 == q // 16
    below, above = (r > q) & chunk, (r < q) & chunk
    made = {"below16": below & block, "rest_below": below & ~block, "above16": above & block, "rest_above": above & ~block,
            "above_eq": above | (r == q), "below_eq": below | (r == q), "above": above, "below": below}
    c["masks"] = np.stack([made[n] for n in MASKS], 1).astype(f)
    c["head_mask"] = (r // HD == q // HD).astype(f)
    t = np.arange(512)
    c["restart"] = np.broadcast_to(np.stack([t % CH != 0, t % CH != CH - 1])[None], (P, 2, 512)).astype(f)
    c["headsum"] = np.stack([2 * p + np.arange(P)[:, None] // HD == np.arange(RH)[None] for p in range(4)], 1).astype(f)
    c["headspread"] = np.concatenate([c["headsum"].transpose(2, 1, 0), np.zeros((P - RH, 4, P))]).astype(f)
    c["iota32"] = np.broadcast_to(np.arange(N_EXP), (P, 1, N_EXP)).astype(f)
    c["tri"] = (r < q).astype(f)
    c["tok_id"] = (np.arange(NTL)[None] * P + np.arange(P)[:, None]).astype(f)
    c["block_id"] = np.broadcast_to(np.arange(TAB), (P, TAB)).astype(f)
    c["pick"] = np.stack([(np.arange(8)[:, None] == n) * np.ones((1, P)) for n in range(8)], 1).astype(f)
    c["causal"] = np.stack([np.where(q <= r, 0, -BIG), np.where(q >= r, 0, -BIG)], 1).astype(f)
    seen = np.full((2, NT, NT), -BIG)
    for d in range(2):
        for t in range(NT):
            for lo, hi in key_runs(d, t):
                for k in range(lo, hi):
                    if k != t:
                        seen[d, t, k] = 0
    c["seen"] = np.broadcast_to(seen, (P, 2, NT, NT)).astype(f)
    for L in (CTX, LAT):
        s, w = np.arange(L)[:, None], (np.arange(L)[None] + 0.5) * np.pi / L
        c[f"dft_c_{L}"], c[f"dft_s_{L}"] = np.cos(s * w).astype(f), np.sin(s * w).astype(f)
        c[f"idft_c_{L}"], c[f"idft_s_{L}"] = (np.cos(s * w).T / L).astype(f), (-np.sin(s * w).T / L).astype(f)
        pos = np.arange(L, dtype=f)
        t = (pos / f(L - 1))[:, None]
        freq = np.linspace(1e-4, 15, 16, dtype=f)
        ang = f(2.0 * np.pi / L) * pos[:, None] * freq[None]
        c[f"hy_z_{L}"] = np.concatenate([t, np.cos(ang), -np.sin(ang)], 1).T.astype(f)
        deltas = np.linspace(np.log(1e-2) / 0.3, np.log(1e-2) / 1.5, 512, dtype=f)
        decay = np.exp(-t * np.abs(np.tile(deltas, 2))[None]) + f(0.05)
        decay[0, 512:] = 0
        c[f"hy_decay_{L}"] = decay.astype(f)
    return c


def columns(v):
    v = np.asarray(v).reshape(-1)
    return v.reshape(-1, P).T if v.size % P == 0 else np.concatenate([v, np.zeros(P - v.size, v.dtype)])[:, None]


def packed_columns(i):
    named = {"c": i["c"], "c_ctx": i["c_ctx"], "b_ada": i["b_ada"], "norm1_g": i["norm1_g"], "norm2_g": i["norm2_g"],
             "pool_scale": i["pool_scale"], "subln_g": i["subln_g"], "mu0": i["shift_mu"][0, 0], "mu1": i["shift_mu"][0, 1],
             "w0": i["decay_w0"], "a0": i["aaa_a0"], "k_k": i["k_k"], "k_a": i["k_a"], "r_k": i["r_k"],
             "gn_w": i["gn_w"], "gn_b": i["gn_b"],
             "c_2": i["c_2"], "c_ctx_2": i["c_ctx_2"], "ada_b_0": i["ada_b_0_2"], "ada_b_1": i["ada_b_1_2"],
             "norm_mix_0": i["norm_mix_0_2"], "norm_ffn_0": i["norm_ffn_0_2"], "norm_mix_1": i["norm_mix_1_2"],
             "norm_ffn_1": i["norm_ffn_1_2"], "hy_conv_w": i["hy_conv_w_2"], "hy_conv_b": i["hy_conv_b_2"], "hy_bias": i["hy_bias_2"],
             "ml_conv_w": i["ml_conv_w_2"], "ml_norm_g": i["ml_norm_g_2"],
             "ffn_conv_w_0": i["ffn_conv_w_0_2"], "ffn_conv_b_0": i["ffn_conv_b_0_2"],
             "ffn_conv_w_1": i["ffn_conv_w_1_2"], "ffn_conv_b_1": i["ffn_conv_b_1_2"],
             "mla_q_norm": i["mla_q_norm_2"], "mla_kv_norm": i["mla_kv_norm_2"],
             "hy_fb1": i["hy_fb1_2"], "hy_fb2": i["hy_fb2_2"], "hy_freq": i["hy_freq_2"],
             "gate_i": i["ml_gate_b_2"].reshape(2, 2, 4)[:, 0], "gate_f": i["ml_gate_b_2"].reshape(2, 2, 4)[:, 1]}
    parts, where, at = [], {}, 0
    for name, v in named.items():
        c = columns(v)
        where[name] = (at, c.shape[1])
        at += c.shape[1]
        parts.append(c)
    return np.ascontiguousarray(np.concatenate(parts, 1)), where


def laid_out(i):
    out = tables()
    out["cols"], where = packed_columns(i)
    out["rows"] = np.concatenate([i["q_norm_g"].reshape(-1), i["k_norm_g"].reshape(-1), i["lambda_qk"].reshape(-1),
                                  i["final_norm_2"].reshape(-1)])[None]
    out["b_ada_row"] = i["b_ada"].reshape(1, -1)
    out["ada_b_0_row"] = i["ada_b_0_2"].reshape(1, -1)
    out["ada_b_1_row"] = i["ada_b_1_2"].reshape(1, -1)
    for name in ("x", "ctx", "w_ada", "w_in", "pool_w", "decay_w2", "aaa_a2", "gate_w2", "w_br", "w_out", "w_exp_gate",
                 "w_exp_up", "w_exp_down", "ctx_2"):
        out[name] = i[name][0]
    out["w_router"] = np.concatenate([i["w_router_group"][0], i["w_router_expert"][0]], 1)
    w = i["w_in_0_2"]
    out["w_in_0"] = np.concatenate([w[:, :3584], w[:, 3584:].reshape(D, 2, 2, 4).transpose(0, 2, 1, 3).reshape(D, 16)], 1)
    for name in ("ada_w_0_2", "ada_w_1_2", "w_out_0_2", "ffn_up_0_2", "ffn_down_0_2", "ffn_up_1_2", "ffn_down_1_2",
                 "mla_w_down_2", "mla_w_uq_2", "mla_w_ukv_2", "mla_w_o_2", "hy_fw1_2", "hy_fw2_2", "hy_fw3_2"):
        out[name[:-2]] = i[name]
    w = i["mla_w_uq_2"].reshape(384, 8, 192)
    out["mla_w_uq"] = np.concatenate([w[:, :, :P].reshape(384, -1), w[:, :, P:].reshape(384, -1)], 1)
    w = i["mla_w_ukv_2"].reshape(256, 8, 2, P)
    out["mla_w_ukv"] = w.transpose(0, 2, 1, 3).reshape(256, -1)
    return {k: np.ascontiguousarray(v) for k, v in out.items()}, where


def kernel(**inputs):
    import concourse.bacc as _bacc
    from concourse.bass_utils import run_bass_kernel_spmd as _run

    i = {k: np.asarray(v) for k, v in inputs.items()}
    arrays, where = laid_out(i)
    nc = _bacc.Bacc("TRN2", target_bir_lowering=False, num_devices=1)
    args = {name: nc.dram_tensor(f"in_{name}", v.shape, mybir.dt.from_np(v.dtype), kind="ExternalInput").ap() for name, v in arrays.items()}
    args["out"] = nc.dram_tensor("out_0", (1, LAT, D), F32, kind="ExternalOutput").ap()
    build(nc, args, where)
    r = _run(nc, [{f"in_{name}": v for name, v in arrays.items()}], core_ids=[0])
    return r.results[0]["out_0"]
```

```python
from contextlib import ExitStack, contextmanager

import numpy as np
import concourse.bass as bass
from concourse import mybir

ALU = mybir.AluOpType
ACT = mybir.ActivationFunctionType
F32 = mybir.dt.float32
AX = mybir.AxisListType.X

P = 128
D = 1024
KD = D // P
CTX = 256
LAT = 512
TOK = CTX + LAT
NT = TOK // P
NTC = CTX // P
NTL = LAT // P
PAD = TOK + 3
SEGS = ((0, 1, CTX), (CTX, CTX + 2, LAT))
BRW = 512
KB = BRW // P
HEADS = 4
HD = 64
RH = 8
CH = 64
N_EXP = 32
N_GRP = 4
EFF = 512
DFF = 2816
KF = DFF // P
EPS = 1e-6
GN_EPS = 64e-5
LAM_INIT = 0.2
BIG = 1e30


class Memory:
    pass


@contextmanager
def stage(nc, **names):
    sems = []
    handles = []
    for key, n in names.items():
        made = [nc.alloc_semaphore(f"{key}_{nc.next_id()}") for _ in range(n)]
        handles += made
        sems.append(made[0] if n == 1 else made)
    with nc.Block() as block:
        yield block, *sems
    nc.clear_and_free_semaphores(handles)
    nc.all_engine_barrier()


class Chain:

    def __init__(self, eng, sem):
        self.eng, self.sem, self.n = eng, sem, 0

    def __call__(self, ins):
        self.n += 1
        ins.then_inc(self.sem, 1)
        self.eng.wait_ge(self.sem, self.n)


def buffers(nc, ctx, **shapes):
    return [ctx.enter_context(nc.sbuf_tensor(f"{name}_{nc.next_id()}", [P, *shape], F32)) for name, shape in shapes.items()]


def bc(ap, n):
    return ap.to_broadcast([ap.shape[0], ap.shape[1], n])



WSLOTS = 3
SIDE_SLOTS = 2
F32R = mybir.dt.float32r


def two_parts(nc, ctx, k, tokens, side="left"):
    return [ctx.enter_context(nc.sbuf_tensor(f"{name}_{nc.next_id()}", [P, k, tokens], F32R, side=side)) for name in ("leading", "rest")]


@contextmanager
def halves(nc, x):
    with ExitStack() as ctx:
        hi, lo = two_parts(nc, ctx, x.shape[1], x.shape[2])
        with stage(nc, rounded=1, rest=1) as (block, rounded_sem, rest_sem):
            @block.scalar
            def _(act):
                for k in range(x.shape[1]):
                    nc.scalar.copy(hi[:, k, :], x[:, k, :]).then_inc(rounded_sem, 1)

            @block.vector
            def _(dve):
                for k in range(x.shape[1]):
                    dve.wait_ge(rounded_sem, k + 1)
                    nc.vector.tensor_tensor(lo[:, k, :], x[:, k, :], hi[:, k, :].bitcast(F32), ALU.subtract).then_inc(rest_sem, 1)
        yield hi, lo


def of_halves(pair, shift=0):
    hi, lo = pair
    return lambda k, t0, tn, j: (hi[:, k, t0 - shift:t0 - shift + tn], lo[:, k, t0 - shift:t0 - shift + tn])


def products(nc, m, jobs, xT, evac, evac_on, banks=4, kt=KD, wslots=WSLOTS, beside=None, width=512, split=False, k_chunks=1, side=()):
    if split:
        wslots = 1
    size = -(-kt // k_chunks)
    steps = [(j, w, n, results, k0, min(k0 + size, kt)) for j, (w, n, results) in enumerate(jobs) for k0 in range(0, kt, size)]
    ends = [0]
    for step in steps:
        ends.append(ends[-1] + len(step[3]))
    total = sum(len(results) for w, n, results in jobs)
    with ExitStack() as ctx:
        slots = [ctx.enter_context(nc.sbuf_tensor(f"w_{nc.next_id()}", [P, size, width], F32)) for _ in range(wslots)]
        leading, rest = [[ctx.enter_context(nc.sbuf_tensor(f"{name}_{nc.next_id()}", [P, size, width], F32R)) for _ in range(2 if split else 0)]
                         for name in ("w_leading", "w_rest")]
        side_w = [ctx.enter_context(nc.sbuf_tensor(f"ws_{nc.next_id()}", [P, KD, P], F32)) for _ in range(SIDE_SLOTS if side else 0)]
        with stage(nc, w_landed=wslots, rounded=1, parted=1, made=1, read=1, chain=1, aux=1, side_landed=SIDE_SLOTS, side_made=1, side_read=1) as (
                block, w_landed_sem, rounded_sem, parted_sem, made_sem, read_sem, chain_sem, aux_sem,
                side_landed_sem, side_made_sem, side_read_sem):
            m.aux_sem = aux_sem
            landed = w_landed_sem if wslots > 1 else [w_landed_sem]
            landings = [16 * (len(step[1]) if isinstance(step[1], tuple) else 1) for step in steps]

            def k_halves(s):
                n = steps[s][5] - steps[s][4]
                return ((0, (n + 1) // 2), ((n + 1) // 2, n))

            def sides_between(r0, r1):
                return range(-(-r0 * len(side) // total), -(-r1 * len(side) // total))

            @block.sync
            def _(sp):
                def load_side(t):
                    sp.dma_start(side_w[t % SIDE_SLOTS][:, :, :], side[t][0].rearrange("(k p) n -> p k n", p=P)
                                 ).then_inc(side_landed_sem[t % SIDE_SLOTS], 16)

                ahead = 2 if split else wslots
                for s in range(len(steps) + ahead - 1):
                    if s < len(steps):
                        j, w, n, results, k0, k1 = steps[s]
                        if s >= wslots and split:
                            sp.wait_ge(parted_sem, 2 * (s - wslots + 1))
                        elif s >= wslots:
                            sp.wait_ge(made_sem, ends[s - wslots + 1])
                        at = 0
                        for part in (w if isinstance(w, tuple) else (w,)):
                            pn = part.shape[1]
                            sp.dma_start(slots[s % wslots][:, 0:k1 - k0, at:at + pn], part[k0 * P:k1 * P, :].rearrange("(k p) n -> p k n", p=P)
                                         ).then_inc(landed[s % wslots], 16)
                            at += pn
                    if s == 0:
                        for t in range(min(SIDE_SLOTS, len(side))):
                            load_side(t)
                    running = s - ahead + 1
                    if side and running >= 0:
                        for t in sides_between(ends[running], ends[running + 1]):
                            if t + SIDE_SLOTS < len(side):
                                sp.wait_ge(side_made_sem, t + 1)
                                load_side(t + SIDE_SLOTS)

            def round_weights(act, s):
                if s >= 2:
                    act.wait_ge(made_sem, ends[s - 1])
                act.wait_ge(landed[s % wslots], sum(landings[s % wslots:s + 1:wslots]))
                n = steps[s][2]
                for k0, k1 in k_halves(s):
                    nc.scalar.copy(leading[s % 2][:, k0:k1, 0:n], slots[s % wslots][:, k0:k1, 0:n]).then_inc(rounded_sem, 1)

            def part_weights(dve, s):
                n = steps[s][2]
                for q, (k0, k1) in enumerate(k_halves(s)):
                    dve.wait_ge(rounded_sem, 2 * s + q + 1)
                    nc.vector.tensor_tensor(rest[s % 2][:, k0:k1, 0:n], slots[s % wslots][:, k0:k1, 0:n], leading[s % 2][:, k0:k1, 0:n].bitcast(F32), ALU.subtract).then_inc(parted_sem, 1)

            def bank_of(r, kind, at):
                return m.ps[0:at[1], r % banks, 0:at[3]] if kind == "T" else m.ps[:, r % banks, 0:at[1]]

            @block.tensor
            def _(pe):
                before = 0
                for s, (j, w, n, results, k0, k1) in enumerate(steps):
                    if not split:
                        pe.wait_ge(landed[s % wslots], sum(landings[s % wslots:s + 1:wslots]))
                    for i, (kind, *at) in enumerate(results):
                        r = before + i
                        if r >= banks and k0 == 0:
                            pe.wait_ge(read_sem, r - banks + 1)

                        def operands(k):
                            x = xT(k, at[2], at[3], j) if kind == "T" else xT(k, at[0] * P, P, j)
                            if split:
                                hi, lo = leading[s % 2][:, k - k0, :], rest[s % 2][:, k - k0, :]
                                pairs = [(lo, x[0]), (hi, x[1]), (hi, x[0])]
                            else:
                                pairs = [(slots[s % wslots][:, k - k0, :], x)]
                            if kind == "T":
                                return [(w_[:, at[0]:at[0] + at[1]], x_) for w_, x_ in pairs]
                            return [(x_, w_[:, 0:at[1]]) for w_, x_ in pairs]

                        for k in range(k0, k1):
                            if split and i == 0 and k - k0 in (0, k_halves(s)[1][0]):
                                pe.wait_ge(parted_sem, 2 * s + 1 + (k > k0))
                            each = operands(k)
                            for q, (lhsT, rhs) in enumerate(each):
                                mm = nc.tensor.matmul(bank_of(r, kind, at), lhsT, rhs, start=(k == 0 and q == 0), stop=(k == kt - 1 and q == len(each) - 1))
                        mm.then_inc(made_sem, 1)
                        if k1 == kt:
                            for t in sides_between(r, r + 1):
                                pe.wait_ge(side_landed_sem[t % SIDE_SLOTS], 16 * (t // SIDE_SLOTS + 1))
                                if t >= 2:
                                    pe.wait_ge(side_read_sem, t - 1)
                                for k in range(KD):
                                    mm = nc.tensor.matmul(m.ps[:, 6 + t % 2, 0:2], side_w[t % SIDE_SLOTS][:, k, :], side[t][1](k), start=(k == 0), stop=(k == KD - 1))
                                mm.then_inc(side_made_sem, 1)
                    if k1 == kt:
                        before += len(results)

            def each_result(eng, between, of_result):
                if split:
                    between(eng, 0)
                r = 0
                for s, (j, w, n, results, k0, k1) in enumerate(steps):
                    for i, (kind, *at) in enumerate(results):
                        if split and i == len(results) // 2 and s + 1 < len(steps):
                            between(eng, s + 1)
                        if k1 == kt:
                            of_result(eng, r, ends[s] + i + 1, j, kind, at)
                            r += 1

            chain = Chain(nc.scalar if evac_on == "scalar" else nc.vector, chain_sem)

            def read(eng, r, count, j, kind, at):
                eng.wait_ge(made_sem, count)
                evac(bank_of(r, kind, at), j, at, chain).then_inc(read_sem, 1)

            def read_both(dve, r, count, j, kind, at):
                if evac_on == "vector":
                    read(dve, r, count, j, kind, at)
                for t in sides_between(r, r + 1):
                    dve.wait_ge(side_made_sem, t + 1)
                    nc.vector.tensor_scalar(side[t][2], m.ps[:, 6 + t % 2, 0:2], side[t][3], None, ALU.add).then_inc(side_read_sem, 1)

            def follow(eng, r, count, j, kind, at):
                if beside is not None:
                    beside(eng, r, j, at, read_sem, aux_sem)

            @block.scalar
            def _(act):
                each_result(act, round_weights, read if evac_on == "scalar" else follow)

            @block.vector
            def _(dve):
                each_result(dve, part_weights, read_both)


def transposes(nc, m, moves):
    with stage(nc, turned=1, read=1) as (block, turned_sem, read_sem):
        @block.tensor
        def _(pe):
            for i, (blocks, dst, mul, add) in enumerate(moves):
                if i >= 4:
                    pe.wait_ge(read_sem, i - 3)
                for n, b in enumerate(blocks):
                    mm = nc.tensor.transpose(m.ps[:, i % 4, n * P:(n + 1) * P], b, m.ident)
                mm.then_inc(turned_sem, 1)

        @block.vector
        def _(dve):
            for i, (blocks, dst, mul, add) in enumerate(moves):
                dve.wait_ge(turned_sem, i + 1)
                src = m.ps[:, i % 4, 0:len(blocks) * P].rearrange("p (n t) -> p n t", t=P)
                if mul is None:
                    nc.vector.tensor_copy(dst, src).then_inc(read_sem, 1)
                elif add is None:
                    nc.vector.tensor_scalar(dst, src, mul, None, ALU.mult).then_inc(read_sem, 1)
                else:
                    nc.vector.tensor_scalar(dst, src, mul, add, ALU.mult, ALU.add).then_inc(read_sem, 1)


ADA = (("w_ada", "c", "c_ctx", "b_ada"), ("ada_w_0", "c_2", "c_ctx_2", "ada_b_0"), ("ada_w_1", "c_2", "c_ctx_2", "ada_b_1"))


def conditions(nc, m):
    with stage(nc, done=1) as (block, done_sem):
        @block.scalar
        def _(act):
            for i, (_, lat, ctx, _) in enumerate(ADA):
                for j, c in enumerate((lat, ctx)):
                    nc.scalar.activation(m.cond[:, i, :, j], cols(m, c), ACT.Silu).then_inc(done_sem, 1)


def modulation_tiles(m, a, i, first, end):
    w, bias = a[ADA[i][0]], cols(m, ADA[i][3])
    return [(w[:, f * P:(f + 1) * P], lambda k: m.cond[:, i, k, :], m.mod[:, i, f, :], bias[:, f:f + 1]) for f in range(first, end)]


def modulation(nc, m, a, i, first, end):
    w, bias = a[ADA[i][0]], cols(m, ADA[i][3])
    jobs = [(w[:, f * P:(f + 4) * P], 4 * P, [("T", x * P, P, 0, 2) for x in range(4)]) for f in range(first, end, 4)]

    def evac(out, j, at, chain):
        tile = first + 4 * j + at[0] // P
        return nc.vector.tensor_scalar(m.mod[:, i, tile, :], out, bias[:, tile:tile + 1], None, ALU.add)

    products(nc, m, jobs, lambda k, t0, tn, j: m.cond[:, i, k, :], evac, "vector")


def gate_rows(nc, m, ctx, i, chunk, n):
    (rows,) = buffers(nc, ctx, gate_rows=[n, D])
    with ExitStack() as own:
        (wide,) = buffers(nc, own, wide=[n, KD, P])
        with stage(nc, widened=1, made=1) as (block, widened_sem, made_sem):
            @block.tensor
            def _(pe):
                for j in range(n):
                    pe.wait_ge(widened_sem, j + 1)
                    for f in range(KD):
                        mm = nc.tensor.matmul(m.ps[:, 2 * j + f // 4, (f % 4) * P:(f % 4 + 1) * P], wide[:, j, f, :], m.ident, start=True, stop=True)
                    mm.then_inc(made_sem, 1)

            @block.vector
            def _(dve):
                for j in range(n):
                    nc.vector.tensor_copy(wide[:, j, :, :], bc(m.mod[:, i, KD * chunk:KD * (chunk + 1), j:j + 1], P)).then_inc(widened_sem, 1)
                for j in range(n):
                    dve.wait_ge(made_sem, j + 1)
                    nc.vector.tensor_copy(rows[:, j, :], m.ps[:, 2 * j:2 * j + 2, :].rearrange("p a b -> p (a b)"))
    return rows


def normed(nc, m, tiles, hT, affine):
    parts = hT if isinstance(hT, list) else None
    kinds = sorted(affine)
    n = len(tiles)
    with ExitStack() as ctx:
        b = Memory()
        b.xn, b.sq, b.whole, b.ss, b.root, b.rstd, b.gain = buffers(nc, ctx, xn=[2, D], sq=[2, D], whole=[2, 4, P], ss=[n], root=[n], rstd=[n], gain=[len(kinds), KD])
        with stage(nc, squared=1, summed=1, rooted=1, inverse=1, scaled=1, turned=1, read=1, rounded=1, rest=1, chain=1) as (
                block, squared_sem, summed_sem, rooted_sem, inverse_sem, scaled_sem, turned_sem, read_sem, rounded_sem, rest_sem, chain_sem):
            def round_tile(act, i):
                for h in range(2):
                    act.wait_ge(read_sem, 2 * i + h + 1)
                    nc.scalar.copy(parts[0][:, 4 * h:4 * h + 4, tiles[i][1]:tiles[i][1] + P], b.whole[:, h, :, :]).then_inc(rounded_sem, 1)

            @block.scalar
            def _(act):
                for i, (x, t0, k) in enumerate(tiles):
                    if i >= 2:
                        act.wait_ge(squared_sem, i - 1)
                    nc.scalar.activation(b.sq[:, i % 2, :], x, ACT.Square, accum_out=b.ss[:, i:i + 1]).then_inc(squared_sem, 1)
                act.wait_ge(summed_sem, 1)
                nc.scalar.activation(b.root[:, :], b.ss[:, :], ACT.Sqrt).then_inc(rooted_sem, 1)
                act.wait_ge(inverse_sem, 1)
                for i in range(n):
                    if i >= 2:
                        act.wait_ge(turned_sem, 2 * (i - 1))
                    nc.scalar.activation(b.xn[:, i % 2, :], tiles[i][0], ACT.Copy, scale=b.rstd[:, i:i + 1]).then_inc(scaled_sem, 1)
                    if parts and i:
                        round_tile(act, i - 1)
                if parts:
                    round_tile(act, n - 1)

            @block.vector
            def _(dve):
                chain = Chain(dve, chain_sem)
                for i, k in enumerate(kinds):
                    g, scale, shift = affine[k]
                    chain(nc.vector.scalar_tensor_tensor(b.gain[:, i, :], scale, 1.0, g, ALU.add, ALU.mult))
                dve.wait_ge(squared_sem, n)
                nc.vector.tensor_scalar(b.ss[:, :], b.ss[:, :], 1.0 / D, EPS, ALU.mult, ALU.add).then_inc(summed_sem, 1)
                dve.wait_ge(rooted_sem, 1)
                nc.vector.reciprocal(b.rstd[:, :], b.root[:, :]).then_inc(inverse_sem, 1)

                def rest_of(q):
                    f, t0 = 4 * (q % 2), tiles[q // 2][1]
                    dve.wait_ge(rounded_sem, q + 1)
                    nc.vector.tensor_tensor(parts[1][:, f:f + 4, t0:t0 + P], b.whole[:, q % 2, :, :],
                                            parts[0][:, f:f + 4, t0:t0 + P].bitcast(F32), ALU.subtract).then_inc(rest_sem, 1)

                for i, (x, t0, k) in enumerate(tiles):
                    shift = affine[k][2]
                    for h in range(2):
                        dve.wait_ge(turned_sem, 2 * i + h + 1)
                        if parts and i:
                            rest_of(2 * i + h - 2)
                            dve.wait_ge(rest_sem, 2 * i + h - 1)
                        for j in range(4):
                            f = 4 * h + j
                            last = nc.vector.tensor_scalar(
                                b.whole[:, h, j, :] if parts else hT[:, f, t0:t0 + P], m.ps[:, (2 * i + h) % 4, j * P:(j + 1) * P],
                                b.gain[:, kinds.index(k), f:f + 1], shift[:, f:f + 1], ALU.mult, ALU.add)
                        last.then_inc(read_sem, 1)
                if parts:
                    rest_of(2 * n - 2)
                    rest_of(2 * n - 1)

            @block.tensor
            def _(pe):
                for i in range(n):
                    pe.wait_ge(scaled_sem, i + 1)
                    for h in range(2):
                        q = 2 * i + h
                        if q >= 4:
                            pe.wait_ge(read_sem, q - 3)
                        for j in range(4):
                            f = 4 * h + j
                            mm = nc.tensor.transpose(m.ps[:, q % 4, j * P:(j + 1) * P], b.xn[:, i % 2, f * P:(f + 1) * P], m.ident)
                        mm.then_inc(turned_sem, 1)


def head_norms(nc, m, xs, width, eps, out_scale=None):
    total = sum(x.shape[1] for x, g in xs)
    biggest = max(x.shape[1] for x, g in xs)
    with ExitStack() as ctx:
        b = Memory()
        b.sq, b.ss, b.root, b.rstd = buffers(nc, ctx, sq=[biggest, width], ss=[total], root=[total], rstd=[total, 1])
        with stage(nc, summed=1, rooted=1, chain=1) as (block, summed_sem, rooted_sem, chain_sem):
            @block.scalar
            def _(act):
                act.wait_ge(summed_sem, 1)
                nc.scalar.activation(b.root[:, :], b.ss[:, :], ACT.Sqrt).then_inc(rooted_sem, 1)

            @block.vector
            def _(dve):
                chain = Chain(dve, chain_sem)
                o = 0
                for x, g in xs:
                    a = x.shape[1]
                    chain(nc.vector.tensor_tensor(b.sq[:, 0:a, :], x, x, ALU.mult))
                    chain(nc.vector.tensor_reduce(b.ss[:, o:o + a], b.sq[:, 0:a, :], AX, ALU.add))
                    o += a
                nc.vector.tensor_scalar(b.ss[:, :], b.ss[:, :], 1.0 / width, eps, ALU.mult, ALU.add).then_inc(summed_sem, 1)
                dve.wait_ge(rooted_sem, 1)
                chain(nc.vector.reciprocal(b.rstd[:, :, 0], b.root[:, :]))
                o = 0
                for x, g in xs:
                    a = x.shape[1]
                    chain(nc.vector.tensor_tensor(x, x, bc(b.rstd[:, o:o + a, :], width), ALU.mult))
                    if g is not None:
                        chain(nc.vector.tensor_tensor(x, x, g.unsqueeze(1).to_broadcast([P, a, width]), ALU.mult))
                    o += a


def rope(nc, m, tiles):
    with ExitStack() as ctx:
        b = Memory()
        (b.swapped,) = buffers(nc, ctx, swapped=[2, 8, HD])
        with stage(nc, chain=1) as (block, chain_sem):
            @block.vector
            def _(dve):
                chain = Chain(dve, chain_sem)
                for i, (x, heads, t) in enumerate(tiles):
                    xv = x.rearrange("p n (a h e) -> p n a h e", a=2, h=2)
                    sw = b.swapped[:, i % 2, 0:heads, :].rearrange("p n (a h e) -> p n a h e", a=2, h=2)
                    sn = m.rope_sin[:, t, :].rearrange("p (a h e) -> p a h e", a=2, h=2)
                    for h in range(2):
                        nc_sin = sn[:, :, h, :].unsqueeze(1).to_broadcast([P, heads, 2, 16])
                        chain(nc.vector.tensor_tensor(sw[:, :, :, h, :], xv[:, :, :, 1 - h, :], nc_sin, ALU.mult))
                    cs = m.rope_cos[:, t, :].unsqueeze(1).to_broadcast([P, heads, HD])
                    chain(nc.vector.tensor_tensor(x, x, cs, ALU.mult))
                    chain(nc.vector.tensor_tensor(x, x, b.swapped[:, i % 2, 0:heads, :], ALU.add))


def attention(nc, m, items, maps, scale, other_weight):
    n = len(items)
    with ExitStack() as ctx:
        b = Memory()
        b.e, b.a, b.aT, b.mx, b.nb, b.sums, b.rec = buffers(
            nc, ctx, e=[2, maps, TOK], a=[2, TOK], aT=[TOK], mx=[maps], nb=[2, maps], sums=[2, maps], rec=[maps])
        with stage(nc, scored=1, biased=1, exped=1, mixed=1, turned=1, copied=1, valued=1, stored=1, chain=1) as (
                block, scored_sem, biased_sem, exped_sem, mixed_sem, turned_sem, copied_sem, valued_sem, stored_sem, chain_sem):
            @block.tensor
            def _(pe):
                def scores(i):
                    if i >= 1:
                        pe.wait_ge(exped_sem, maps * i)
                    for q in range(maps):
                        parts = items[i][0][q]
                        for j, (lhsT, rhs) in enumerate(parts):
                            for c, w in ((0, 512), (512, 256)):
                                mm = nc.tensor.matmul(m.ps[:, 2 * q + c // 512, 0:w], lhsT, rhs[:, c:c + w],
                                                      start=(j == 0), stop=(j == len(parts) - 1))
                    mm.then_inc(scored_sem, 1)

                scores(0)
                for i in range(n):
                    if i + 1 < n:
                        scores(i + 1)
                    pe.wait_ge(mixed_sem, i + 1)
                    if i >= 1:
                        pe.wait_ge(copied_sem, i)
                    for k in range(NT):
                        mm = nc.tensor.transpose(m.ps[:, 4 + k // 4, (k % 4) * P:(k % 4 + 1) * P], b.a[:, i % 2, k * P:(k + 1) * P], m.ident)
                    mm.then_inc(turned_sem, 1)
                    pe.wait_ge(copied_sem, i + 1)
                    if i >= 1:
                        pe.wait_ge(stored_sem, i)
                    for k in range(NT):
                        mm = nc.tensor.matmul(m.ps[:, 6, 0:P], b.aT[:, k * P:(k + 1) * P], items[i][1](k),
                                              start=(k == 0), stop=(k == NT - 1))
                    mm.then_inc(valued_sem, 1)

            @block.scalar
            def _(act):
                for i in range(n):
                    act.wait_ge(biased_sem, i + 1)
                    for q in range(maps):
                        nc.scalar.activation(b.e[:, i % 2, q, :], m.ps[:, 2 * q:2 * q + 2, :].rearrange("p a b -> p (a b)")[:, 0:TOK],
                                             ACT.Exp, bias=b.nb[:, i % 2, q:q + 1], scale=scale,
                                             accum_out=b.sums[:, i % 2, q:q + 1]).then_inc(exped_sem, 1)
                    act.wait_ge(turned_sem, i + 1)
                    if i >= 1:
                        act.wait_ge(valued_sem, i)
                    nc.scalar.copy(b.aT[:, :], m.ps[:, 4:6, :].rearrange("p a b -> p (a b)")[:, 0:TOK]).then_inc(copied_sem, 1)

            @block.vector
            def _(dve):
                chain = Chain(dve, chain_sem)

                def maxima(i):
                    dve.wait_ge(scored_sem, i + 1)
                    for q in range(maps):
                        last = nc.vector.tensor_reduce(b.mx[:, q:q + 1], m.ps[:, 2 * q:2 * q + 2, :].rearrange("p a b -> p (a b)")[:, 0:TOK], AX, ALU.max)
                        chain(last)
                    if i >= 2:
                        dve.wait_ge(exped_sem, maps * (i - 1))
                    nc.vector.tensor_scalar(b.nb[:, i % 2, :], b.mx[:, :], -scale, None, ALU.mult).then_inc(biased_sem, 1)

                maxima(0)
                for i in range(n):
                    dve.wait_ge(exped_sem, maps * (i + 1))
                    chain(nc.vector.reciprocal(b.rec[:, :], b.sums[:, i % 2, :]))
                    if i >= 2:
                        dve.wait_ge(turned_sem, i - 1)
                    if maps == 1:
                        nc.vector.tensor_scalar(b.a[:, i % 2, :], b.e[:, i % 2, 0, :], b.rec[:, 0:1], None, ALU.mult).then_inc(mixed_sem, 1)
                    else:
                        chain(nc.vector.tensor_tensor(b.rec[:, 1:2], b.rec[:, 1:2], other_weight, ALU.mult))
                        chain(nc.vector.tensor_scalar(b.a[:, i % 2, :], b.e[:, i % 2, 0, :], b.rec[:, 0:1], None, ALU.mult))
                        nc.vector.scalar_tensor_tensor(b.a[:, i % 2, :], b.e[:, i % 2, 1, :], b.rec[:, 1:2], b.a[:, i % 2, :],
                                                       ALU.mult, ALU.add).then_inc(mixed_sem, 1)
                    if i + 1 < n:
                        maxima(i + 1)
                    dve.wait_ge(valued_sem, i + 1)
                    nc.vector.tensor_copy(items[i][2], m.ps[:, 6, 0:P]).then_inc(stored_sem, 1)


def cols(m, name):
    a, n = m.where[name]
    return m.cols[:, a:a + n]


def load(nc, pairs):
    with stage(nc, landed=1) as (block, landed_sem):
        @block.sync
        def _(sp):
            for dst, src in pairs:
                sp.dma_start(dst[:], src).then_inc(landed_sem, 16)
            sp.wait_ge(landed_sem, 16 * len(pairs))


def load_constants(nc, m, a):
    m.loads = [(m.ident, a["ident"]), (m.cols, a["cols"]), (m.rope_cos, a["rope_cos"]), (m.rope_sin, a["rope_sin"]),
               (m.qk_gain, a["rows"][:, 0:2 * HD].to_broadcast([P, 2 * HD])),
               (m.lam_rows, a["rows"][:, 2 * HD:6 * HD].to_broadcast([P, 4 * HD])),
               (m.masks, a["masks"]), (m.restart, a["restart"]), (m.headsum, a["headsum"]), (m.headspread, a["headspread"]),
               (m.head_mask, a["head_mask"])]
    with stage(nc, landed=1, lam=1, chain=1) as (block, landed_sem, lam_sem, chain_sem):
        @block.sync
        def _(sp):
            for dst, src in m.loads:
                sp.dma_start(dst[:], src).then_inc(landed_sem, 16)
            sp.wait_ge(landed_sem, 16 * len(m.loads))

        @block.vector
        def _(dve):
            chain = Chain(dve, chain_sem)
            dve.wait_ge(landed_sem, 16 * len(m.loads))
            pairs = m.lam_rows[:, :].rearrange("p (a b c) -> p a b c", a=2, b=2)
            chain(nc.vector.tensor_tensor(m.lam_prod[:, :, :], pairs[:, :, 0, :], pairs[:, :, 1, :], ALU.mult))
            nc.vector.tensor_reduce(m.lam_sum[:, :], m.lam_prod[:, :, :], AX, ALU.add).then_inc(lam_sem, 1)
            dve.wait_ge(lam_sem, 2)
            chain(nc.vector.tensor_tensor(m.neg_lam[:, :], m.lam_exp[:, 1:2], m.lam_exp[:, 0:1], ALU.subtract))
            chain(nc.vector.tensor_scalar(m.neg_lam[:, :], m.neg_lam[:, :], -LAM_INIT, None, ALU.add))
            chain(nc.vector.tensor_scalar(m.subln[:, :], cols(m, "subln_g"), 1.0 - LAM_INIT, None, ALU.mult))

        @block.scalar
        def _(act):
            act.wait_ge(lam_sem, 1)
            nc.scalar.activation(m.lam_exp[:, :], m.lam_sum[:, :], ACT.Exp).then_inc(lam_sem, 1)


def block_one(nc, m, a):
    with ExitStack() as outer:
        branches = outer.enter_context(ExitStack())
        (m.br_rw,) = buffers(nc, branches, br_rw=[KB, LAT])
        with ExitStack() as c1:
            m.lam_rows, m.lam_prod, m.lam_sum, m.lam_exp = buffers(nc, c1, lam_rows=[4 * HD], lam_prod=[2, HD], lam_sum=[2], lam_exp=[2])
            load_constants(nc, m, a)
        conditions(nc, m)
        modulation(nc, m, a, 0, 0, 16)

        def mods(chunk, j):
            return m.mod[:, 0, 8 * chunk:8 * chunk + 8, j]

        def first_normed():
            g1 = cols(m, "norm1_g")
            with ExitStack() as rows:
                m.x, m.xc = buffers(nc, rows, x=[NTL, D], xc=[NTC, D])
                load(nc, [(m.x, a["x"].rearrange("(t p) d -> p t d", p=P)), (m.xc, a["ctx"].rearrange("(t p) d -> p t d", p=P))])
                normed(nc, m, [(m.xc[:, t, :], t * P, "ctx") for t in range(NTC)] + [(m.x[:, t, :], CTX + t * P, "lat") for t in range(NTL)],
                       m.hT, {"ctx": (g1, mods(1, 1), mods(0, 1)), "lat": (g1, mods(1, 0), mods(0, 0))})

        rwkv_branch(nc, m, a, first_normed)
        (m.brT,) = buffers(nc, branches, brT=[2, KB, LAT])
        with ExitStack() as mix:
            (m.merged,) = buffers(nc, mix, merged=[KD, LAT])
            with ExitStack() as inputs:
                m.hT = two_parts(nc, inputs, KD, TOK)
                first_normed()
                attention_branch(nc, m, a)
                pool_branch(nc, m, a)
                merge(nc, m, a)
            m.x = m.keep.enter_context(nc.sbuf_tensor("x_rows", [P, NTL, D], F32, side="right"))
            load(nc, [(m.x, a["x"].rearrange("(t p) d -> p t d", p=P))])
            gate = gate_rows(nc, m, mix, 0, 2, 1)
            with halves(nc, m.merged) as pair:
                project_add(nc, m, a["w_out"], of_halves(pair), KD, [(t, m.x[:, t, :], gate[:, 0, :]) for t in range(NTL)], split=True, width=256)
        branches.close()
        (m.hT,) = buffers(nc, outer, hT=[KD, TOK])
        normed(nc, m, [(m.x[:, t, :], CTX + t * P, "lat") for t in range(NTL)], m.hT, {"lat": (cols(m, "norm2_g"), mods(4, 0), mods(3, 0))})
        expert_layer(nc, m, a)


def hT_of(m):
    return of_halves(m.hT)


def attention_branch(nc, m, a):
    with ExitStack() as ctx:
        m.v, m.qT, m.kT = buffers(nc, ctx, v=[NT, 512], qT=[HEADS, LAT], kT=[HEADS, TOK])
        with ExitStack() as rows:
            m.q, m.k = buffers(nc, rows, q=[NTL, 512], k=[NT, 512])
            jobs = [(a["w_in"][:, 512 + c:512 + c + 256], 256, [("N", t, 256) for t in range(NTC if c < 512 else 0, NT)])
                    for c in range(0, 3 * 512, 256)]

            def evac(out, j, at, chain):
                dst = (m.q, m.k, m.v)[j // 2][:, at[0] - (NTC if j < 2 else 0), 256 * (j % 2):256 * (j % 2 + 1)]
                return nc.vector.tensor_copy(dst, out)

            products(nc, m, jobs, hT_of(m), evac, "vector", split=True, width=256, side=modulation_tiles(m, a, 0, 16, 48))
            head_norms(nc, m, [(m.q[:].rearrange("p t (n e) -> p (t n) e", e=HD), m.qk_gain[:, 0:HD]),
                               (m.k[:].rearrange("p t (n e) -> p (t n) e", e=HD), m.qk_gain[:, HD:2 * HD])], HD, EPS)
            heads = lambda x, t: x[:, t, :].rearrange("p (n e) -> p n e", e=HD)
            rope(nc, m, [(heads(m.q, t), 8, t) for t in range(NTL)] + [(heads(m.k, NTC + t), 8, t) for t in range(NTL)])
            transposes(nc, m, [([m.q[:, t, h * P:(h + 1) * P] for h in range(4)], m.qT[:, :, t * P:(t + 1) * P], None, None) for t in range(NTL)]
                       + [([m.k[:, t, h * P:(h + 1) * P] for h in range(4)], m.kT[:, :, t * P:(t + 1) * P], None, None) for t in range(NT)])
        (m.att,) = buffers(nc, ctx, att=[NTL, 512])
        items = []
        for t in range(NTL):
            for h in range(HEADS):
                scores = [[(m.qT[q * HD:(q + 1) * HD, h, t * P:(t + 1) * P], m.kT[q * HD:(q + 1) * HD, h, :])] for q in range(2)]
                items.append((scores, lambda k, h=h: m.v[:, k, h * P:(h + 1) * P], m.att[:, t, h * P:(h + 1) * P]))
        attention(nc, m, items, 2, HD ** -0.5, m.neg_lam[:, :])
        head_norms(nc, m, [(m.att[:].rearrange("p t (h e) -> p (t h) e", e=P), None)], P, EPS)
        transposes(nc, m, [([m.att[:, t, h * P:(h + 1) * P] for h in range(4)], m.brT[:, 1, :, t * P:(t + 1) * P], m.subln[:, :], None) for t in range(NTL)])


def pool_branch(nc, m, a):
    with ExitStack() as ctx:
        m.u, m.bands, m.pw, m.diffT = buffers(nc, ctx, u=[NTL, 512], bands=[2, NTL, LAT], pw=[4, P], diffT=[2, LAT])

        def evac(out, j, at, chain):
            return nc.scalar.copy(m.u[:, at[0] - NTC, 256 * j:256 * (j + 1)], out)

        products(nc, m, [(a["w_in"][:, c:c + 256], 256, [("N", NTC + t, 256) for t in range(NTL)]) for c in (0, 256)], hT_of(m), evac, "scalar",
                 split=True, width=256)
        with stage(nc, weights=1, banded=2, diffed=1, copied=1, mapped=1, read=1) as (
                block, weights_sem, banded_sem, diffed_sem, copied_sem, mapped_sem, read_sem):
            @block.sync
            def _(sp):
                sp.dma_start(m.pw[:], a["pool_w"].rearrange("g c d -> c g d")).then_inc(weights_sem, 16)
                for g in range(4):
                    if g >= 2:
                        sp.wait_ge(diffed_sem, g - 1)
                    sp.dma_start(m.bands[:, g % 2], a["bands"][g].rearrange("(k p) t -> p k t", p=P)).then_inc(banded_sem[g % 2], 16)

            @block.tensor
            def _(pe):
                for g in range(4):
                    pe.wait_ge(banded_sem[g % 2], 16 * (g // 2 + 1))
                    if g >= 2:
                        pe.wait_ge(copied_sem, g - 1)
                    for k in range(NTL):
                        mm = nc.tensor.matmul(m.ps[:, g % 2, :], m.u[:, k, g * P:(g + 1) * P], m.bands[:, g % 2, k, :],
                                              start=(k == 0), stop=(k == NTL - 1))
                    mm.then_inc(diffed_sem, 1)
                    pe.wait_ge(copied_sem, g + 1)
                    if g == 0:
                        pe.wait_ge(weights_sem, 16)
                    if g >= 2:
                        pe.wait_ge(read_sem, g - 1)
                    nc.tensor.matmul(m.ps[:, 2 + g % 2, :], m.pw[:, g, :], m.diffT[:, g % 2, :], start=True, stop=True).then_inc(mapped_sem, 1)

            @block.vector
            def _(dve):
                for g in range(4):
                    dve.wait_ge(diffed_sem, g + 1)
                    if g >= 2:
                        dve.wait_ge(mapped_sem, g - 1)
                    nc.vector.tensor_copy(m.diffT[:, g % 2, :], m.ps[:, g % 2, :]).then_inc(copied_sem, 1)
                    dve.wait_ge(mapped_sem, g + 1)
                    nc.vector.tensor_scalar(m.brT[:, 0, g, :], m.ps[:, 2 + g % 2, :], cols(m, "pool_scale")[:, g:g + 1], None,
                                            ALU.mult).then_inc(read_sem, 1)



DECAY_C = float(np.exp(-0.5))
MASKS = ("below16", "rest_below", "above16", "rest_above", "above_eq", "below_eq", "above", "below")


def mask(m, name, n):
    return m.masks[:, MASKS.index(name), :].unsqueeze(1).to_broadcast([P, n, P])


def pad_zeros(nc, m, bufs):
    with stage(nc, done=1) as (block, done_sem):
        @block.vector
        def _(dve):
            for b in bufs:
                for at in (0, CTX + 1, PAD - 1):
                    nc.vector.memset(b[:, at:at + 1], 0.0).then_inc(done_sem, 1)


def taps(dve, chain, pad, seg, w, bias, dst):
    t0, p0, n = SEGS[seg]
    if bias is None:
        chain(dve.tensor_scalar(dst, pad[:, p0 - 1:p0 - 1 + n], w[0], None, ALU.mult))
    else:
        chain(dve.tensor_scalar(dst, pad[:, p0 - 1:p0 - 1 + n], w[0], bias, ALU.mult, ALU.add))
    chain(dve.scalar_tensor_tensor(dst, pad[:, p0:p0 + n], w[1], dst, ALU.mult, ALU.add))
    return dve.scalar_tensor_tensor(dst, pad[:, p0 + 1:p0 + 1 + n], w[2], dst, ALU.mult, ALU.add)


def rwkv_branch(nc, m, a, normed_inputs):
    with ExitStack() as ctx:
        m.rw, m.v_rows, m.y, m.coef, m.knorm = buffers(nc, ctx, rw=[15, TOK], v_rows=[NT, 512], y=[NTL, 512], coef=[LAT], knorm=[TOK])
        with ExitStack() as inputs:
            m.hT = two_parts(nc, inputs, KD, TOK)
            normed_inputs()
            rwkv_inputs(nc, m, a)
        with ExitStack() as run:
            m.w2, m.a2, m.at, m.bt, m.kt, m.rt, m.wc, m.zeros, m.bt_rows, m.kt_rows, m.z, m.u, m.S, m.wmask = buffers(
                nc, run, w2=[512], a2=[512], at=[4, P], bt=[4, P], kt=[4, P], rt=[4, P], wc=[4, 2], zeros=[512], bt_rows=[512], kt_rows=[512], z=[512], u=[512], S=[4, P], wmask=[4, P])
            pairs = [2, 4, P]
            m.D, m.DT, m.N, m.NT, m.AKT, m.RBT, m.RKT = buffers(
                nc, run, D=pairs, DT=pairs, N=pairs, NT=pairs, AKT=pairs, RBT=pairs, RKT=pairs)
            m.D2, m.D2T, m.D4, m.D4T, m.D8, m.ET = buffers(nc, run, D2=pairs, D2T=pairs, D4=pairs, D4T=pairs, D8=pairs, ET=pairs)
            m.filled = nc.alloc_semaphore("rows_filled")
            m.y_dram = nc.dram_tensor("expert_rows", [TAB * SLOTS, D], F32).ap()
            rwkv_start(nc, m, a)
            for d in range(2):
                order = range(NT) if d == 0 else [1, 0, 5, 4, 3, 2]
                for n, t in enumerate(order):
                    rwkv_rows(nc, m, d, t)
                    rwkv_products(nc, m, d, t)
                    rwkv_inverse(nc, m)
                    rwkv_chunks(nc, m, d, t, first=(n == 0), last=(n == NT - 1))
            with nc.Block() as block:
                @block.sync
                def _(sp):
                    sp.wait_ge(m.filled, 16 * FILLS)
        rwkv_result(nc, m, a)


def rwkv_inputs(nc, m, a):
    with ExitStack() as ctx:
        m.pad, m.mid = buffers(nc, ctx, pad=[2, PAD], mid=[15])
        pad_zeros(nc, m, [m.pad[:, 0, :], m.pad[:, 1, :]])
        mu0, mu1 = cols(m, "mu0"), cols(m, "mu1")
        with stage(nc, chain=1) as (block, chain_sem):
            @block.vector
            def _(dve):
                chain = Chain(dve, chain_sem)
                chain(nc.vector.tensor_tensor(m.mid[:, :], mu0, mu1, ALU.add))
                chain(nc.vector.tensor_scalar(m.mid[:, :], m.mid[:, :], -1.0, 1.0, ALU.mult, ALU.add))
        jobs, where = [], []
        for c in range(0, 1920, 256):
            n = min(256, 1920 - c)
            results = []
            for x in range(0, n, P):
                tile = (c + x) // P
                for seg in ((1,) if tile < 4 or tile == 14 else (0, 1)):
                    t0, p0, tn = SEGS[seg]
                    results.append(("T", x, P, t0, tn))
            jobs.append((a["w_in"][:, 2048 + c:2048 + c + n], n, results))

        def evac(out, j, at, chain):
            tile = 2 * j + at[0] // P
            seg = 0 if at[2] == 0 else 1
            t0, p0, tn = SEGS[seg]
            pad = m.pad[:, tile % 2, :]
            chain(nc.vector.tensor_copy(pad[:, p0:p0 + tn], out))
            return taps(nc.vector, chain, pad, seg, (mu0[:, tile:tile + 1], m.mid[:, tile:tile + 1], mu1[:, tile:tile + 1]),
                        None, m.rw[:, tile, t0:t0 + tn])

        products(nc, m, jobs, hT_of(m), evac, "vector", split=True, width=256)
    transposes(nc, m, [([m.rw[:, 8 + p, t * P:(t + 1) * P] for p in range(4)], m.v_rows[:, t, :].rearrange("p (n e) -> p n e", e=P), None, None)
                       for t in range(NT)])
    with ExitStack() as ctx:
        (m.sq,) = buffers(nc, ctx, sq=[4, TOK])
        with stage(nc, squared=1, summed=1, rooted=1, chain=1) as (block, squared_sem, summed_sem, rooted_sem, chain_sem):
            @block.scalar
            def _(act):
                nc.scalar.activation(m.rw[:, 12, :], m.rw[:, 12, :], ACT.Tanh)
                nc.scalar.activation(m.rw[:, 14, CTX:TOK], m.rw[:, 14, CTX:TOK], ACT.Sigmoid)
                act.wait_ge(summed_sem, 1)
                nc.scalar.activation(m.knorm[0:RH, :], m.ps[0:RH, 0:2, :].rearrange("p a b -> p (a b)")[:, 0:TOK], ACT.Sqrt).then_inc(rooted_sem, 1)

            @block.vector
            def _(dve):
                chain = Chain(dve, chain_sem)
                chain(nc.vector.tensor_tensor(m.sq[:, :, :], m.rw[:, 4:8, :], bc(cols(m, "k_k").unsqueeze(2), TOK), ALU.mult))
                nc.vector.tensor_tensor(m.sq[:, :, :], m.sq[:, :, :], m.sq[:, :, :], ALU.mult).then_inc(squared_sem, 1)
                dve.wait_ge(rooted_sem, 1)
                chain(nc.vector.tensor_scalar(m.knorm[0:RH, :], m.knorm[0:RH, :], 1e-12, None, ALU.max))
                chain(nc.vector.reciprocal(m.knorm[0:RH, :], m.knorm[0:RH, :]))

            @block.tensor
            def _(pe):
                pe.wait_ge(squared_sem, 1)
                for c, w in ((0, 512), (512, 256)):
                    for p in range(4):
                        mm = nc.tensor.matmul(m.ps[0:RH, c // 512, 0:w], m.headsum[:, p, :], m.sq[:, p, c:c + w], start=(p == 0), stop=(p == 3))
                mm.then_inc(summed_sem, 1)


def rwkv_start(nc, m, a):
    with stage(nc, landed=1, done=1) as (block, landed_sem, done_sem):
        @block.sync
        def _(sp):
            sp.dma_start(m.w2[:, :], a["decay_w2"].rearrange("d r c -> (d r) c")).then_inc(landed_sem, 16)
            sp.dma_start(m.a2[:, :], a["aaa_a2"].rearrange("d r c -> (d r) c")).then_inc(landed_sem, 16)
            sp.wait_ge(landed_sem, 32)
            sp.wait_ge(done_sem, 1)
            fill_rows(nc, m, m.zeros[:, :])

        @block.vector
        def _(dve):
            nc.vector.memset(m.zeros[:, :], 0.0).then_inc(done_sem, 1)
            nc.vector.memset(m.z[:, :], 0.0).then_inc(done_sem, 1)
            nc.vector.memset(m.u[:, :], 0.0).then_inc(done_sem, 1)


def rwkv_rows(nc, m, d, t):
    t0 = t * P
    lat = t >= NTC
    r, k = m.rw[:, 0:4, t0:t0 + P], m.rw[:, 4:8, t0:t0 + P]
    rows = slice(HD * d, HD * (d + 1))
    with ExitStack() as ctx:
        b = Memory()
        b.sg, b.aa, b.cs, b.kk, b.km, b.e_up, b.e_dn, b.e_pr, b.cf = [
            x[:, i] for x in (m.D2, m.D2T, m.D4, m.D4T, m.D8) for i in range(2)][0:9]
        col = lambda name, o=0: bc(cols(m, name)[:, o:o + 4].unsqueeze(2), P)
        with stage(nc, made=1, gated=1, run=1, exps=1, coefs=1, summed=1, chain=1) as (
                block, made_sem, gated_sem, run_sem, exps_sem, coefs_sem, summed_sem, chain_sem):
            @block.tensor
            def _(pe):
                for w, x, bank in ((m.w2, 12, 0), (m.a2, 13, 1)):
                    for p in range(4):
                        nc.tensor.matmul(m.ps[:, bank, p * P:(p + 1) * P], w[rows, p * P:(p + 1) * P], m.rw[rows, x, t0:t0 + P], start=True, stop=True)
                for p in range(4):
                    mm = nc.tensor.matmul(m.ps[:, 2, p * P:(p + 1) * P], m.headspread[0:RH, p, :], m.knorm[0:RH, t0:t0 + P], start=True, stop=True)
                mm.then_inc(made_sem, 1)
                if lat:
                    pe.wait_ge(coefs_sem, 1)
                    for p in range(4):
                        mm = nc.tensor.matmul(m.ps[0:RH, 3, 0:P], m.headsum[:, p, :], b.cf[:, p, :], start=(p == 0), stop=(p == 3))
                    mm.then_inc(summed_sem, 1)

            @block.scalar
            def _(act):
                act.wait_ge(made_sem, 1)
                for name, dst, bank in (("w0", b.sg, 0), ("a0", b.aa, 1)):
                    for p in range(4):
                        nc.scalar.activation(dst[:, p, :], m.ps[:, bank, p * P:(p + 1) * P], ACT.Sigmoid,
                                             bias=cols(m, name)[:, 4 * d + p:4 * d + p + 1]).then_inc(gated_sem, 1)
                act.wait_ge(run_sem, 2)
                nc.scalar.activation(b.e_up[:, :, :], b.cs[:, :, :], ACT.Exp, scale=DECAY_C).then_inc(exps_sem, 1)
                nc.scalar.activation(b.e_dn[:, :, :], b.cs[:, :, :], ACT.Exp, scale=-DECAY_C).then_inc(exps_sem, 1)
                nc.scalar.activation(b.e_pr[:, :, :], b.sg[:, :, :], ACT.Exp, scale=-DECAY_C).then_inc(exps_sem, 1)

            @block.vector
            def _(dve):
                chain = Chain(dve, chain_sem)
                chain(nc.vector.tensor_tensor(b.kk[:, :, :], k, col("k_k"), ALU.mult))
                dve.wait_ge(made_sem, 1)
                chain(nc.vector.tensor_tensor(b.kk[:, :, :], b.kk[:, :, :], m.ps[:, 2, :].rearrange("p (n e) -> p n e", e=P), ALU.mult))
                dve.wait_ge(gated_sem, 8)
                flat = lambda x: x[:, :, :].rearrange("p n e -> p (n e)")
                sg, cs = flat(b.sg), flat(b.cs)
                restart = m.restart[:, d, :]
                if d:
                    sg, cs, restart = sg[:, ::-1], cs[:, ::-1], restart[:, ::-1]
                nc.vector.tensor_tensor_scan(cs, restart, sg, 0.0, ALU.mult, ALU.add).then_inc(run_sem, 1)
                dve.wait_ge(run_sem, 1)
                nc.vector.tensor_tensor(b.sg[:, :, :], b.cs[:, :, :], b.sg[:, :, :], ALU.subtract).then_inc(run_sem, 1)
                chain(nc.vector.scalar_tensor_tensor(b.km[:, :, :], b.aa[:, :, :], 1.0, col("k_a"), ALU.subtract, ALU.mult))
                chain(nc.vector.scalar_tensor_tensor(b.km[:, :, :], b.km[:, :, :], 1.0, k, ALU.add, ALU.mult))
                chain(nc.vector.tensor_tensor(b.aa[:, :, :], b.aa[:, :, :], b.kk[:, :, :], ALU.mult))
                if lat:
                    chain(nc.vector.tensor_tensor(b.cf[:, :, :], b.km[:, :, :], r, ALU.mult))
                    nc.vector.tensor_tensor(b.cf[:, :, :], b.cf[:, :, :], col("r_k"), ALU.mult).then_inc(coefs_sem, 1)
                dve.wait_ge(exps_sem, 3)
                chain(nc.vector.tensor_tensor(m.bt[:, :, :], b.aa[:, :, :], b.e_up[:, :, :], ALU.mult))
                chain(nc.vector.tensor_tensor(m.kt[:, :, :], b.km[:, :, :], b.e_up[:, :, :], ALU.mult))
                chain(nc.vector.scalar_tensor_tensor(m.at[:, :, :], b.kk[:, :, :], -1.0, b.e_pr[:, :, :], ALU.mult, ALU.mult))
                end = 0 if d else CH - 1
                chain(nc.vector.tensor_copy(m.wc[:, :, :], b.e_dn[:, :, :].rearrange("p n (c e) -> p n c e", e=CH)[:, :, :, end]))
                if lat:
                    chain(nc.vector.tensor_tensor(m.rt[:, :, :], r, b.e_dn[:, :, :], ALU.mult))
                    dve.wait_ge(summed_sem, 1)
                    c = m.coef[0:RH, t0 - CTX:t0 - CTX + P]
                    if d == 0:
                        chain(nc.vector.tensor_copy(c, m.ps[0:RH, 3, 0:P]))
                    else:
                        chain(nc.vector.tensor_tensor(c, c, m.ps[0:RH, 3, 0:P], ALU.add))


def rwkv_products(nc, m, d, t):
    lat = t >= NTC
    lo, up = ("below", "above") if d == 0 else ("above", "below")
    kinds = [(m.at, m.bt, [(m.D, lo + "16"), (m.N, "rest_" + lo)]), (m.bt, m.at, [(m.DT, up + "16"), (m.NT, "rest_" + up)]),
             (m.kt, m.at, [(m.AKT, up)])]
    if lat:
        kinds += [(m.bt, m.rt, [(m.RBT, up + "_eq")]), (m.kt, m.rt, [(m.RKT, up + "_eq")])]
    with stage(nc, turned=1, made=1, read=1, chain=1) as (block, turned_sem, made_sem, read_sem, chain_sem):
        @block.tensor
        def _(pe):
            for i, (lhs, rhs, outs) in enumerate(kinds):
                for hh in range(2):
                    q = 2 * i + hh
                    if q >= 6:
                        pe.wait_ge(read_sem, q - 5)
                    h = slice(HD * hh, HD * (hh + 1))
                    for p in range(4):
                        mm = nc.tensor.matmul(m.ps[:, 2 + q % 6, p * P:(p + 1) * P], lhs[h, p, :], rhs[h, p, :], start=True, stop=True)
                    mm.then_inc(made_sem, 1)
                if i == 1:
                    for bank, x in ((0, m.bt), (1, m.kt)):
                        for p in range(4):
                            mm = nc.tensor.transpose(m.ps[:, bank, p * P:(p + 1) * P], x[:, p, :], m.ident)
                        mm.then_inc(turned_sem, 1)

        @block.scalar
        def _(act):
            for i, dst in enumerate((m.bt_rows, m.kt_rows)):
                act.wait_ge(turned_sem, i + 1)
                nc.scalar.copy(dst[:, :], m.ps[:, i, :])

        @block.vector
        def _(dve):
            for i, (lhs, rhs, outs) in enumerate(kinds):
                for hh in range(2):
                    q = 2 * i + hh
                    dve.wait_ge(made_sem, q + 1)
                    src = m.ps[:, 2 + q % 6, :].rearrange("p (n e) -> p n e", e=P)
                    for dst, name in outs:
                        last = nc.vector.tensor_tensor(dst[:, hh, :, :], src, mask(m, name, 4), ALU.mult)
                    last.then_inc(read_sem, 1)


def rwkv_inverse(nc, m):
    copies = (2, 2, 1, 0, 1, 2, 1, 0, 0)
    adds = (0, 1, 1, 1, 0, 0, 0, 1, 1)
    with stage(nc, ready=1, made=2, copied=2, added=2) as (block, ready_sem, made_sem, copied_sem, added_sem):
        def rounds(hh):
            x = lambda b: b[:, hh]
            D, DT, N, NT, D2, D2T, D4, D4T, D8, ET = (x(b) for b in (m.D, m.DT, m.N, m.NT, m.D2, m.D2T, m.D4, m.D4T, m.D8, m.ET))
            E, M, MT, M2, Y = D8, D2, D2T, D4, D4T
            return [([(DT, D, D2), (D, DT, D2T)], []),
                    ([(D2T, D2, D4), (D2, D2T, D4T)], [(D2, ET, ET, ET)]),
                    ([(D4T, D4, D8)], [(D4, ET, ET, ET)]),
                    ([], [(D8, ET, ET, ET)]),
                    ([(ET, None, E)], []),
                    ([(NT, E, M), (E, NT, MT)], []),
                    ([(MT, M, M2)], []),
                    ([], [(M2, ET, ET, Y)]),
                    ([], [(M, Y, Y, D)])]

        @block.tensor
        def _(pe):
            for r in range(9):
                for hh in range(2):
                    copy, add = rounds(hh)[r]
                    if r == 1:
                        pe.wait_ge(ready_sem, hh + 1)
                    if sum(copies[:r]):
                        pe.wait_ge(copied_sem[hh], sum(copies[:r]))
                    if sum(adds[:r]):
                        pe.wait_ge(added_sem[hh], sum(adds[:r]))
                    for q, (lhsT, rhs, *_) in enumerate(copy + add):
                        for p in range(4):
                            mm = nc.tensor.matmul(m.ps[:, 4 * hh + q, p * P:(p + 1) * P], lhsT[:, p, :],
                                                  m.ident if rhs is None else rhs[:, p, :], start=True, stop=True)
                    mm.then_inc(made_sem[hh], 1)

        @block.scalar
        def _(act):
            for r in range(9):
                for hh in range(2):
                    copy, add = rounds(hh)[r]
                    if copy:
                        act.wait_ge(made_sem[hh], r + 1)
                    for q, (lhsT, rhs, dst) in enumerate(copy):
                        nc.scalar.copy(dst, m.ps[:, 4 * hh + q, :].rearrange("p (n e) -> p n e", e=P)).then_inc(copied_sem[hh], 1)

        @block.vector
        def _(dve):
            for hh in range(2):
                nc.vector.tensor_tensor(m.ET[:, hh], m.DT[:, hh], m.ident.unsqueeze(1).to_broadcast([P, 4, P]), ALU.add).then_inc(ready_sem, 1)
            for r in range(9):
                for hh in range(2):
                    copy, add = rounds(hh)[r]
                    if add:
                        dve.wait_ge(made_sem[hh], r + 1)
                        if sum(adds[:r]):
                            dve.wait_ge(added_sem[hh], sum(adds[:r]))
                        else:
                            dve.wait_ge(ready_sem, hh + 1)
                    for q, (lhsT, rhs, addend, dst) in enumerate(add):
                        nc.vector.tensor_tensor(dst, m.ps[:, 4 * hh + len(copy) + q, :].rearrange("p (n e) -> p n e", e=P), addend,
                                                ALU.add).then_inc(added_sem[hh], 1)


def rwkv_chunks(nc, m, d, t, first, last):
    lat = t >= NTC
    chunks = (0, 1) if d == 0 else (1, 0)
    with stage(nc, cleared=1, z_made=1, z_read=1, u_made=1, u_read=1, y_made=1, y_read=1, s_made=1, s_new=1, chain=1) as (
            block, cleared_sem, z_made_sem, z_read_sem, u_made_sem, u_read_sem, y_made_sem, y_read_sem, s_made_sem, s_new_sem, chain_sem):
        @block.tensor
        def _(pe):
            if first:
                pe.wait_ge(cleared_sem, 1)
            halves_of = [(p, hh, slice(p * P + hh * HD, p * P + (hh + 1) * HD)) for p in range(4) for hh in range(2)]
            for i, c in enumerate(chunks):
                R = slice(CH * c, CH * (c + 1))
                if i:
                    pe.wait_ge(z_read_sem, i)
                for p, hh, h in halves_of:
                    nc.tensor.matmul(m.ps[R, 0, h], m.AKT[:, hh, p, R], m.v_rows[:, t, h], start=(p + hh == 0), stop=False)
                if i:
                    pe.wait_ge(s_new_sem, i)
                for p in range(4):
                    mm = nc.tensor.matmul(m.ps[R, 0, p * P:(p + 1) * P], m.at[:, p, R], m.S[:, p, :], start=False, stop=(p == 3))
                mm.then_inc(z_made_sem, 1)
                for p in range(4):
                    w = slice(p * P, (p + 1) * P)
                    nc.tensor.matmul(m.ps[:, 3, w], m.kt_rows[R, w], m.v_rows[R, t, w], start=(p == 0), stop=False)
                pe.wait_ge(z_read_sem, i + 1)
                for p, hh, h in halves_of:
                    mm = nc.tensor.matmul(m.ps[R, 1, h], m.D[:, hh, p, R], m.z[:, h], start=True, stop=True)
                mm.then_inc(u_made_sem, 1)
                if lat:
                    if i:
                        pe.wait_ge(y_read_sem, i)
                    for p in range(4):
                        nc.tensor.matmul(m.ps[R, 2, p * P:(p + 1) * P], m.rt[:, p, R], m.S[:, p, :], start=(p == 0), stop=False)
                    for p, hh, h in halves_of:
                        nc.tensor.matmul(m.ps[R, 2, h], m.RKT[:, hh, p, R], m.v_rows[:, t, h], start=False, stop=False)
                pe.wait_ge(u_read_sem, i + 1)
                for p in range(4):
                    w = slice(p * P, (p + 1) * P)
                    mm = nc.tensor.matmul(m.ps[:, 3, w], m.bt_rows[R, w], m.u[R, w], start=False, stop=(p == 3))
                mm.then_inc(s_made_sem, 1)
                if lat:
                    for p, hh, h in halves_of:
                        mm = nc.tensor.matmul(m.ps[R, 2, h], m.RBT[:, hh, p, R], m.u[:, h], start=False, stop=(p + hh == 4))
                    mm.then_inc(y_made_sem, 1)

        @block.scalar
        def _(act):
            for i, c in enumerate(chunks):
                R = slice(CH * c, CH * (c + 1))
                act.wait_ge(z_made_sem, i + 1)
                nc.scalar.copy(m.z[R, :], m.ps[R, 0, :]).then_inc(z_read_sem, 1)
                act.wait_ge(u_made_sem, i + 1)
                nc.scalar.copy(m.u[R, :], m.ps[R, 1, :]).then_inc(u_read_sem, 1)

        @block.vector
        def _(dve):
            chain = Chain(dve, chain_sem)
            if first:
                nc.vector.memset(m.S[:, :, :], 0.0).then_inc(cleared_sem, 1)
                dve.wait_ge(cleared_sem, 1)
            for i, c in enumerate(chunks):
                R = slice(CH * c, CH * (c + 1))
                chain(nc.vector.tensor_tensor(m.wmask[:, :, :], m.head_mask.unsqueeze(1).to_broadcast([P, 4, P]), bc(m.wc[:, :, c:c + 1], P), ALU.mult))
                dve.wait_ge(s_made_sem, i + 1)
                chain(nc.vector.tensor_tensor(m.S[:, :, :], m.S[:, :, :], m.ps[:, 3, :].rearrange("p (n e) -> p n e", e=P), ALU.add))
                nc.vector.tensor_tensor(m.S[:, :, :], m.S[:, :, :], m.wmask[:, :, :], ALU.mult).then_inc(s_new_sem, 1)
                dve.wait_ge(s_new_sem, i + 1)
                if lat:
                    dve.wait_ge(y_made_sem, i + 1)
                    y = m.y[R, t - NTC, :]
                    if d == 0:
                        nc.vector.tensor_copy(y, m.ps[R, 2, :]).then_inc(y_read_sem, 1)
                    else:
                        nc.vector.tensor_tensor(y, y, m.ps[R, 2, :], ALU.add).then_inc(y_read_sem, 1)


def rwkv_result(nc, m, a):
    with ExitStack() as ctx:
        b = Memory()
        b.mean, b.ss, b.root, b.rstd, b.sq, b.g2, b.t = buffers(
            nc, ctx, mean=[NTL * RH, 1], ss=[NTL * RH], root=[NTL * RH], rstd=[NTL * RH, 1], sq=[NTL * RH, HD], g2=[512], t=[KB, LAT])
        y = m.y[:].rearrange("p t (h e) -> p (t h) e", e=HD)
        n = NTL * RH
        with stage(nc, landed=1, summed=1, rooted=1, chain=1) as (block, landed_sem, summed_sem, rooted_sem, chain_sem):
            @block.sync
            def _(sp):
                sp.dma_start(b.g2[:, :], a["gate_w2"]).then_inc(landed_sem, 16)
                sp.wait_ge(landed_sem, 16)

            @block.scalar
            def _(act):
                act.wait_ge(summed_sem, 1)
                nc.scalar.activation(b.root[:, :], b.ss[:, :], ACT.Sqrt).then_inc(rooted_sem, 1)

            @block.vector
            def _(dve):
                chain = Chain(dve, chain_sem)
                chain(nc.vector.tensor_reduce(b.mean[:, :, 0], y, AX, ALU.add))
                chain(nc.vector.tensor_scalar(b.mean[:, :, 0], b.mean[:, :, 0], 1.0 / HD, None, ALU.mult))
                chain(nc.vector.tensor_tensor(y, y, bc(b.mean[:, :, :], HD), ALU.subtract))
                chain(nc.vector.tensor_tensor(b.sq[:, :, :], y, y, ALU.mult))
                chain(nc.vector.tensor_reduce(b.ss[:, :], b.sq[:, :, :], AX, ALU.add))
                nc.vector.tensor_scalar(b.ss[:, :], b.ss[:, :], 1.0 / HD, GN_EPS, ALU.mult, ALU.add).then_inc(summed_sem, 1)
                dve.wait_ge(rooted_sem, 1)
                chain(nc.vector.reciprocal(b.rstd[:, :, 0], b.root[:, :]))
                chain(nc.vector.tensor_tensor(y, y, bc(b.rstd[:, :, :], HD), ALU.mult))
        gw, gb = cols(m, "gn_w"), cols(m, "gn_b")
        transposes(nc, m, [([m.y[:, t, h * P:(h + 1) * P]], m.br_rw[:, h:h + 1, t * P:(t + 1) * P], gw[:, h:h + 1], gb[:, h:h + 1])
                           for t in range(NTL) for h in range(KB)])
        with stage(nc, made=1, chain=1) as (block, made_sem, chain_sem):
            @block.tensor
            def _(pe):
                for p in range(KB):
                    nc.tensor.matmul(m.ps[:, p, :], b.g2[:, p * P:(p + 1) * P], m.rw[:, 14, CTX:TOK], start=True, stop=True)
                    nc.tensor.matmul(m.ps[:, 4 + p, :], m.headspread[0:RH, p, :], m.coef[0:RH, :], start=True, stop=True).then_inc(made_sem, 1)

            @block.vector
            def _(dve):
                chain = Chain(dve, chain_sem)
                for p in range(KB):
                    dve.wait_ge(made_sem, p + 1)
                    chain(nc.vector.tensor_tensor(b.t[:, p, :], m.ps[:, 4 + p, :], m.rw[:, 8 + p, CTX:TOK], ALU.mult))
                    chain(nc.vector.tensor_tensor(b.t[:, p, :], b.t[:, p, :], m.br_rw[:, p, :], ALU.add))
                    chain(nc.vector.tensor_tensor(m.br_rw[:, p, :], b.t[:, p, :], m.ps[:, p, :], ALU.mult))



I32 = mybir.dt.int32
U32 = mybir.dt.uint32
SLOTS = 128
TAB = 2 * LAT // SLOTS + N_EXP
FILLS = TAB


def merge(nc, m, a):
    with ExitStack() as ctx:
        (m.gates,) = buffers(nc, ctx, gates=[3, KD, LAT])
        jobs = [(a["w_in"][:, 3968 + c:3968 + c + 256], 256, [("T", x, P, CTX, LAT) for x in (0, P)]) for c in range(0, 3 * D, 256)]
        products(nc, m, jobs, hT_of(m), lambda out, j, at, chain: nc.scalar.activation(
            m.gates[:, j // 4, 2 * (j % 4) + at[0] // P, :], out, ACT.Sigmoid), "scalar", split=True, width=256)
        jobs = [(a["w_br"][j // 4][:, (j % 4) * 256:(j % 4 + 1) * 256], 256, [("T", x, P, 0, LAT) for x in (0, P)]) for j in range(12)]

        def evac(out, j, at, chain):
            tile = 2 * (j % 4) + at[0] // P
            gate, sum_ = m.gates[:, j // 4, tile, :], m.merged[:, tile, :]
            if j < 4:
                return nc.vector.tensor_tensor(sum_, out, gate, ALU.mult)
            chain(nc.vector.tensor_tensor(gate, out, gate, ALU.mult))
            return nc.vector.tensor_tensor(sum_, sum_, gate, ALU.add)

        branch = (m.brT[:, 0], m.brT[:, 1], m.br_rw)
        products(nc, m, jobs, lambda k, t0, tn, j: branch[j // 4][:, k, t0:t0 + tn], evac, "vector", kt=KB, width=256, side=modulation_tiles(m, a, 1, 0, 16))


def project_add(nc, m, w, xT, kt, tiles, wslots=3, width=512, split=False, banks=4, k_chunks=1):
    jobs = [(w[:, c:c + width], width, [("N", t, width) for t, _, _ in tiles]) for c in range(0, D, width)]
    by_tile = {t: (x, g) for t, x, g in tiles}
    with ExitStack() as ctx:
        b = Memory()
        (b.t,) = buffers(nc, ctx, t=[2, width])
        turn = [0]

        def evac(out, j, at, chain):
            x, g = by_tile[at[0]]
            c = slice(width * j, width * (j + 1))
            turn[0] ^= 1
            chain(nc.vector.tensor_tensor(b.t[:, turn[0], 0:width], out, g[:, c], ALU.mult))
            return nc.vector.tensor_tensor(x[:, c], x[:, c], b.t[:, turn[0], 0:width], ALU.add)

        products(nc, m, jobs, xT, evac, "vector", kt=kt, wslots=wslots, width=width, split=split, banks=banks, k_chunks=k_chunks)


def first_highest(nc, chain, values, top, found, iota, work, hot):
    tiles, n = values.shape[1], values.shape[2]
    chain(nc.vector.tensor_reduce(top, values, AX, ALU.max))
    chain(nc.vector.tensor_tensor(hot, values, bc(top.unsqueeze(2), n), ALU.is_equal))
    chain(nc.vector.scalar_tensor_tensor(work, hot, -float(n), iota, ALU.mult, ALU.add))
    chain(nc.vector.tensor_reduce(found, work, AX, ALU.min))
    chain(nc.vector.tensor_tensor(hot, work, bc(found.unsqueeze(2), n), ALU.is_equal))


def route(nc, m, a):
    T = NTL
    with ExitStack() as ctx:
        b = Memory()
        (b.w, b.iota, b.tri, b.ones, b.tok_id, b.lg, b.le, b.top, b.found, b.work4, b.group, b.e4, b.p,
         b.work, b.hot1, b.hot2, b.m1, b.m2, b.e2, b.den, b.mask, b.where, b.count, b.blocks, b.more, b.end,
         b.one, b.bid, b.cmp, b.exp, b.slot, b.nb) = buffers(
            nc, ctx, w=[KD, N_GRP + N_EXP], iota=[1, N_EXP], tri=[P], ones=[P], tok_id=[T], lg=[T, N_GRP], le=[T, N_EXP], top=[T], found=[T], work4=[T, N_GRP], group=[T, N_GRP], e4=[T, N_GRP], p=[T], work=[T, N_EXP], hot1=[T, N_EXP], hot2=[T, N_EXP], m1=[T], m2=[T], e2=[T], den=[T], mask=[T, N_EXP], where=[T, N_EXP], count=[N_EXP], blocks=[N_EXP], more=[N_EXP], end=[N_EXP], one=[N_EXP], bid=[TAB], cmp=[TAB, N_EXP], exp=[TAB], slot=[2, T], nb=[1])
        tok_i = ctx.enter_context(nc.sbuf_tensor(f"tok_i_{nc.next_id()}", [P, T], U32))
        zero_i = ctx.enter_context(nc.sbuf_tensor(f"zero_i_{nc.next_id()}", [P, TAB + 1], U32))
        with stage(nc, landed=1, logits=1, expd=1, masked=1, ranked=1, table=1, cleared=1, scattered=1, chain=1, zeroed=1) as (
                block, landed_sem, logits_sem, expd_sem, masked_sem, ranked_sem, table_sem, cleared_sem, scattered_sem, chain_sem, zeroed_sem):
            @block.sync
            def _(sp):
                for dst, src in ((b.w[:, :, :], a["w_router"].rearrange("(k p) n -> p k n", p=P)), (b.iota[:, :, :], a["iota32"]),
                                 (b.tri[:, :], a["tri"]), (b.tok_id[:, :], a["tok_id"]), (b.bid[:, :], a["block_id"])):
                    sp.dma_start(dst, src).then_inc(landed_sem, 16)
                sp.wait_ge(zeroed_sem, 1)
                sp.dma_start(m.table_dram.rearrange("(p b) o -> p (b o)", p=P), zero_i[:, :]).then_inc(cleared_sem, 16)
                sp.wait_ge(scattered_sem, 16 * 2 * T)
                with nc.allow_non_contiguous_dma(reason="a small table turned over"):
                    sp.dma_start(m.token_of[:, :], m.table_dram.rearrange("(b p) o -> p (b o)", p=P)).then_inc(cleared_sem, 16)
                sp.wait_ge(cleared_sem, 32)

            @block.tensor
            def _(pe):
                pe.wait_ge(landed_sem, 80)
                for t in range(T):
                    for k in range(KD):
                        mm = nc.tensor.matmul(m.ps[:, 0, t * 64:t * 64 + N_GRP + N_EXP], m.hT[:, k, CTX + t * P:CTX + (t + 1) * P],
                                              b.w[:, k, :], start=(k == 0), stop=(k == KD - 1))
                mm.then_inc(logits_sem, 1)
                pe.wait_ge(masked_sem, 1)
                for t in range(T):
                    out = m.ps[:, 1, t * N_EXP:(t + 1) * N_EXP]
                    for q in range(t):
                        nc.tensor.matmul(out, b.ones[:, :], b.mask[:, q, :], start=(q == 0), stop=False)
                    nc.tensor.matmul(out, b.tri[:, :], b.mask[:, t, :], start=(t == 0), stop=True)
                for q in range(T):
                    mm = nc.tensor.matmul(m.ps[:, 2, 0:N_EXP], b.ones[:, :], b.mask[:, q, :], start=(q == 0), stop=(q == T - 1))
                mm.then_inc(ranked_sem, 1)

            @block.scalar
            def _(act):
                act.wait_ge(table_sem, 1)
                nc.scalar.activation(b.e4[:, :, :], b.e4[:, :, :], ACT.Exp).then_inc(expd_sem, 1)
                act.wait_ge(table_sem, 2)
                nc.scalar.activation(b.e2[:, :], b.e2[:, :], ACT.Exp).then_inc(expd_sem, 1)

            @block.vector
            def _(dve):
                chain = Chain(dve, chain_sem)
                v = nc.vector
                v.memset(zero_i[:, :], 0).then_inc(zeroed_sem, 1)
                chain(v.memset(b.ones[:, :], 1.0))
                chain(v.memset(b.one[:, :], 1.0))
                dve.wait_ge(landed_sem, 80)
                dve.wait_ge(logits_sem, 1)
                L = m.ps[:, 0, 0:T * 64].rearrange("p (t e) -> p t e", e=64)
                chain(v.tensor_copy(b.lg[:, :, :], L[:, :, 0:N_GRP]))
                chain(v.tensor_copy(b.le[:, :, :], L[:, :, N_GRP:N_GRP + N_EXP]))
                first_highest(nc, chain, b.lg[:, :, :], b.top[:, :], b.found[:, :], b.iota[:, :, 0:N_GRP].to_broadcast([P, T, N_GRP]), b.work4[:, :, :], b.group[:, :, :])
                v.tensor_tensor(b.e4[:, :, :], b.lg[:, :, :], bc(b.top[:, :].unsqueeze(2), N_GRP), ALU.subtract).then_inc(table_sem, 1)
                chain(v.tensor_scalar(b.work4[:, :, :], b.group[:, :, :], 1.0, BIG, ALU.subtract, ALU.mult))
                le = b.le[:, :, :].rearrange("p t (g e) -> p t g e", g=N_GRP)
                chain(v.tensor_tensor(le, le, b.work4[:, :, :].unsqueeze(3).to_broadcast([P, T, N_GRP, N_EXP // N_GRP]), ALU.add))
                iota = b.iota[:, :, :].to_broadcast([P, T, N_EXP])
                first_highest(nc, chain, b.le[:, :, :], b.m1[:, :], b.found[:, :], iota, b.work[:, :, :], b.hot1[:, :, :])
                chain(v.scalar_tensor_tensor(b.le[:, :, :], b.hot1[:, :, :], -BIG, b.le[:, :, :], ALU.mult, ALU.add))
                first_highest(nc, chain, b.le[:, :, :], b.m2[:, :], b.found[:, :], iota, b.work[:, :, :], b.hot2[:, :, :])
                chain(v.tensor_tensor(b.mask[:, :, :], b.hot1[:, :, :], b.hot2[:, :, :], ALU.add))
                v.sem_inc(masked_sem, 1)
                v.tensor_tensor(b.e2[:, :], b.m2[:, :], b.m1[:, :], ALU.subtract).then_inc(table_sem, 1)
                dve.wait_ge(expd_sem, 2)
                chain(v.tensor_reduce(b.p[:, :], b.e4[:, :, :], AX, ALU.add))
                chain(v.tensor_scalar(b.den[:, :], b.e2[:, :], 1.0, None, ALU.add))
                chain(v.tensor_tensor(b.den[:, :], b.den[:, :], b.p[:, :], ALU.mult))
                chain(v.reciprocal(m.gate_of[:, 0, :], b.den[:, :]))
                chain(v.tensor_tensor(m.gate_of[:, 1, :], m.gate_of[:, 0, :], b.e2[:, :], ALU.mult))
                dve.wait_ge(ranked_sem, 1)
                chain(v.tensor_copy(b.count[:, :], m.ps[:, 2, 0:N_EXP]))
                chain(v.tensor_scalar(b.blocks[:, :], b.count[:, :], 0.5, None, ALU.is_gt))
                for n in range(SLOTS, LAT, SLOTS):
                    chain(v.tensor_scalar(b.more[:, :], b.count[:, :], n + 0.5, None, ALU.is_gt))
                    chain(v.tensor_tensor(b.blocks[:, :], b.blocks[:, :], b.more[:, :], ALU.add))
                chain(v.tensor_tensor_scan(b.end[:, :], b.one[:, :], b.blocks[:, :], 0.0, ALU.mult, ALU.add))
                chain(v.tensor_scalar(b.nb[:, :], b.end[:, N_EXP - 1:N_EXP], 0.5, 0.25, ALU.mult, ALU.add))
                chain(v.tensor_copy(m.n_pairs[:, :], b.nb[:, :]))
                chain(v.tensor_tensor(b.cmp[:, :, :], b.end[:, :].unsqueeze(1).to_broadcast([P, TAB, N_EXP]), bc(b.bid[:, :].unsqueeze(2), N_EXP), ALU.is_le))
                chain(v.tensor_reduce(b.exp[:, :], b.cmp[:, :, :], AX, ALU.add))
                chain(v.tensor_scalar(b.exp[:, :], b.exp[:, :], float(N_EXP - 1), None, ALU.min))
                chain(v.tensor_copy(m.expert_of[:, :], b.exp[:, :]))
                chain(v.tensor_tensor(b.end[:, :], b.end[:, :], b.blocks[:, :], ALU.subtract))
                chain(v.scalar_tensor_tensor(b.where[:, :, :], b.end[:, :].unsqueeze(1).to_broadcast([P, T, N_EXP]), float(SLOTS),
                                             m.ps[:, 1, 0:T * N_EXP].rearrange("p (t e) -> p t e", e=N_EXP), ALU.mult, ALU.add))
                for j, hot in enumerate((b.hot1, b.hot2)):
                    chain(v.tensor_tensor(b.work[:, :, :], hot[:, :, :], b.where[:, :, :], ALU.mult))
                    chain(v.tensor_reduce(b.slot[:, j, :], b.work[:, :, :], AX, ALU.add))
                    chain(v.tensor_copy(m.place_of[:, j, :], b.slot[:, j, :]))
                v.tensor_copy(tok_i[:, :], b.tok_id[:, :]).then_inc(table_sem, 1)

            @block.gpsimd
            def _(pool):
                pool.wait_ge(table_sem, 3)
                pool.wait_ge(cleared_sem, 16)
                for j in range(2):
                    for t in range(T):
                        nc.gpsimd.indirect_dma_start(m.table_dram, bass.IndirectOffsetOnAxis(ap=m.place_of[:, j, t:t + 1], axis=0),
                                                     tok_i[:, t:t + 1], None).then_inc(scattered_sem, 16)
                pool.wait_ge(scattered_sem, 16 * 2 * T)


def experts(nc, m, a):
    with ExitStack() as ctx:
        b = Memory()
        b.xg0, b.xg1, b.xT, b.wg0, b.wg1, b.wu0, b.wu1, b.wd0, b.wd1, b.sg, b.h, b.hT, b.y0, b.y1 = buffers(
            nc, ctx, xg0=[D], xg1=[D], xT=[KD, P], wg0=[KD, EFF], wg1=[KD, EFF], wu0=[KD, EFF], wu1=[KD, EFF], wd0=[4, D], wd1=[4, D], sg=[EFF], h=[EFF], hT=[4, P], y0=[D], y1=[D])
        xg, wg, wu, wd, y = (b.xg0, b.xg1), (b.wg0, b.wg1), (b.wu0, b.wu1), (b.wd0, b.wd1), (b.y0, b.y1)
        idx = [ctx.enter_context(nc.sbuf_tensor(f"idx{u}_{nc.next_id()}", [P, 1], U32)) for u in range(2)]
        n_pairs_max = TAB // 2
        with stage(nc, x_in=2, g_in=2, u_in=2, d_in=2, idx_new=1, turned=1, x_copied=1, g_made=1, u_made=1, silu=1, h_new=1, h_turned=1,
                   h_copied=1, y_made=1, y_read=1, stored=2, chain=1, credit=1) as (
                block, x_in_sem, g_in_sem, u_in_sem, d_in_sem, idx_new_sem, turned_sem, x_copied_sem, g_made_sem, u_made_sem, silu_sem, h_new_sem, h_turned_sem, h_copied_sem, y_made_sem, y_read_sem, stored_sem, chain_sem, credit_sem):
            def pairs(eng):
                return eng.value_load(m.n_pairs[0:1, 0:1], min_val=1, max_val=n_pairs_max)

            @block.sync
            def _(sp):
                with sp.Fori(0, pairs(sp)) as it:
                    for u in range(2):
                        e = sp.value_load(m.expert_of[0:1, bass.ds(2 * it + u, 1)], min_val=0, max_val=N_EXP - 1)
                        sp.wait_ge(g_made_sem, 2 * it + u + 1)
                        sp.dma_start(wg[u][:, :, :], a["w_exp_gate"][bass.ds(e, 1)].rearrange("o (k p) n -> p (o k) n", p=P)).then_inc(g_in_sem[u], 16)
                        sp.wait_ge(u_made_sem, 2 * it + u + 1)
                        sp.dma_start(wu[u][:, :, :], a["w_exp_up"][bass.ds(e, 1)].rearrange("o (k p) n -> p (o k) n", p=P)).then_inc(u_in_sem[u], 16)
                        sp.wait_ge(y_made_sem, 2 * it + u + 1)
                        sp.dma_start(wd[u][:, :, :], a["w_exp_down"][bass.ds(e, 1)].rearrange("o (k p) n -> p (o k) n", p=P)).then_inc(d_in_sem[u], 16)

            @block.gpsimd
            def _(pool):
                def gather(i, u, count):
                    nc.gpsimd.tensor_copy(idx[u][:, :], m.token_of[:, i]).then_inc(idx_new_sem, 1)
                    pool.wait_ge(idx_new_sem, count)
                    pool.sem_inc(credit_sem, 1)
                    nc.gpsimd.indirect_dma_start(xg[u][:, :], None, m.f_dram, bass.IndirectOffsetOnAxis(ap=idx[u][:, :], axis=0)).then_inc(x_in_sem[u], 16)

                gather(slice(0, 1), 0, 1)
                with pool.Fori(0, pairs(pool)) as it:
                    for u in range(2):
                        i = 2 * it + u
                        pool.wait_ge(turned_sem, i + 1)
                        gather(bass.ds(i + 1, 1), 1 - u, i + 2)

            @block.tensor
            def _(pe):
                pe.sem_inc(g_made_sem, 2)
                pe.sem_inc(u_made_sem, 2)
                pe.sem_inc(y_made_sem, 2)

                def turn(u, landed):
                    pe.wait_ge(x_in_sem[u], landed)
                    for k in range(KD):
                        mm = nc.tensor.transpose(m.ps[:, k // 4, (k % 4) * P:(k % 4 + 1) * P], xg[u][:, k * P:(k + 1) * P], m.ident)
                    mm.then_inc(turned_sem, 1)

                turn(0, 16)
                with pe.Fori(0, pairs(pe)) as it:
                    for u in range(2):
                        i = 2 * it + u
                        pe.wait_ge(x_copied_sem, i + 1)
                        for w, bank, landed, made in ((wg, 2, g_in_sem, g_made_sem), (wu, 3, u_in_sem, u_made_sem)):
                            pe.wait_ge(landed[u], 16 * it + 16)
                            for k in range(KD):
                                mm = nc.tensor.matmul(m.ps[:, bank, :], b.xT[:, k, :], w[u][:, k, :], start=(k == 0), stop=(k == KD - 1))
                            mm.then_inc(made, 1)
                        turn(1 - u, 16 * it + 16 + (16 if u else 0))
                        pe.wait_ge(h_new_sem, i + 1)
                        for k in range(4):
                            mm = nc.tensor.transpose(m.ps[:, 4, k * P:(k + 1) * P], b.h[:, k * P:(k + 1) * P], m.ident)
                        mm.then_inc(h_turned_sem, 1)
                        pe.wait_ge(h_copied_sem, i + 1)
                        pe.wait_ge(d_in_sem[u], 16 * it + 16)
                        pe.wait_ge(y_read_sem, i + 1)
                        for c in range(2):
                            for k in range(4):
                                mm = nc.tensor.matmul(m.ps[:, 5 + c, :], b.hT[:, k, :], wd[u][:, k, c * 512:(c + 1) * 512], start=(k == 0), stop=(k == 3))
                        mm.then_inc(y_made_sem, 1)

            @block.scalar
            def _(act):
                act.sem_inc(stored_sem[0], 16)
                act.sem_inc(stored_sem[1], 16)

                def copy_x(i):
                    act.wait_ge(turned_sem, i + 1)
                    nc.scalar.copy(b.xT[:, :, :].rearrange("p k e -> p (k e)"), m.ps[:, 0:2, :].rearrange("p a b -> p (a b)")).then_inc(x_copied_sem, 1)

                copy_x(0)
                n = pairs(act)
                with act.Fori(0, n) as it:
                    for u in range(2):
                        i = 2 * it + u
                        act.wait_ge(g_made_sem, i + 3)
                        nc.scalar.activation(b.sg[:, :], m.ps[:, 2, :], ACT.Silu).then_inc(silu_sem, 1)
                        copy_x(i + 1)
                        act.wait_ge(h_turned_sem, i + 1)
                        nc.scalar.copy(b.hT[:, :, :].rearrange("p k e -> p (k e)"), m.ps[:, 4, :]).then_inc(h_copied_sem, 1)
                        act.wait_ge(y_read_sem, i + 2)
                        act.dma_start(m.y_dram[bass.ds(i * SLOTS, SLOTS), :], y[u][:, :]).then_inc(stored_sem[u], 16)
                for u in range(2):
                    act.wait_ge(stored_sem[u], 16 * n + 16)
                    act.sem_inc(credit_sem, 1)

            @block.vector
            def _(dve):
                dve.sem_inc(y_read_sem, 1)
                with dve.Fori(0, pairs(dve)) as it:
                    for u in range(2):
                        i = 2 * it + u
                        dve.wait_ge(silu_sem, i + 1)
                        dve.wait_ge(u_made_sem, i + 3)
                        nc.vector.tensor_tensor(b.h[:, :], b.sg[:, :], m.ps[:, 3, :], ALU.mult).then_inc(h_new_sem, 1)
                        dve.wait_ge(y_made_sem, i + 3)
                        dve.wait_ge(stored_sem[u], 16 * it + 16)
                        nc.vector.tensor_copy(y[u][:, :], m.ps[:, 5:7, :].rearrange("p a b -> p (a b)")).then_inc(y_read_sem, 1)


def combine(nc, m):
    with ExitStack() as ctx:
        b = Memory()
        b.r0, b.r1 = buffers(nc, ctx, r0=[NTL, D], r1=[NTL, D])
        rows = (b.r0, b.r1)
        gate = gate_rows(nc, m, ctx, 0, 5, 1)
        with stage(nc, landed=8, chain=1) as (block, landed_sem, chain_sem):
            @block.gpsimd
            def _(pool):
                for t in range(NTL):
                    for j in range(2):
                        nc.gpsimd.indirect_dma_start(rows[j][:, t, :], None, m.y_dram, bass.IndirectOffsetOnAxis(ap=m.place_of[:, j, t:t + 1], axis=0)
                                                     ).then_inc(landed_sem[2 * t + j], 16)

            @block.vector
            def _(dve):
                chain = Chain(dve, chain_sem)
                for t in range(NTL):
                    dve.wait_ge(landed_sem[2 * t], 16)
                    chain(nc.vector.tensor_scalar(rows[0][:, t, :], rows[0][:, t, :], m.gate_of[:, 0, t:t + 1], None, ALU.mult))
                    dve.wait_ge(landed_sem[2 * t + 1], 16)
                    chain(nc.vector.scalar_tensor_tensor(rows[0][:, t, :], rows[1][:, t, :], m.gate_of[:, 1, t:t + 1], rows[0][:, t, :], ALU.mult, ALU.add))
                    chain(nc.vector.tensor_tensor(rows[0][:, t, :], rows[0][:, t, :], gate[:, 0, :], ALU.mult))
                    chain(nc.vector.tensor_tensor(m.x[:, t, :], m.x[:, t, :], rows[0][:, t, :], ALU.add))


def fill_rows(nc, m, zeros):
    view = m.y_dram.rearrange("(f p) (h n) -> f p h n", p=P, h=2)
    for f in range(FILLS):
        nc.sync.dma_start(view[f], zeros.unsqueeze(1).to_broadcast([P, 2, 512])).then_inc(m.filled, 16)


def expert_layer(nc, m, a):
    with ExitStack() as ctx:
        def ints(name, shape, dt):
            return ctx.enter_context(nc.sbuf_tensor(f"{name}_{nc.next_id()}", [P, *shape], dt))
        m.place_of = ints("place_of", [2, NTL], U32)
        m.token_of = ints("token_of", [TAB + 1], U32)
        m.expert_of = ints("expert_of", [TAB], I32)
        m.n_pairs = ints("n_pairs", [1], I32)
        (m.gate_of,) = buffers(nc, ctx, gate_of=[2, NTL])
        m.f_dram = nc.dram_tensor("expert_inputs", [LAT, D], F32).ap()
        m.table_dram = nc.dram_tensor("token_table", [(TAB + 1) * SLOTS, 1], U32).ap()
        rows_back(nc, m)
        route(nc, m, a)
        experts(nc, m, a)
        combine(nc, m)


def rows_back(nc, m):
    with ExitStack() as ctx:
        b = Memory()
        (b.f,) = buffers(nc, ctx, f=[2, D])
        with stage(nc, turned=1, read=1, stored=2) as (block, turned_sem, read_sem, stored_sem):
            @block.tensor
            def _(pe):
                for t in range(NTL):
                    if t >= 2:
                        pe.wait_ge(read_sem, t - 1)
                    for k in range(KD):
                        mm = nc.tensor.transpose(m.ps[:, 2 * (t % 2) + k // 4, (k % 4) * P:(k % 4 + 1) * P], m.hT[:, k, CTX + t * P:CTX + (t + 1) * P], m.ident)
                    mm.then_inc(turned_sem, 1)

            @block.vector
            def _(dve):
                for t in range(NTL):
                    dve.wait_ge(turned_sem, t + 1)
                    if t >= 2:
                        dve.wait_ge(stored_sem[t % 2], 16 * (t // 2))
                    nc.vector.tensor_copy(b.f[:, t % 2, :], m.ps[:, 2 * (t % 2):2 * (t % 2) + 2, :].rearrange("p a b -> p (a b)")).then_inc(read_sem, 1)

            @block.sync
            def _(sp):
                for t in range(NTL):
                    sp.wait_ge(read_sem, t + 1)
                    sp.dma_start(m.f_dram[t * P:(t + 1) * P, :], b.f[:, t % 2, :]).then_inc(stored_sem[t % 2], 16)
                for u in range(2):
                    sp.wait_ge(stored_sem[u], 16 * NTL // 2)



TWO_PI_HI = 6.28125
TWO_PI_LO = float(2 * np.pi - TWO_PI_HI)
ROUND = 1.5 * 2.0 ** 23
QSCALE = float(P) ** -0.5


def key_runs(d, t):
    if d == 0:
        return [(0, t + 1)]
    if t < NTC:
        return [(t, NTC)]
    return [(0, NT)] if t == NTC else [(0, NTC), (t, NT)]


def second_block(nc, m, a):
    m.xc = m.keep.enter_context(nc.sbuf_tensor("ctx_rows", [P, NTC, D], F32, side="right"))
    load(nc, [(m.xc, a["ctx_2"].rearrange("(t p) d -> p t d", p=P))])
    lat = [(t, m.x[:, t, :]) for t in range(NTL)]
    for layer in range(2):
        with ExitStack() as ctx:
            n = 2 - layer
            mods = lambda chunk, j: m.mod[:, 1 + layer, 8 * chunk:8 * chunk + 8, j]
            both = [(m.xc[:, t, :], t * P, "ctx") for t in range(NTC)] + [(x, CTX + t * P, "lat") for t, x in lat]

            def adds(ctx, chunk):
                gate = gate_rows(nc, m, ctx, 1 + layer, chunk, n)
                c = [] if layer else [(t, m.xc[:, t, :], gate[:, 1, :]) for t in range(NTC)]
                return c + [(NTC + t, x, gate[:, 0, :]) for t, x in lat]

            with ExitStack() as c1:
                m.inputs = c1.enter_context(ExitStack())
                m.hT = two_parts(nc, m.inputs, KD, TOK, side="right")
                g = cols(m, f"norm_mix_{layer}")
                normed(nc, m, both, m.hT, {"ctx": (g, mods(1, 1), mods(0, 1)), "lat": (g, mods(1, 0), mods(0, 0))})
                if layer == 0:
                    (m.mixT,) = buffers(nc, c1, mixT=[KD, TOK])
                    hyena(nc, m, a)
                    mlstm(nc, m, a)
                    tiles = adds(c1, 2)
                    with halves(nc, m.mixT) as pair:
                        project_add(nc, m, a["w_out_0"], of_halves(pair), KD, tiles, split=True, width=256)
                else:
                    (m.oT,) = buffers(nc, c1, oT=[KD, LAT])
                    latent_attention(nc, m, a)
                    tiles = adds(c1, 2)
                    with halves(nc, m.oT) as pair:
                        project_add(nc, m, a["mla_w_o"], of_halves(pair, CTX), KD, tiles, split=True, width=256)
            with ExitStack() as c1:
                first = CTX * layer
                m.fT = two_parts(nc, c1, KF, LAT) if layer else buffers(nc, c1, fT=[KF, TOK])[0]
                g = cols(m, f"norm_ffn_{layer}")
                kinds = {"ctx": (g, mods(4, 1), mods(3, 1)), "lat": (g, mods(4, 0), mods(3, 0))}
                if layer:
                    both, kinds = both[NTC:], {"lat": kinds["lat"]}
                with ExitStack() as c2:
                    m.hT = two_parts(nc, c2, KD, TOK)
                    normed(nc, m, both, m.hT, kinds)
                    ffn_up(nc, m, a, layer, (1,) if layer else (0, 1))
                if layer:
                    project_add(nc, m, a["ffn_down_1"], of_halves(m.fT, first), KF, adds(c1, 5), width=256, split=True, banks=8, k_chunks=4)
                else:
                    project_add(nc, m, a["ffn_down_0"], lambda k, t0, tn, j: m.fT[:, k, t0:t0 + tn], KF, adds(c1, 5), width=256, wslots=2)
    with ExitStack() as ctx:
        (m.final_gain,) = buffers(nc, ctx, final_gain=[D])
        load(nc, [(m.final_gain, a["rows"][:, 6 * HD:6 * HD + D].to_broadcast([P, D]))])
        head_norms(nc, m, [(m.x[:, :, :], m.final_gain[:, :])], D, EPS)
    with stage(nc, stored=1) as (block, stored_sem):
        @block.sync
        def _(sp):
            sp.dma_start(a["out"][0].rearrange("(t p) d -> p t d", p=P), m.x[:]).then_inc(stored_sem, 16)
            sp.wait_ge(stored_sem, 16)


def tapped(nc, m, w, c0, tiles, cw, cb, ncw, dst, side=()):
    with ExitStack() as ctx:
        (m.pad,) = buffers(nc, ctx, pad=[2, PAD])
        pad_zeros(nc, m, [m.pad[:, 0, :], m.pad[:, 1, :]])
        jobs = [(w[:, c0 + c:c0 + c + 256], 256, [("T", x, P, SEGS[s][0], SEGS[s][2]) for x in (0, P) for s in range(2)])
                for c in range(0, tiles * P, 256)]

        def evac(out, j, at, chain):
            tile, seg = 2 * j + at[0] // P, int(at[2] > 0)
            t0, p0, tn = SEGS[seg]
            pad = m.pad[:, tile % 2, :]
            chain(nc.vector.tensor_copy(pad[:, p0:p0 + tn], out))
            return taps(nc.vector, chain, pad, seg, [cw[:, q * ncw + tile:q * ncw + tile + 1] for q in range(3)],
                        None if cb is None else cb[:, tile:tile + 1], dst[:, tile, t0:t0 + tn])

        products(nc, m, jobs, hT_of(m), evac, "vector", split=True, width=256, side=side)


def sines(nc, chain, reduced_sem, x, k):
    v = nc.vector
    chain(v.tensor_scalar(k, x, float(1 / (2 * np.pi)), ROUND, ALU.mult, ALU.add))
    chain(v.tensor_scalar(k, k, ROUND, None, ALU.subtract))
    chain(v.scalar_tensor_tensor(x, k, -TWO_PI_HI, x, ALU.mult, ALU.add))
    chain(v.scalar_tensor_tensor(x, k, -TWO_PI_LO, x, ALU.mult, ALU.add))
    v.tensor_scalar(x, x, float(np.float32(3.1415925)), -float(np.float32(3.1415925)), ALU.min, ALU.max).then_inc(reduced_sem, 1)


def hyena(nc, m, a):
    with ExitStack() as ctx:
        (m.hy,) = buffers(nc, ctx, hy=[12, TOK])
        tapped(nc, m, a["w_in_0"], 0, 12, cols(m, "hy_conv_w"), cols(m, "hy_conv_b"), 12, m.hy, modulation_tiles(m, a, 1, 16, 48))
        with stage(nc, chain=1) as (block, chain_sem):
            @block.vector
            def _(dve):
                Chain(dve, chain_sem)(nc.vector.tensor_tensor(m.hy[:, 4:8, :], m.hy[:, 4:8, :], m.hy[:, 8:12, :], ALU.mult))
        for seg in range(2):
            t0, _, L = SEGS[seg]
            n = L // P
            with ExitStack() as c1:
                b = Memory()
                b.Kc, b.Ks, b.Kr, b.Ki = buffers(nc, c1, Kc=[n, 512], Ks=[n, 512], Kr=[n, 512], Ki=[n, 512])
                b.g = m.hy[:, 8:12, :].rearrange("p a b -> p (a b)")[:, 0:n * 512].rearrange("p (n e) -> p n e", e=512)
                with ExitStack() as c2:
                    b.z, b.w1, b.w2, b.w3, b.h1, b.h2, b.turns, b.decay = buffers(
                        nc, c2, z=[L], w1=[HD], w2=[HD], w3=[2 * 512], h1=[L], h2=[L], turns=[L], decay=[2, 1024])
                    fb1, fb2, fq = cols(m, "hy_fb1"), cols(m, "hy_fb2"), cols(m, "hy_freq")
                    R = slice(0, HD)
                    with stage(nc, landed=1, decays=2, made=1, reduced=1, sined=1, read=1, chain=1) as (
                            block, landed_sem, decays_sem, made_sem, reduced_sem, sined_sem, read_sem, chain_sem):
                        @block.sync
                        def _(sp):
                            for dst, src in ((b.z[0:33, :], a[f"hy_z_{L}"]), (b.w1[0:33, :], a["hy_fw1"]), (b.w2[R, :], a["hy_fw2"]), (b.w3[R, :], a["hy_fw3"])):
                                sp.dma_start(dst, src).then_inc(landed_sem, 16)
                            for t in range(n):
                                if t >= 2:
                                    sp.wait_ge(read_sem, 2 * (t - 1))
                                sp.dma_start(b.decay[:, t % 2, :], a[f"hy_decay_{L}"][t * P:(t + 1) * P, :]).then_inc(decays_sem[t % 2], 16)

                        @block.tensor
                        def _(pe):
                            pe.wait_ge(landed_sem, 64)
                            nc.tensor.matmul(m.ps[R, 0, 0:L], b.w1[0:33, :], b.z[0:33, :], start=True, stop=True).then_inc(made_sem, 1)
                            pe.wait_ge(sined_sem, 1)
                            nc.tensor.matmul(m.ps[R, 1, 0:L], b.w2[R, :], b.h1[R, :], start=True, stop=True).then_inc(made_sem, 1)
                            pe.wait_ge(sined_sem, 2)
                            for t in range(n):
                                if t >= 2:
                                    pe.wait_ge(read_sem, 2 * (t - 1))
                                for c in range(2):
                                    mm = nc.tensor.matmul(m.ps[:, 2 + 2 * (t % 2) + c, :], b.h2[R, t * P:(t + 1) * P], b.w3[R, c * 512:(c + 1) * 512], start=True, stop=True)
                                mm.then_inc(made_sem, 1)

                        @block.scalar
                        def _(act):
                            for i, h in enumerate((b.h1, b.h2)):
                                act.wait_ge(reduced_sem, i + 1)
                                nc.scalar.activation(h[R, :], h[R, :], ACT.Sin).then_inc(sined_sem, 1)

                        @block.vector
                        def _(dve):
                            chain = Chain(dve, chain_sem)
                            for i, (h, fb) in enumerate(((b.h1, fb1), (b.h2, fb2))):
                                dve.wait_ge(made_sem, i + 1)
                                chain(nc.vector.tensor_scalar(h[R, :], m.ps[R, i, 0:L], fb[R, :], fq[R, :], ALU.add, ALU.mult))
                                if i:
                                    dve.wait_ge(sined_sem, 1)
                                sines(nc, chain, reduced_sem, h[R, :], b.turns[R, :])
                            for t in range(n):
                                dve.wait_ge(made_sem, 3 + t)
                                dve.wait_ge(decays_sem[t % 2], 16 * (t // 2 + 1))
                                dec = b.decay[:, t % 2, :]
                                chain(nc.vector.tensor_tensor(b.Kr[:, t, :], m.ps[:, 2 + 2 * (t % 2), :], dec[:, 0:512], ALU.mult))
                                chain(nc.vector.tensor_tensor(b.Ki[:, t, :], m.ps[:, 3 + 2 * (t % 2), :], dec[:, 512:1024], ALU.mult))
                                nc.vector.tensor_tensor(b.Kc[:, t, :], b.Kr[:, t, :], b.Ki[:, t, :], ALU.add).then_inc(read_sem, 1)
                                nc.vector.tensor_tensor(b.Ks[:, t, :], b.Ki[:, t, :], b.Kr[:, t, :], ALU.subtract).then_inc(read_sem, 1)
                transposes(nc, m, [([m.hy[:, 4 + p, t0 + t * P:t0 + (t + 1) * P] for p in range(4)], b.g[:, t, :].rearrange("p (n e) -> p n e", e=P), None, None)
                                   for t in range(n)])
                b.C, b.S, b.Gr, b.Gs = buffers(nc, c1, C=[n, L], S=[n, L], Gr=[n, 512], Gs=[n, 512])
                specs = [(b.C, b.Kc, b.Kr), (b.S, b.Ks, b.Ki), (b.C, b.g, b.Gr), (b.S, b.g, b.Gs)]
                with stage(nc, landed=4, made=1, read=1, mixed=1, out=1, chain=1) as (
                        block, landed_sem, made_sem, read_sem, mixed_sem, out_sem, chain_sem):
                    @block.sync
                    def _(sp):
                        for i, (dst, name) in enumerate(((b.C, "dft_c"), (b.S, "dft_s"), (b.C, "idft_c"), (b.S, "idft_s"))):
                            if i >= 2:
                                sp.wait_ge(made_sem, (i + 1) * n)
                            sp.dma_start(dst[:], a[f"{name}_{L}"].rearrange("(k p) f -> p k f", p=P)).then_inc(landed_sem[i], 16)
                        for i in range(4):
                            sp.wait_ge(landed_sem[i], 16)

                    @block.tensor
                    def _(pe):
                        r = 0
                        for i, (table, x, dst) in enumerate(specs):
                            pe.wait_ge(landed_sem[i % 2], 16)
                            for f in range(n):
                                if r >= 4:
                                    pe.wait_ge(read_sem, r - 3)
                                for k in range(n):
                                    mm = nc.tensor.matmul(m.ps[:, r % 4, :], table[:, k, f * P:(f + 1) * P], x[:, k, :], start=(k == 0), stop=(k == n - 1))
                                mm.then_inc(made_sem, 1)
                                r += 1
                        pe.wait_ge(landed_sem[2], 16)
                        pe.wait_ge(landed_sem[3], 16)
                        pe.wait_ge(mixed_sem, 1)
                        for p in range(4):
                            for j, (spec, table) in enumerate(((b.Kc, b.C), (b.Ks, b.S))):
                                for f in range(n):
                                    mm = nc.tensor.matmul(m.ps[:, 4 + p, 0:L], spec[:, f, p * P:(p + 1) * P], table[:, f, :], start=(j == 0 and f == 0), stop=(j == 1 and f == n - 1))
                            mm.then_inc(out_sem, 1)

                    @block.scalar
                    def _(act):
                        r = 0
                        for i, (table, x, dst) in enumerate(specs):
                            for f in range(n):
                                act.wait_ge(made_sem, r + 1)
                                nc.scalar.copy(dst[:, f, :], m.ps[:, r % 4, :]).then_inc(read_sem, 1)
                                r += 1

                    @block.vector
                    def _(dve):
                        chain = Chain(dve, chain_sem)
                        v = nc.vector
                        dve.wait_ge(read_sem, 4 * n)
                        x = lambda t: t[:, :, :]
                        chain(v.tensor_tensor(x(b.Kc), x(b.Gr), x(b.Kr), ALU.mult))
                        chain(v.tensor_tensor(x(b.Ks), x(b.Gr), x(b.Ki), ALU.mult))
                        chain(v.tensor_tensor(x(b.Ki), x(b.Gs), x(b.Ki), ALU.mult))
                        chain(v.tensor_tensor(x(b.Kr), x(b.Gs), x(b.Kr), ALU.mult))
                        chain(v.tensor_tensor(x(b.Kc), x(b.Kc), x(b.Ki), ALU.add))
                        v.tensor_tensor(x(b.Ks), x(b.Ks), x(b.Kr), ALU.subtract).then_inc(mixed_sem, 1)
                        for p in range(4):
                            dve.wait_ge(out_sem, p + 1)
                            T = slice(t0, t0 + L)
                            chain(v.scalar_tensor_tensor(m.mixT[:, p, T], m.hy[:, 4 + p, T], cols(m, "hy_bias")[:, p:p + 1], m.ps[:, 4 + p, 0:L], ALU.mult, ALU.add))
                            chain(v.tensor_tensor(m.mixT[:, p, T], m.mixT[:, p, T], m.hy[:, p, T], ALU.mult))


def mlstm(nc, m, a):
    with ExitStack() as ctx:
        (m.qkT,) = buffers(nc, ctx, qkT=[8, TOK])
        tapped(nc, m, a["w_in_0"], 1536, 8, cols(m, "ml_conv_w"), None, 8, m.qkT)
        m.v, m.og, m.gi, m.gf = buffers(nc, ctx, v=[NT, 512], og=[4, TOK], gi=[TOK], gf=[TOK])
        w = a["w_in_0"]
        jobs = [(w[:, c:c + 256], 256, [("N", t, 256) for t in range(NT)]) for c in (2560, 2816)]
        jobs += [(w[:, c:c + 256], 256, [("T", x, P, SEGS[s][0], SEGS[s][2]) for x in (0, P) for s in range(2)]) for c in (3072, 3328)]
        jobs += [(w[:, 3584:3600], 16, [("T", x, 8, SEGS[s][0], SEGS[s][2]) for x in (0, 8) for s in range(2)])]

        def evac(out, j, at, chain):
            if j < 2:
                return nc.scalar.copy(m.v[:, at[0], 256 * j:256 * (j + 1)], out)
            T = slice(at[2], at[2] + at[3])
            if j < 4:
                return nc.scalar.activation(m.og[:, 2 * (j - 2) + at[0] // P, T], out, ACT.Sigmoid)
            dst, bias = (m.gf, "gate_f") if at[0] else (m.gi, "gate_i")
            return nc.scalar.activation(dst[0:8, T], out, ACT.Identity, bias=cols(m, bias)[0:8, :])

        products(nc, m, jobs, hT_of(m), evac, "scalar", split=True, width=256)
        m.inputs.close()
        m.h, m.F, m.r, m.Fcol = buffers(nc, ctx, h=[NT, 512], F=[2, TOK], r=[2, TOK], Fcol=[NT, 2, 8])
        with ExitStack() as c1:
            b = Memory()
            b.e, b.one = buffers(nc, c1, e=[TOK], one=[TOK])
            R = slice(0, 8)
            with stage(nc, expd=1, bent=1, rows=1, turned=1, chain=1) as (block, expd_sem, bent_sem, rows_sem, turned_sem, chain_sem):
                @block.scalar
                def _(act):
                    act.wait_ge(bent_sem, 1)
                    nc.scalar.activation(b.e[R, :], b.e[R, :], ACT.Exp).then_inc(expd_sem, 1)
                    act.wait_ge(bent_sem, 2)
                    nc.scalar.activation(b.e[R, :], b.e[R, :], ACT.Ln).then_inc(expd_sem, 1)
                    for n in (0, 1):
                        nc.scalar.activation(m.qkT[:, 4 * n:4 * n + 4, :], m.qkT[:, 4 * n:4 * n + 4, :], ACT.Silu)

                @block.vector
                def _(dve):
                    chain = Chain(dve, chain_sem)
                    v = nc.vector
                    chain(v.memset(b.one[R, :], 1.0))
                    chain(v.tensor_scalar(b.e[R, :], m.gf[R, :], -1.0, None, ALU.mult))
                    v.tensor_tensor(b.e[R, :], b.e[R, :], m.gf[R, :], ALU.min).then_inc(bent_sem, 1)
                    dve.wait_ge(expd_sem, 1)
                    v.tensor_scalar(b.e[R, :], b.e[R, :], 1.0, None, ALU.add).then_inc(bent_sem, 1)
                    dve.wait_ge(expd_sem, 2)
                    chain(v.tensor_scalar(m.gf[R, :], m.gf[R, :], 0.0, None, ALU.min))
                    chain(v.tensor_tensor(m.gf[R, :], m.gf[R, :], b.e[R, :], ALU.subtract))
                    chain(v.tensor_tensor_scan(m.F[R, 0, :], b.one[R, :], m.gf[R, :], 0.0, ALU.mult, ALU.add))
                    back = lambda x, lo, hi: x[R, hi - 1:(lo - 1 if lo else None):-1]
                    chain(v.tensor_tensor_scan(back(m.F[:, 1, :], 0, CTX), back(b.one, 0, CTX), back(m.gf, 0, CTX), 0.0, ALU.mult, ALU.add))
                    chain(v.tensor_tensor_scan(back(m.F[:, 1, :], CTX, TOK), back(b.one, CTX, TOK), back(m.gf, CTX, TOK), m.F[R, 1, 0:1], ALU.mult, ALU.add))
                    for d in range(2):
                        v.tensor_tensor(m.r[R, d, :], m.gi[R, :], m.F[R, d, :], ALU.subtract).then_inc(rows_sem, 1)
                    dve.wait_ge(turned_sem, 1)
                    chain(v.tensor_copy(m.Fcol[:, :, :, :].rearrange("p t d h -> p (t d h)"), m.ps[:, 0, 0:NT * 16]))

                @block.tensor
                def _(pe):
                    pe.wait_ge(rows_sem, 2)
                    for t in range(NT):
                        for d in range(2):
                            o = (t * 2 + d) * 8
                            mm = nc.tensor.transpose(m.ps[:, 0, o:o + 8], m.F[R, d, t * P:(t + 1) * P], m.ident[R, R])
                    mm.then_inc(turned_sem, 1)
        mlstm_heads(nc, m, a)
        head_norms(nc, m, [(m.h[:].rearrange("p t (h e) -> p (t h) e", e=P), None)], P, EPS)
        g = cols(m, "ml_norm_g")
        transposes(nc, m, [([m.h[:, t, h * P:(h + 1) * P]], m.mixT[:, 4 + h:5 + h, t * P:(t + 1) * P], g[:, h:h + 1], None) for t in range(NT) for h in range(4)])
        with stage(nc, chain=1) as (block, chain_sem):
            @block.vector
            def _(dve):
                Chain(dve, chain_sem)(nc.vector.tensor_tensor(m.mixT[:, 4:8, :], m.mixT[:, 4:8, :], m.og[:, :, :], ALU.mult))


def mlstm_heads(nc, m, a):
    with ExitStack() as ctx:
        b = Memory()
        b.pick, b.causal, b.seen, b.dm, b.tm, b.seen_max, b.mu, b.neg_mu, b.em, b.den, b.dn, b.rec, b.wT = buffers(
            nc, ctx, pick=[8, P], causal=[2, P], seen=[2, NT, NT], dm=[2, NT], tm=[2, NT], seen_max=[2, NT, NT], mu=[2, NT], neg_mu=[2, NT], em=[2, NT], den=[2, 2], dn=[2], rec=[2], wT=[2, NT, P])
        b.rb, b.dg, b.e, b.w = buffers(nc, ctx, rb=[2, NT, P], dg=[2, NT, P], e=[2, NT, P], w=[2, NT, P])
        with stage(nc, landed=1, spread=1, copied=1, mu=1, bounded=1, scored=1, expd=1, weighed=1, turned=1, wt=1, valued=1, stored=1, chain=1) as (
                block, landed_sem, spread_sem, copied_sem, mu_sem, bounded_sem, scored_sem, expd_sem, weighed_sem, turned_sem, wt_sem, valued_sem, stored_sem, chain_sem):
            units = [(h, t) for h in range(HEADS) for t in range(NT)]

            def flat(bank):
                return m.ps[:, bank:bank + 2, :].rearrange("p a b -> p (a b)")[:, 0:TOK]

            @block.sync
            def _(sp):
                sp.dma_start(b.pick[0:8, :, :], a["pick"]).then_inc(landed_sem, 16)
                sp.dma_start(b.causal[:, :, :], a["causal"]).then_inc(landed_sem, 16)
                sp.dma_start(b.seen[:, :, :, :], a["seen"]).then_inc(landed_sem, 16)
                sp.wait_ge(landed_sem, 48)

            @block.tensor
            def _(pe):
                def rows(h):
                    for d in range(2):
                        for c, w in ((0, 512), (512, 256)):
                            mm = nc.tensor.matmul(m.ps[:, 4 + 2 * d + c // 512, 0:w], b.pick[0:8, 4 * d + h, :], m.r[0:8, d, c:c + w], start=True, stop=True)
                    mm.then_inc(spread_sem, 1)

                def scores(i):
                    if i:
                        pe.wait_ge(weighed_sem, 2 * i)
                    h, t = units[i]
                    n = NTC if t < NTC else NT
                    for c, w in ((0, min(n, 4)), (4, n - 4)):
                        if w > 0:
                            mm = nc.tensor.matmul(m.ps[:, c // 4, 0:w * P], m.qkT[:, h, t * P:(t + 1) * P], m.qkT[:, 4 + h, c * P:(c + w) * P], start=True, stop=True)
                    mm.then_inc(scored_sem, 1)

                pe.wait_ge(landed_sem, 48)
                scores(0)
                for i, (h, t) in enumerate(units):
                    if t == 0:
                        if i:
                            pe.wait_ge(stored_sem, 2 * i)
                        rows(h)
                    if t == 0:
                        pe.wait_ge(copied_sem, 2 * (h + 1))
                    for d in range(2):
                        pe.wait_ge(weighed_sem, 2 * i + d + 1)
                        if i or d:
                            pe.wait_ge(wt_sem, 2 * i + d)
                        for lo, hi in key_runs(d, t):
                            for k in range(lo, hi):
                                mm = nc.tensor.transpose(m.ps[:, 2 + k // 4, (k % 4) * P:(k % 4 + 1) * P], b.w[:, d, k, :], m.ident)
                        mm.then_inc(turned_sem, 1)
                        if d == 1 and i + 1 < len(units):
                            scores(i + 1)
                        pe.wait_ge(wt_sem, 2 * i + d + 1)
                        if i:
                            pe.wait_ge(stored_sem, 2 * i - 1 + d)
                        keys = [k for lo, hi in key_runs(d, t) for k in range(lo, hi)]
                        for k in keys:
                            mm = nc.tensor.matmul(m.ps[:, 4 + d, 0:P], b.wT[:, d, k, :], m.v[:, k, h * P:(h + 1) * P], start=(k == keys[0]), stop=(k == keys[-1]))
                        mm.then_inc(valued_sem, 1)

            @block.scalar
            def _(act):
                for i, (h, t) in enumerate(units):
                    if t == 0:
                        act.wait_ge(spread_sem, h + 1)
                        if i:
                            act.wait_ge(weighed_sem, 2 * i)
                        for d in range(2):
                            nc.scalar.copy(b.rb[:, d, :, :].rearrange("p t e -> p (t e)"), flat(4 + 2 * d)).then_inc(copied_sem, 1)
                        act.wait_ge(mu_sem, h + 1)
                        nc.scalar.activation(b.em[:, :, :], b.em[:, :, :], ACT.Exp, scale=-1.0).then_inc(bounded_sem, 1)
                    for d in range(2):
                        if i:
                            act.wait_ge(weighed_sem, 2 * i - 1 + d)
                        nm = b.neg_mu[:, d, t:t + 1]
                        for lo, hi in key_runs(d, t):
                            for x0, x1 in ((lo, min(hi, t)), (max(lo, t + 1), hi)):
                                if x1 > x0:
                                    nc.scalar.activation(b.e[:, d, x0:x1, :], b.rb[:, d, x0:x1, :], ACT.Exp, bias=nm)
                        nc.scalar.activation(b.e[:, d, t, :], b.dg[:, d, t, :], ACT.Exp, bias=nm).then_inc(expd_sem, 1)
                    for d in range(2):
                        act.wait_ge(turned_sem, 2 * i + d + 1)
                        if i:
                            act.wait_ge(valued_sem, 2 * i - 1 + d)
                        runs = key_runs(d, t)
                        for j, (lo, hi) in enumerate(runs):
                            src = m.ps[:, 2:4, :].rearrange("p a (b e) -> p (a b) e", e=P)[:, lo:hi, :]
                            last = nc.scalar.copy(b.wT[:, d, lo:hi, :], src)
                        last.then_inc(wt_sem, 1)

            @block.vector
            def _(dve):
                chain = Chain(dve, chain_sem)
                v = nc.vector
                dve.wait_ge(landed_sem, 48)
                for i, (h, t) in enumerate(units):
                    if t == 0:
                        dve.wait_ge(copied_sem, 2 * (h + 1))
                        for d in range(2):
                            chain(v.tensor_tensor(b.dg[:, d, :, :], b.rb[:, d, :, :], b.causal[:, d, :].unsqueeze(1).to_broadcast([P, NT, P]), ALU.add))
                        chain(v.tensor_reduce(b.dm[:, :, :], b.dg[:, :, :, :], AX, ALU.max))
                        chain(v.tensor_reduce(b.tm[:, :, :], b.rb[:, :, :, :], AX, ALU.max))
                        for d in range(2):
                            chain(v.tensor_tensor(b.seen_max[:, d, :, :], b.seen[:, d, :, :], b.tm[:, d, :].unsqueeze(1).to_broadcast([P, NT, NT]), ALU.add))
                        chain(v.tensor_reduce(b.mu[:, :, :], b.seen_max[:, :, :, :], AX, ALU.max))
                        chain(v.scalar_tensor_tensor(b.mu[:, :, :], b.mu[:, :, :], 0.0, b.dm[:, :, :], ALU.max, ALU.max))
                        chain(v.tensor_scalar(b.neg_mu[:, :, :], b.mu[:, :, :], -1.0, None, ALU.mult))
                        for d in range(2):
                            last = v.tensor_tensor(b.em[:, d, :], b.mu[:, d, :], m.Fcol[:, :, d, 4 * d + h], ALU.add)
                            if d == 0:
                                chain(last)
                        last.then_inc(mu_sem, 1)
                        dve.wait_ge(bounded_sem, h + 1)
                    dve.wait_ge(scored_sem, i + 1)
                    for d in range(2):
                        dve.wait_ge(expd_sem, 2 * i + d + 1)
                        if i:
                            dve.wait_ge(turned_sem, 2 * i - 1 + d)
                        runs = key_runs(d, t)
                        if len(runs) == 1:
                            chain(v.memset(b.den[:, d, 1:2], 0.0))
                        for j, (lo, hi) in enumerate(runs):
                            last = v.scalar_tensor_tensor(b.w[:, d, lo:hi, :].rearrange("p t e -> p (t e)"), flat(0)[:, lo * P:hi * P], QSCALE,
                                                          b.e[:, d, lo:hi, :].rearrange("p t e -> p (t e)"), ALU.mult, ALU.mult, accum_out=b.den[:, d, j:j + 1])
                            if j < len(runs) - 1:
                                chain(last)
                        last.then_inc(weighed_sem, 1)
                    dve.wait_ge(weighed_sem, 2 * i + 2)
                    chain(v.tensor_tensor(b.dn[:, :], b.den[:, :, 0], b.den[:, :, 1], ALU.add))
                    chain(v.scalar_tensor_tensor(b.dn[:, :], b.dn[:, :], -1.0, b.dn[:, :], ALU.mult, ALU.max))
                    chain(v.tensor_tensor(b.dn[:, :], b.dn[:, :], b.em[:, :, t], ALU.max))
                    chain(v.reciprocal(b.rec[:, :], b.dn[:, :]))
                    out = m.h[:, t, h * P:(h + 1) * P]
                    dve.wait_ge(valued_sem, 2 * i + 1)
                    v.tensor_scalar(out, m.ps[:, 4, 0:P], b.rec[:, 0:1], None, ALU.mult).then_inc(stored_sem, 1)
                    dve.wait_ge(valued_sem, 2 * i + 2)
                    dve.wait_ge(stored_sem, 2 * i + 1)
                    v.scalar_tensor_tensor(out, m.ps[:, 5, 0:P], b.rec[:, 1:2], out, ALU.mult, ALU.add).then_inc(stored_sem, 1)
                    dve.wait_ge(stored_sem, 2 * i + 2)


def latent_attention(nc, m, a):
    with ExitStack() as ctx:
        m.v, m.knT, m.krT, m.qnT, m.qrT = buffers(nc, ctx, v=[NT, D], knT=[8, TOK], krT=[1, TOK], qnT=[8, LAT], qrT=[4, LAT])
        with ExitStack() as c1:
            flat = m.oT[:, :, :].rearrange("p a b -> p (a b)")
            m.qa = flat[:, 0:NTL * 384].rearrange("p (t n) -> p t n", n=384)
            m.kva = flat[:, NTL * 384:NTL * 384 + NT * 320].rearrange("p (t n) -> p t n", n=320)
            m.kr2, m.qaT, m.kvaT, m.qr = buffers(nc, c1, kr2=[NT, P], qaT=[3, LAT], kvaT=[2, TOK], qr=[NTL, 512])
            jobs = [(a["mla_w_down"][:, 0:384], 384, [("N", NTC + t, 384) for t in range(NTL)]),
                    (a["mla_w_down"][:, 384:704], 320, [("N", t, 320) for t in range(NT)])]
            products(nc, m, jobs, hT_of(m), lambda out, j, at, chain: nc.vector.tensor_copy(
                m.kva[:, at[0], :] if j else m.qa[:, at[0] - NTC, :], out), "vector", split=True, width=384, banks=8, k_chunks=4)
            m.inputs.close()
            head_norms(nc, m, [(m.qa[:, :, :], None)], 384, EPS)
            head_norms(nc, m, [(m.kva[:, :, 0:256], None)], 256, EPS)
            rope(nc, m, [(m.kva[:, NTC + t, 256:320].unsqueeze(1), 1, t) for t in range(NTL)])
            with stage(nc, done=1) as (block, done_sem):
                @block.vector
                def _(dve):
                    for c in range(2):
                        nc.vector.tensor_copy(m.kr2[:, :, c * HD:(c + 1) * HD], m.kva[:, :, 256:320]).then_inc(done_sem, 1)
            gq, gkv = cols(m, "mla_q_norm"), cols(m, "mla_kv_norm")
            transposes(nc, m, [([m.qa[:, t, k * P:(k + 1) * P]], m.qaT[:, k:k + 1, t * P:(t + 1) * P], gq[:, k:k + 1], None) for t in range(NTL) for k in range(3)]
                       + [([m.kva[:, t, k * P:(k + 1) * P]], m.kvaT[:, k:k + 1, t * P:(t + 1) * P], gkv[:, k:k + 1], None) for t in range(NT) for k in range(2)]
                       + [([m.kr2[:, t, :]], m.krT[:, 0:1, t * P:(t + 1) * P], None, None) for t in range(NT)])
            w = a["mla_w_uq"]
            jobs = [(w[:, 0:512], 512, [("T", x, P, 0, LAT) for x in range(0, 512, P)]), (w[:, 512:1024], 512, [("T", x, P, 0, LAT) for x in range(0, 512, P)]),
                    (w[:, 1024:1536], 512, [("N", t, 512) for t in range(NTL)])]
            with halves(nc, m.qaT) as pair:
                products(nc, m, jobs, of_halves(pair), lambda out, j, at, chain: nc.vector.tensor_copy(
                    m.qr[:, at[0], :] if j == 2 else m.qnT[:, 4 * j + at[0] // P, :], out), "vector", kt=3, split=True)
            rope(nc, m, [(m.qr[:, t, :].rearrange("p (n e) -> p n e", e=HD), 8, t) for t in range(NTL)])
            transposes(nc, m, [([m.qr[:, t, p * P:(p + 1) * P] for p in range(4)], m.qrT[:, :, t * P:(t + 1) * P], None, None) for t in range(NTL)])
            w = a["mla_w_ukv"]
            jobs = [(w[:, c:c + 512], 512, [("T", x, P, SEGS[s][0], SEGS[s][2]) for x in range(0, 512, P) for s in range(2)]) for c in (0, 512)]
            jobs += [(w[:, c:c + 512], 512, [("N", t, 512) for t in range(NT)]) for c in (1024, 1536)]
            with halves(nc, m.kvaT) as pair:
                products(nc, m, jobs, of_halves(pair), lambda out, j, at, chain: nc.vector.tensor_copy(
                    m.v[:, at[0], (j - 2) * 512:(j - 1) * 512] if j >= 2 else m.knT[:, 4 * j + at[0] // P, at[2]:at[2] + at[3]], out),
                    "vector", kt=2, split=True)
        (m.att,) = buffers(nc, ctx, att=[NTL, D])
        items = []
        for t in range(NTL):
            T = slice(t * P, (t + 1) * P)
            for h in range(8):
                R = slice(HD * (h % 2), HD * (h % 2 + 1))
                items.append(([[(m.qnT[:, h, T], m.knT[:, h, :]), (m.qrT[R, h // 2, T], m.krT[R, 0, :])]],
                              lambda k, h=h: m.v[:, k, h * P:(h + 1) * P], m.att[:, t, h * P:(h + 1) * P]))
        attention(nc, m, items, 1, float(192) ** -0.5, None)
        transposes(nc, m, [([m.att[:, t, (4 * g + q) * P:(4 * g + q + 1) * P] for q in range(4)], m.oT[:, 4 * g:4 * g + 4, t * P:(t + 1) * P], None, None)
                           for t in range(NTL) for g in range(2)])


def ffn_up(nc, m, a, layer, segs):
    w, cw, cb = a[f"ffn_up_{layer}"], cols(m, f"ffn_conv_w_{layer}"), cols(m, f"ffn_conv_b_{layer}")
    with ExitStack() as ctx:
        (m.pad,) = buffers(nc, ctx, pad=[2, PAD])
        pad_zeros(nc, m, [m.pad[:, 0, :], m.pad[:, 1, :]])
        jobs = []
        for c in range(0, DFF, P):
            results = [("T", o, P, SEGS[s][0], SEGS[s][2]) for o in (0, P) for s in segs]
            jobs.append(((w[:, c:c + P], w[:, DFF + c:DFF + c + P]), 2 * P, results))

        first, n_segs = SEGS[segs[0]][0], len(segs)
        parts = layer > 0
        if parts:
            (m.whole,) = buffers(nc, ctx, whole=[2, TOK - first])
        silu_done = lambda tile, i: (1 + parts) * n_segs * tile + i + 1
        rounded = lambda tile, i: 2 * n_segs * tile + n_segs + i + 1

        def places(tile, at):
            T = slice(at[2] - first, at[2] - first + at[3])
            return segs.index(int(at[2] > 0)), m.whole[:, tile % 2, T] if parts else m.fT[:, tile, T], T

        def rest(tile, i, whole, T):
            nc.vector.wait_ge(m.aux_sem, rounded(tile, i))
            return nc.vector.tensor_tensor(m.fT[1][:, tile, T], whole, m.fT[0][:, tile, T].bitcast(F32), ALU.subtract)

        def evac(out, tile, at, chain):
            i, whole, T = places(tile, at)
            if at[0] > 0:
                nc.vector.wait_ge(m.aux_sem, silu_done(tile, i))
                return nc.vector.tensor_tensor(whole, out, whole, ALU.mult)
            if parts and tile:
                chain(rest(tile - 1, i, places(tile - 1, at)[1], T))
            t0, p0, tn = SEGS[segs[i]]
            pad = m.pad[:, tile % 2, :]
            chain(nc.vector.tensor_copy(pad[:, p0:p0 + tn], out))
            return taps(nc.vector, chain, pad, segs[i], [cw[:, q * KF + tile:q * KF + tile + 1] for q in range(3)], cb[:, tile:tile + 1], whole)

        def beside(act, r, tile, at, read_sem, aux_sem):
            i, whole, T = places(tile, at)
            if at[0] == 0 or parts:
                act.wait_ge(read_sem, r + 1)
            if at[0] == 0:
                nc.scalar.activation(whole, whole, ACT.Silu).then_inc(aux_sem, 1)
            elif parts:
                nc.scalar.copy(m.fT[0][:, tile, T], whole).then_inc(aux_sem, 1)

        products(nc, m, jobs, hT_of(m), evac, "vector", beside=beside, split=True, width=2 * P, k_chunks=1 + layer,
                 side=() if layer else modulation_tiles(m, a, 2, 0, 48))
        if parts:
            with stage(nc, parted=1) as (block, parted_sem):
                @block.vector
                def _(dve):
                    nc.vector.tensor_tensor(m.fT[1][:, KF - 1, :], m.whole[:, (KF - 1) % 2, :], m.fT[0][:, KF - 1, :].bitcast(F32),
                                            ALU.subtract).then_inc(parted_sem, 1)



def build(nc, a, where):
    m = Memory()
    m.where = where
    n_cols = a["cols"].shape[1]
    with ExitStack() as ctx:
        m.ps = ctx.enter_context(nc.psum_tensor("banks", [P, 8, 512], F32))
        m.ident, m.cols, m.rope_cos, m.rope_sin, m.qk_gain, m.neg_lam, m.subln, m.mod, m.cond = buffers(
            nc, ctx, ident=[P], cols=[n_cols], rope_cos=[NTL, HD], rope_sin=[NTL, HD], qk_gain=[2 * HD], neg_lam=[1], subln=[1], mod=[3, 48, 2], cond=[3, KD, 2])
        m.ident, m.cols = m.ident[:, :], m.cols[:, :]
        m.keep = ctx.enter_context(ExitStack())
        with ExitStack() as first:
            m.masks, m.restart, m.headsum, m.headspread, m.head_mask = buffers(
                nc, first, masks=[len(MASKS), P], restart=[2, 512], headsum=[4, RH], headspread=[4, P], head_mask=[P])
            m.head_mask = m.head_mask[:, :]
            block_one(nc, m, a)
        second_block(nc, m, a)



def tables():
    c = {}
    f = np.float32
    c["ident"] = np.eye(P, dtype=f)
    pos = np.arange(LAT)
    inv = f(10000.0) ** (-np.arange(16, dtype=f) / f(16))
    ang = np.stack([(pos // 64).astype(f)[:, None] * inv, (pos % 64).astype(f)[:, None] * inv], 1)
    cs, sn = np.cos(ang.astype(np.float64)), np.sin(ang.astype(np.float64))
    fold = lambda x: x.reshape(NTL, P, HD).transpose(1, 0, 2).astype(f)
    c["rope_cos"] = fold(np.stack([cs, cs], 2).reshape(LAT, HD))
    c["rope_sin"] = fold(np.stack([-sn, sn], 2).reshape(LAT, HD))
    bands = np.zeros((4, LAT, LAT))
    for g, w in enumerate((2, 4, 8, 16)):
        lo, hi = np.clip(pos - w // 2, 0, LAT - 1), np.clip(pos + w // 2 - 1, 0, LAT - 1)
        s = np.arange(LAT)[:, None]
        bands[g] = ((s >= lo) & (s <= hi)) / (hi - lo + 1) - (s == pos)
    c["bands"] = bands.astype(f)
    r, q = np.arange(P)[:, None], np.arange(P)[None]
    chunk, block = r // CH == q // CH, r // 16 == q // 16
    below, above = (r > q) & chunk, (r < q) & chunk
    made = {"below16": below & block, "rest_below": below & ~block, "above16": above & block, "rest_above": above & ~block,
            "above_eq": above | (r == q), "below_eq": below | (r == q), "above": above, "below": below}
    c["masks"] = np.stack([made[n] for n in MASKS], 1).astype(f)
    c["head_mask"] = (r // HD == q // HD).astype(f)
    t = np.arange(512)
    c["restart"] = np.broadcast_to(np.stack([t % CH != 0, t % CH != CH - 1])[None], (P, 2, 512)).astype(f)
    c["headsum"] = np.stack([2 * p + np.arange(P)[:, None] // HD == np.arange(RH)[None] for p in range(4)], 1).astype(f)
    c["headspread"] = np.concatenate([c["headsum"].transpose(2, 1, 0), np.zeros((P - RH, 4, P))]).astype(f)
    c["iota32"] = np.broadcast_to(np.arange(N_EXP), (P, 1, N_EXP)).astype(f)
    c["tri"] = (r < q).astype(f)
    c["tok_id"] = (np.arange(NTL)[None] * P + np.arange(P)[:, None]).astype(f)
    c["block_id"] = np.broadcast_to(np.arange(TAB), (P, TAB)).astype(f)
    c["pick"] = np.stack([(np.arange(8)[:, None] == n) * np.ones((1, P)) for n in range(8)], 1).astype(f)
    c["causal"] = np.stack([np.where(q <= r, 0, -BIG), np.where(q >= r, 0, -BIG)], 1).astype(f)
    seen = np.full((2, NT, NT), -BIG)
    for d in range(2):
        for t in range(NT):
            for lo, hi in key_runs(d, t):
                for k in range(lo, hi):
                    if k != t:
                        seen[d, t, k] = 0
    c["seen"] = np.broadcast_to(seen, (P, 2, NT, NT)).astype(f)
    for L in (CTX, LAT):
        s, w = np.arange(L)[:, None], (np.arange(L)[None] + 0.5) * np.pi / L
        c[f"dft_c_{L}"], c[f"dft_s_{L}"] = np.cos(s * w).astype(f), np.sin(s * w).astype(f)
        c[f"idft_c_{L}"], c[f"idft_s_{L}"] = (np.cos(s * w).T / L).astype(f), (-np.sin(s * w).T / L).astype(f)
        pos = np.arange(L, dtype=f)
        t = (pos / f(L - 1))[:, None]
        freq = np.linspace(1e-4, 15, 16, dtype=f)
        ang = f(2.0 * np.pi / L) * pos[:, None] * freq[None]
        c[f"hy_z_{L}"] = np.concatenate([t, np.cos(ang), -np.sin(ang)], 1).T.astype(f)
        deltas = np.linspace(np.log(1e-2) / 0.3, np.log(1e-2) / 1.5, 512, dtype=f)
        decay = np.exp(-t * np.abs(np.tile(deltas, 2))[None]) + f(0.05)
        decay[0, 512:] = 0
        c[f"hy_decay_{L}"] = decay.astype(f)
    return c


def columns(v):
    v = np.asarray(v).reshape(-1)
    return v.reshape(-1, P).T if v.size % P == 0 else np.concatenate([v, np.zeros(P - v.size, v.dtype)])[:, None]


def packed_columns(i):
    named = {"c": i["c"], "c_ctx": i["c_ctx"], "b_ada": i["b_ada"], "norm1_g": i["norm1_g"], "norm2_g": i["norm2_g"],
             "pool_scale": i["pool_scale"], "subln_g": i["subln_g"], "mu0": i["shift_mu"][0, 0], "mu1": i["shift_mu"][0, 1],
             "w0": i["decay_w0"], "a0": i["aaa_a0"], "k_k": i["k_k"], "k_a": i["k_a"], "r_k": i["r_k"],
             "gn_w": i["gn_w"], "gn_b": i["gn_b"],
             "c_2": i["c_2"], "c_ctx_2": i["c_ctx_2"], "ada_b_0": i["ada_b_0_2"], "ada_b_1": i["ada_b_1_2"],
             "norm_mix_0": i["norm_mix_0_2"], "norm_ffn_0": i["norm_ffn_0_2"], "norm_mix_1": i["norm_mix_1_2"],
             "norm_ffn_1": i["norm_ffn_1_2"], "hy_conv_w": i["hy_conv_w_2"], "hy_conv_b": i["hy_conv_b_2"], "hy_bias": i["hy_bias_2"],
             "ml_conv_w": i["ml_conv_w_2"], "ml_norm_g": i["ml_norm_g_2"],
             "ffn_conv_w_0": i["ffn_conv_w_0_2"], "ffn_conv_b_0": i["ffn_conv_b_0_2"],
             "ffn_conv_w_1": i["ffn_conv_w_1_2"], "ffn_conv_b_1": i["ffn_conv_b_1_2"],
             "mla_q_norm": i["mla_q_norm_2"], "mla_kv_norm": i["mla_kv_norm_2"],
             "hy_fb1": i["hy_fb1_2"], "hy_fb2": i["hy_fb2_2"], "hy_freq": i["hy_freq_2"],
             "gate_i": i["ml_gate_b_2"].reshape(2, 2, 4)[:, 0], "gate_f": i["ml_gate_b_2"].reshape(2, 2, 4)[:, 1]}
    parts, where, at = [], {}, 0
    for name, v in named.items():
        c = columns(v)
        where[name] = (at, c.shape[1])
        at += c.shape[1]
        parts.append(c)
    return np.ascontiguousarray(np.concatenate(parts, 1)), where


def laid_out(i):
    out = tables()
    out["cols"], where = packed_columns(i)
    out["rows"] = np.concatenate([i["q_norm_g"].reshape(-1), i["k_norm_g"].reshape(-1), i["lambda_qk"].reshape(-1),
                                  i["final_norm_2"].reshape(-1)])[None]
    for name in ("x", "ctx", "w_ada", "w_in", "pool_w", "decay_w2", "aaa_a2", "gate_w2", "w_br", "w_out", "w_exp_gate",
                 "w_exp_up", "w_exp_down", "ctx_2"):
        out[name] = i[name][0]
    out["w_router"] = np.concatenate([i["w_router_group"][0], i["w_router_expert"][0]], 1)
    w = i["w_in_0_2"]
    out["w_in_0"] = np.concatenate([w[:, :3584], w[:, 3584:].reshape(D, 2, 2, 4).transpose(0, 2, 1, 3).reshape(D, 16)], 1)
    for name in ("ada_w_0_2", "ada_w_1_2", "w_out_0_2", "ffn_up_0_2", "ffn_down_0_2", "ffn_up_1_2", "ffn_down_1_2",
                 "mla_w_down_2", "mla_w_uq_2", "mla_w_ukv_2", "mla_w_o_2", "hy_fw1_2", "hy_fw2_2", "hy_fw3_2"):
        out[name[:-2]] = i[name]
    w = i["mla_w_uq_2"].reshape(384, 8, 192)
    out["mla_w_uq"] = np.concatenate([w[:, :, :P].reshape(384, -1), w[:, :, P:].reshape(384, -1)], 1)
    w = i["mla_w_ukv_2"].reshape(256, 8, 2, P)
    out["mla_w_ukv"] = w.transpose(0, 2, 1, 3).reshape(256, -1)
    return {k: np.ascontiguousarray(v) for k, v in out.items()}, where


def kernel(**inputs):
    import concourse.bacc as _bacc
    from concourse.bass_utils import run_bass_kernel_spmd as _run

    i = {k: np.asarray(v) for k, v in inputs.items()}
    arrays, where = laid_out(i)
    nc = _bacc.Bacc("TRN2", target_bir_lowering=False, num_devices=1)
    args = {name: nc.dram_tensor(f"in_{name}", v.shape, mybir.dt.from_np(v.dtype), kind="ExternalInput").ap() for name, v in arrays.items()}
    args["out"] = nc.dram_tensor("out_0", (1, LAT, D), F32, kind="ExternalOutput").ap()
    build(nc, args, where)
    r = _run(nc, [{f"in_{name}": v for name, v in arrays.items()}], core_ids=[0])
    return r.results[0]["out_0"]
```
